# Optimizing a Trainium2 kernel written in Bass

```python
import math
import jax, jax.numpy as jnp
from jax import lax
import numpy as np

D_MODEL = 1024
BATCH = 1
SEQ = 1024
DEPTH = 2

N_MIXERS = 3
LAYER_MIXER = tuple(i % N_MIXERS for i in range(DEPTH))
N_S5 = LAYER_MIXER.count(0)
N_HG = LAYER_MIXER.count(1)
N_MLA = LAYER_MIXER.count(2)
MIX_WIDTH = D_MODEL
S5_GROUP = 16
S5_GROUPS = MIX_WIDTH // S5_GROUP
S5_STATE = 64
S5_DT_MIN = 0.001
S5_DT_MAX = 0.1
S5_BLOCK = 1024
HG_HEAD_DIM = 128
HG_HEADS = MIX_WIDTH // HG_HEAD_DIM
HG_CHUNK = 64
MLA_HEADS = 8
MLA_NOPE = 128
MLA_ROPE = 64
MLA_V = 128
MLA_Q_LORA = 384
MLA_KV_LORA = 256
ROPE_THETA = 10000.0
ATTN_BLOCK = 128
MAX_POS_OFFSET = 4096
FFN_HIDDEN = -(-8 * D_MODEL // (3 * 256)) * 256
DEEPNORM_ALPHA = (2 * DEPTH) ** 0.25
DEEPNORM_BETA = (8 * DEPTH) ** -0.25
LN_EPS = 1e-5
RMS_EPS = 1e-6

kernel_name = 'hybrid_s5_hgrn2_mla_deepnorm_encoder'

def layer_norm(x, g, b):
    xf = x.astype(jnp.float32)
    mu = jnp.mean(xf, axis=-1, keepdims=True)
    var = jnp.mean(jnp.square(xf - mu), axis=-1, keepdims=True)
    return ((xf - mu) * lax.rsqrt(var + LN_EPS) * g + b).astype(x.dtype)

def rms_norm(x, g):
    xf = x.astype(jnp.float32)
    return (xf * lax.rsqrt(jnp.mean(xf * xf, axis=-1, keepdims=True) + RMS_EPS) * g).astype(x.dtype)

def swiglu(x, w_in, w_out):
    gate, up = jnp.split(x @ w_in, 2, axis=-1)
    return (jax.nn.silu(gate) * up) @ w_out

def s5_direction(u, lam_re, lam_im, log_step, b_re, b_im, c_re, c_im):
    seq, bsz = u.shape[0], u.shape[1]
    blk = math.gcd(seq, S5_BLOCK)
    f32 = jnp.float32
    lam = lax.complex(lam_re.astype(f32), lam_im.astype(f32))
    step = jnp.exp(log_step.astype(f32))[:, None]
    lam_dt = lam * step
    lam_bar = jnp.exp(lam_dt)
    b = lax.complex(b_re.astype(f32), b_im.astype(f32))
    b_bar = ((lam_bar - 1.0) / lam)[..., None] * b
    c = lax.complex(c_re.astype(f32), c_im.astype(f32))
    powers = jnp.exp(lam_dt[None] * jnp.arange(1, blk + 1, dtype=f32)[:, None, None])
    a_blk = jnp.broadcast_to(lam_bar, (blk, 1) + lam_bar.shape)
    u_blocks = u.astype(f32).reshape(seq // blk, blk, bsz, S5_GROUPS, S5_GROUP)

    def combine(left, right):
        a_l, b_l = left
        a_r, b_r = right
        return a_r * a_l, a_r * b_l + b_r

    def step_fn(h, u_blk):
        bu = jnp.einsum('lbgh,gph->lbgp', u_blk.astype(jnp.complex64), b_bar)
        _, h_loc = lax.associative_scan(combine, (a_blk, bu), axis=0)
        h_all = h_loc + powers[:, None] * h[None]
        y = jnp.einsum('ghp,lbgp->lbgh', c, h_all).real
        return h_all[-1], y

    h0 = jnp.zeros((bsz, S5_GROUPS, S5_STATE), jnp.complex64)
    _, y = lax.scan(step_fn, h0, u_blocks)
    return y.reshape(seq, bsz, S5_GROUPS, S5_GROUP)

def s5_mixer(x, w_in, lam_re, lam_im, log_step, b_re, b_im, c_re, c_im, d_skip, w_glu, b_glu, w_out):
    bsz, seq, _ = x.shape
    u = x @ w_in
    u_s = jnp.swapaxes(u, 0, 1).reshape(seq, bsz, S5_GROUPS, S5_GROUP)
    y_fw = s5_direction(u_s, lam_re[0], lam_im[0], log_step[0], b_re[0], b_im[0], c_re[0], c_im[0])
    y_bw = jnp.flip(s5_direction(jnp.flip(u_s, 0), lam_re[1], lam_im[1], log_step[1],
                                 b_re[1], b_im[1], c_re[1], c_im[1]), 0)
    y = jnp.swapaxes((y_fw + y_bw).reshape(seq, bsz, MIX_WIDTH), 0, 1).astype(x.dtype) + d_skip * u
    y = jax.nn.gelu(y)
    y = y * jax.nn.sigmoid(y @ w_glu + b_glu)
    return y @ w_out

def chunked_gated_recurrence(q, k, v, log_f):
    n, h, seq, dk = q.shape
    dv = v.shape[-1]
    nc = seq // HG_CHUNK

    def to_chunks(t):
        return jnp.moveaxis(t.reshape(n, h, nc, HG_CHUNK, t.shape[-1]), 2, 0)

    lower = jnp.tril(jnp.ones((HG_CHUNK, HG_CHUNK), bool))[:, :, None]

    def step(state, inp):
        qc, kc, vc, lfc = inp
        b = jnp.cumsum(lfc, axis=2)
        b_last = b[:, :, -1:, :]
        o_inter = jnp.einsum('nhtk,nhkv->nhtv', qc * jnp.exp(b), state)
        diff = b[:, :, :, None, :] - b[:, :, None, :, :]
        decay = jnp.where(lower, jnp.exp(jnp.where(lower, diff, 0.0)), 0.0)
        scores = jnp.einsum('nhtk,nhsk,nhtsk->nhts', qc, kc, decay)
        o_intra = jnp.einsum('nhts,nhsv->nhtv', scores, vc)
        new_state = (jnp.exp(b_last[:, :, 0, :])[..., None] * state
                     + jnp.einsum('nhsk,nhsv->nhkv', kc * jnp.exp(b_last - b), vc))
        return new_state, o_inter + o_intra

    s0 = jnp.zeros((n, h, dk, dv), jnp.float32)
    _, o = lax.scan(step, s0, (to_chunks(q), to_chunks(k), to_chunks(v), to_chunks(log_f)))
    return jnp.moveaxis(o, 0, 2).reshape(n, h, seq, dv)

def hgrn2_mixer(x, w_in, lower_bound, norm_g, w_out):
    bsz, seq, _ = x.shape
    q, f_fw, f_bw, i_in, g = jnp.split(x @ w_in, 5, axis=-1)

    def heads(t):
        return t.reshape(bsz, seq, HG_HEADS, HG_HEAD_DIM).transpose(0, 2, 1, 3).astype(jnp.float32)

    q = jax.nn.silu(heads(q))
    v = heads(i_in)
    lb = lower_bound.reshape(HG_HEADS, 1, HG_HEAD_DIM).astype(jnp.float32)

    def gates(f):
        z = heads(f)
        log_f = jnp.logaddexp(jnp.log(lb), jnp.log1p(-lb) + jax.nn.log_sigmoid(z))
        k = (1.0 - lb) * jax.nn.sigmoid(-z)
        return log_f, k

    lf_fw, k_fw = gates(f_fw)
    lf_bw, k_bw = gates(f_bw)
    flip = lambda t: jnp.flip(t, axis=2)
    q2 = jnp.concatenate([q, flip(q)], axis=0)
    k2 = jnp.concatenate([k_fw, flip(k_bw)], axis=0)
    v2 = jnp.concatenate([v, flip(v)], axis=0)
    lf2 = jnp.concatenate([lf_fw, flip(lf_bw)], axis=0)
    o = chunked_gated_recurrence(q2, k2, v2, lf2)
    o = o[:bsz] + flip(o[bsz:])
    o = rms_norm(o, norm_g)
    o = o.transpose(0, 2, 1, 3).reshape(bsz, seq, MIX_WIDTH).astype(x.dtype)
    o = o * jax.nn.silu(g)
    return o @ w_out

def rope_cos_sin(positions):
    half = MLA_ROPE // 2
    inv_freq = 1.0 / (ROPE_THETA ** (jnp.arange(half, dtype=jnp.float32) * (2.0 / MLA_ROPE)))
    ang = positions.astype(jnp.float32)[..., None] * inv_freq
    return jnp.cos(ang), jnp.sin(ang)

def apply_rope(t, cos, sin):
    half = t.shape[-1] // 2
    t1, t2 = t[..., :half], t[..., half:]
    return jnp.concatenate([t1 * cos - t2 * sin, t1 * sin + t2 * cos], axis=-1).astype(t.dtype)

def dense_attention(q_nope, q_pe, k_nope, k_pe, v):
    bsz, seq, h, _ = q_nope.shape
    nb = seq // ATTN_BLOCK
    qn_b = jnp.moveaxis(q_nope.reshape(bsz, nb, ATTN_BLOCK, h, MLA_NOPE), 1, 0)
    qp_b = jnp.moveaxis(q_pe.reshape(bsz, nb, ATTN_BLOCK, h, MLA_ROPE), 1, 0)

    def one_block(blk):
        qn, qp = blk
        s = (jnp.einsum('bqhd,bkhd->bhqk', qn, k_nope, preferred_element_type=jnp.float32)
             + jnp.einsum('bqhr,bkr->bhqk', qp, k_pe, preferred_element_type=jnp.float32))
        p = jax.nn.softmax(s, axis=-1).astype(v.dtype)
        return jnp.einsum('bhqk,bkhd->bqhd', p, v)

    o = lax.map(one_block, (qn_b, qp_b))
    return jnp.moveaxis(o, 0, 1).reshape(bsz, seq, h, MLA_V)

def mla_mixer(x, positions, w_in, q_norm_g, w_q_b, kv_norm_g, w_kv_b, w_out):
    bsz, seq, _ = x.shape
    q_lat, kv_lat, k_rope = jnp.split(x @ w_in, [MLA_Q_LORA, MLA_Q_LORA + MLA_KV_LORA], axis=-1)
    q = (rms_norm(q_lat, q_norm_g) @ w_q_b).reshape(bsz, seq, MLA_HEADS, MLA_NOPE + MLA_ROPE)
    kv = (rms_norm(kv_lat, kv_norm_g) @ w_kv_b).reshape(bsz, seq, MLA_HEADS, MLA_NOPE + MLA_V)
    cos, sin = rope_cos_sin(positions)
    scale = (MLA_NOPE + MLA_ROPE) ** -0.5
    q_nope = q[..., :MLA_NOPE] * scale
    q_pe = apply_rope(q[..., MLA_NOPE:], cos[:, :, None, :], sin[:, :, None, :]) * scale
    k_pe = apply_rope(k_rope, cos, sin)
    k_nope, v = kv[..., :MLA_NOPE], kv[..., MLA_NOPE:]
    o = dense_attention(q_nope, q_pe, k_nope, k_pe, v)
    return o.reshape(bsz, seq, MLA_HEADS * MLA_V) @ w_out

def setup_inputs(seed: int = 0) -> dict:
    key = jax.random.key(seed)
    ks = iter(jax.random.split(key, 40))
    f32 = jnp.float32
    d, w = D_MODEL, MIX_WIDTH
    g, p, hs = S5_GROUPS, S5_STATE, S5_GROUP

    def nrm(shape, scale):
        return jax.random.normal(next(ks), shape, f32) * scale

    inp = {}
    inp['x'] = nrm((BATCH, SEQ, d), 1.0)
    inp['positions'] = (jnp.arange(SEQ, dtype=jnp.int32)[None, :]
                        + jax.random.randint(next(ks), (BATCH, 1), 0, MAX_POS_OFFSET, dtype=jnp.int32))
    inp['ln_mix_g'] = 1.0 + nrm((DEPTH, d), 0.02)
    inp['ln_mix_b'] = nrm((DEPTH, d), 0.01)
    inp['ln_ffn_g'] = 1.0 + nrm((DEPTH, d), 0.02)
    inp['ln_ffn_b'] = nrm((DEPTH, d), 0.01)
    inp['ffn_w_in'] = nrm((DEPTH, d, 2 * FFN_HIDDEN), d ** -0.5)
    inp['ffn_w_out'] = nrm((DEPTH, FFN_HIDDEN, d), DEEPNORM_BETA * FFN_HIDDEN ** -0.5)
    inp['s5_w_in'] = nrm((N_S5, d, w), d ** -0.5)
    inp['s5_lam_re'] = -0.5 + nrm((N_S5, 2, g, p), 0.01)
    inp['s5_lam_im'] = jnp.pi * jnp.arange(p, dtype=f32) + nrm((N_S5, 2, g, p), 0.01)
    inp['s5_log_step'] = jax.random.uniform(next(ks), (N_S5, 2, g), f32,
                                            math.log(S5_DT_MIN), math.log(S5_DT_MAX))
    inp['s5_b_re'] = nrm((N_S5, 2, g, p, hs), (2 * hs) ** -0.5)
    inp['s5_b_im'] = nrm((N_S5, 2, g, p, hs), (2 * hs) ** -0.5)
    inp['s5_c_re'] = nrm((N_S5, 2, g, hs, p), (2 * p) ** -0.5)
    inp['s5_c_im'] = nrm((N_S5, 2, g, hs, p), (2 * p) ** -0.5)
    inp['s5_d'] = nrm((N_S5, w), 1.0)
    inp['s5_w_glu'] = nrm((N_S5, w, w), w ** -0.5)
    inp['s5_b_glu'] = nrm((N_S5, w), 0.01)
    inp['s5_w_out'] = nrm((N_S5, w, d), DEEPNORM_BETA * w ** -0.5)
    inp['hg_w_in'] = nrm((N_HG, d, 5 * w), d ** -0.5)
    inp['hg_lower_bound'] = nrm((DEPTH, w), 0.1)
    inp['hg_norm_g'] = 1.0 + nrm((N_HG, HG_HEAD_DIM), 0.02)
    inp['hg_w_out'] = nrm((N_HG, w, d), DEEPNORM_BETA * w ** -0.5)
    inp['mla_w_in'] = nrm((N_MLA, d, MLA_Q_LORA + MLA_KV_LORA + MLA_ROPE), d ** -0.5)
    inp['mla_q_norm_g'] = 1.0 + nrm((N_MLA, MLA_Q_LORA), 0.02)
    inp['mla_w_q_b'] = nrm((N_MLA, MLA_Q_LORA, MLA_HEADS * (MLA_NOPE + MLA_ROPE)), MLA_Q_LORA ** -0.5)
    inp['mla_kv_norm_g'] = 1.0 + nrm((N_MLA, MLA_KV_LORA), 0.02)
    inp['mla_w_kv_b'] = nrm((N_MLA, MLA_KV_LORA, MLA_HEADS * (MLA_NOPE + MLA_V)), MLA_KV_LORA ** -0.5)
    inp['mla_w_out'] = nrm((N_MLA, MLA_HEADS * MLA_V, d), DEEPNORM_BETA * (MLA_HEADS * MLA_V) ** -0.5)
    return inp

def reference(x, positions, ln_mix_g, ln_mix_b, ln_ffn_g, ln_ffn_b, ffn_w_in, ffn_w_out,
              s5_w_in, s5_lam_re, s5_lam_im, s5_log_step, s5_b_re, s5_b_im, s5_c_re, s5_c_im,
              s5_d, s5_w_glu, s5_b_glu, s5_w_out,
              hg_w_in, hg_lower_bound, hg_norm_g, hg_w_out,
              mla_w_in, mla_q_norm_g, mla_w_q_b, mla_kv_norm_g, mla_w_kv_b, mla_w_out):
    lbs = jax.nn.softmax(hg_lower_bound.astype(jnp.float32), axis=0)
    lbs = jnp.cumsum(lbs, axis=0) - lbs[0]
    h = x
    for layer in range(DEPTH):
        kind = LAYER_MIXER[layer]
        slot = layer // N_MIXERS
        if kind == 0:
            m = s5_mixer(h, s5_w_in[slot], s5_lam_re[slot], s5_lam_im[slot], s5_log_step[slot],
                         s5_b_re[slot], s5_b_im[slot], s5_c_re[slot], s5_c_im[slot],
                         s5_d[slot], s5_w_glu[slot], s5_b_glu[slot], s5_w_out[slot])
        elif kind == 1:
            m = hgrn2_mixer(h, hg_w_in[slot], lbs[layer], hg_norm_g[slot], hg_w_out[slot])
        else:
            m = mla_mixer(h, positions, mla_w_in[slot], mla_q_norm_g[slot], mla_w_q_b[slot],
                          mla_kv_norm_g[slot], mla_w_kv_b[slot], mla_w_out[slot])
        h = layer_norm(DEEPNORM_ALPHA * h + m, ln_mix_g[layer], ln_mix_b[layer])
        f = swiglu(h, ffn_w_in[layer], ffn_w_out[layer])
        h = layer_norm(DEEPNORM_ALPHA * h + f, ln_ffn_g[layer], ln_ffn_b[layer])
    return h


_drawn_inputs = setup_inputs


def setup_inputs(seed=0):
    import zlib

    import numpy as np

    out = dict(_drawn_inputs(seed))
    spreads = {}
    factors = {'ln_mix_b': 3.724,
     'ln_ffn_b': 3.444,
     's5_lam_re': 64.0,
     's5_lam_im': 39.112,
     's5_log_step': 40.072,
     's5_b_re': 55.28,
     's5_b_im': 55.36,
     's5_c_re': 54.64,
     's5_c_im': 54.688,
     's5_b_glu': 56.718,
     'hg_lower_bound': 8.0,
     'hg_norm_g': 30.269}
    for name, (base, spread) in spreads.items():
        noise = np.random.default_rng([zlib.crc32(name.encode()), seed]).standard_normal(out[name].shape)
        drawn = base * np.exp(spread * noise) if base else spread * noise
        out[name] = __import__('jax').numpy.asarray(drawn.astype(out[name].dtype))
    for name, factor in factors.items():
        out[name] = (out[name] * factor).astype(out[name].dtype)
    return out
```

```python
from contextlib import ExitStack
import math

import numpy as np

import concourse.bass as bass
from concourse import mybir

F32 = mybir.dt.float32
F32R = mybir.dt.float32r
I32 = mybir.dt.int32
ALU = mybir.AluOpType
ACT = mybir.ActivationFunctionType
AX_X = mybir.AxisListType.X
ds = bass.ds

P = 128
D = 1024
T = 1024
KT = D // P
NT = T // P
HALF = 512
FFN = 2816
NF = FFN // P
FG = 2
NG = NF // FG
DEPTH = 2
ALPHA = float((2 * DEPTH) ** 0.25)
LN_EPS = 1e-5
RMS_EPS = 1e-6
GRP = 16
ST = 64
SG = D // GRP
L = 8
NC = T // L
GJ = P // GRP
PR = GJ // 2
DP = 2 * PR
LV = 7
HEADS = 8
HC = 128
NHC = T // HC
HLV = 7


def split_hi(eng, hi, src):
    return eng.activation(hi, src, ACT.Copy)


class Steps:

    def __init__(self, sem, base=0):
        self.sem, self.base, self.n = sem, base, 0

    def step(self):
        self.n += 1
        return self.base + self.n

    def count(self):
        return self.base + self.n


class Core:

    def __init__(self, nc, ctx):
        self.nc, self.ctx = nc, ctx
        self.phase = None
        self.fresh, self.old = [], []

    def open(self):
        self.phase = ExitStack()
        self.phase.__enter__()

    def close(self):
        self.phase.close()
        self.end_sems()

    def end_sems(self):
        for s in self.old:
            self.nc.release_semaphore(s)
        self.old, self.fresh = self.fresh, []

    def clear_old(self, g):
        for s in self.old:
            g.sem_clear(s)

    def sb(self, name, shape, dt=F32, keep=False):
        return (self.ctx if keep else self.phase).enter_context(self.nc.sbuf_tensor(name, shape, dt))

    def sem(self, name, keep=False):
        if keep:
            return self.ctx.enter_context(self.nc.semaphore(name))
        self.fresh.append(self.nc.alloc_semaphore(name=name))
        return self.fresh[-1]


def carry(eng, n):
    if not isinstance(n, int):
        eng.sem_inc(TICKS.get(eng.engine, TICKS[None]), 1)


TICKS = {}


def bc(ap, axis, shape):
    return ap.unsqueeze(axis).broadcast_to(shape)


def rsqrt_steps(link, v, y, t, x):
    v.tensor_scalar(y.bitcast(I32), x.bitcast(I32), -0.5, 1597463007.0, ALU.mult, ALU.add).then_inc(link.sem, 1)
    v.wait_ge(link.sem, link.step())
    for _ in range(4):
        v.tensor_tensor(t, y, y, ALU.mult).then_inc(link.sem, 1)
        v.wait_ge(link.sem, link.step())
        v.tensor_tensor(t, t, x, ALU.mult).then_inc(link.sem, 1)
        v.wait_ge(link.sem, link.step())
        v.tensor_scalar(t, t, -0.5, 1.5, ALU.mult, ALU.add).then_inc(link.sem, 1)
        v.wait_ge(link.sem, link.step())
        v.tensor_tensor(y, y, t, ALU.mult).then_inc(link.sem, 1)
        v.wait_ge(link.sem, link.step())


RSQRT_STEPS = 17


def transpose_and_split(k, tag, src_ready, natural):
    nc, ps, h, ident = k.nc, k.ps, k.h, k.ident
    turned, hi_done, lo_done = (k.sem(tag + n) for n in ("_turned", "_hi_done", "_lo_done"))

    def out_view(a, tt, d4):
        o = a[:, d4 * 4:d4 * 4 + 4, :]
        if natural:
            return o.rearrange("p d (c s) -> p d s c", s=NT)[:, :, tt, :]
        return o[:, :, tt * P:(tt + 1) * P]

    def bank(n):
        return ps[:, 4 + n % 4, :].rearrange("p (d c) -> p d c", d=4)

    def pe(t):
        for n in range(2 * NT):
            tt, d4 = n // 2, n % 2
            src_ready(t, tt)
            if n >= 4:
                t.wait_ge(lo_done, n - 3)
            for q in range(4):
                d = d4 * 4 + q
                ins = t.transpose(ps[:, 4 + n % 4, q * P:(q + 1) * P], h[:, tt, d * P:(d + 1) * P], ident[:, :])
            ins.then_inc(turned, 1)

    def act(a):
        for n in range(2 * NT):
            a.wait_ge(turned, n + 1)
            split_hi(a, out_view(k.aT_hi, n // 2, n % 2), bank(n)).then_inc(hi_done, 1)

    def dve(v):
        for n in range(2 * NT):
            v.wait_ge(hi_done, n + 1)
            v.tensor_tensor(out_view(k.aT_lo, n // 2, n % 2), bank(n),
                            out_view(k.aT_hi, n // 2, n % 2).bitcast(F32), ALU.subtract).then_inc(lo_done, 1)

    return pe, act, dve, lo_done


def layer_norm_block(k, tag, gamma, beta, out=None, natural=False, spill=None):
    nc, h = k.nc, k.h
    k.open()
    g_row, b_row = k.sb(tag + "_g", [P, D]), k.sb(tag + "_b", [P, D])
    stats = k.sb(tag + "_stats", [P, NT, 2, 6])
    mv = k.sb(tag + "_mv", [P, NT, 2])
    var, y, tmp = (k.sb(tag + n, [P, NT]) for n in ("_var", "_y", "_tmp"))
    loaded, chain, scaled, normed, stored, raised = (
        k.sem(tag + n) for n in ("_loaded", "_chain", "_scaled", "_normed", "_stored", "_raised"))
    if out is None:
        pe_t, act_t, dve_t, lo_done = transpose_and_split(
            k, tag, lambda t, tt: t.wait_ge(normed, tt + 1), natural)
    with nc.Block() as block:
        @block.sync
        def _(s):
            s.dma_start(g_row[:, :], gamma.partition_broadcast(P)).then_inc(loaded, 16)
            s.dma_start(b_row[:, :], beta.partition_broadcast(P)).then_inc(loaded, 16)
            if out is not None:
                rows = out.rearrange("(p s) d -> p s d", s=NT)
                for tt in range(NT):
                    s.wait_ge(normed, tt + 1)
                    s.dma_start(rows[:, tt, :], h[:, tt, :]).then_inc(stored, 16)
                s.wait_ge(stored, 16 * NT)
            elif spill is not None:
                for tt in range(NT):
                    s.wait_ge(raised, tt + 1)
                    s.dma_start(spill[:, tt, :], h[:, tt, :]).then_inc(stored, 16)
                s.wait_ge(stored, 16 * NT)

        @block.vector
        def _(v):
            link = Steps(chain)
            for tt in range(NT):
                for q in range(2):
                    v.bn_stats(stats[:, tt, q, :], h[:, tt, q * HALF:(q + 1) * HALF]).then_inc(chain, 1)
                    link.step()
            v.wait_ge(chain, link.count())
            for tt in range(NT):
                v.bn_aggr(mv[:, tt, :], stats[:, tt, :, :].rearrange("p a b -> p (a b)")).then_inc(chain, 1)
                link.step()
            v.wait_ge(chain, link.count())
            v.tensor_scalar(var[:, :], mv[:, :, 1], LN_EPS, None, ALU.add).then_inc(chain, 1)
            v.wait_ge(chain, link.step())
            rsqrt_steps(link, v, y[:, :], tmp[:, :], var[:, :])
            for tt in range(NT):
                v.tensor_scalar(h[:, tt, :], h[:, tt, :], mv[:, tt, 0:1], y[:, tt:tt + 1],
                                ALU.subtract, ALU.mult).then_inc(chain, 1)
                v.wait_ge(chain, link.step())
                if tt == 0:
                    v.wait_ge(loaded, 32)
                v.tensor_tensor(h[:, tt, :], h[:, tt, :], g_row[:, :], ALU.mult).then_inc(scaled, 1)
            if out is None:
                dve_t(v)

        @block.gpsimd
        def _(g):
            k.clear_old(g)
            g.wait_ge(loaded, 32)
            for tt in range(NT):
                g.wait_ge(scaled, tt + 1)
                g.tensor_tensor(h[:, tt, :], h[:, tt, :], b_row[:, :], ALU.add).then_inc(normed, 1)
            if out is None:
                for tt in range(NT):
                    g.wait_ge(lo_done, 2 * tt + 2)
                    g.tensor_scalar(h[:, tt, :], h[:, tt, :], ALPHA, None, ALU.mult).then_inc(raised, 1)

        if out is None:
            @block.tensor
            def _(t):
                pe_t(t)

            @block.scalar
            def _(a):
                act_t(a)
    k.close()


def ffn_block(k, tag, w_in, w_out):
    nc, ps, h = k.nc, k.ps, k.h
    k.open()
    w1_raw = [k.sb(f"{tag}_w1_raw{b}", [P, 2, KT, P]) for b in range(2)]
    w1_hi = [k.sb(f"{tag}_w1_hi{b}", [P, 2, KT, P], F32R) for b in range(2)]
    w1_lo = [k.sb(f"{tag}_w1_lo{b}", [P, 2, KT, P], F32R) for b in range(2)]
    w2_raw = k.sb(tag + "_w2_raw", [P, FG, D])
    w2_hi = k.sb(tag + "_w2_hi", [P, FG, D], F32R)
    w2_lo = k.sb(tag + "_w2_lo", [P, FG, D], F32R)
    hid_hi = k.sb(tag + "_hid_hi", [P, FG, T], F32R)
    hid_lo = k.sb(tag + "_hid_lo", [P, FG, T], F32R)
    act_out = [k.sb(f"{tag}_act_out{b}", [P, HALF]) for b in range(2)]
    s_w1 = [k.sem(f"{tag}_w1_loaded{b}") for b in range(2)]
    s_w1h = [k.sem(f"{tag}_w1_hi_done{b}") for b in range(2)]
    s_w1l = [k.sem(f"{tag}_w1_lo_done{b}") for b in range(2)]
    s_w2, s_w2h, s_w2l = (k.sem(tag + n) for n in ("_w2_loaded", "_w2_hi_done", "_w2_lo_done"))
    s_unit, s_silu, s_prod, s_hh, s_hl, s_tile, s_acc = (
        k.sem(tag + n) for n in ("_unit_done", "_silu_done", "_prod_done", "_hid_hi_done", "_hid_done",
                                 "_out_tile_done", "_acc_done"))
    w_in_v = w_in.rearrange("(k p) (a n) -> p a k n", p=P, a=2)
    w_out_v = w_out.rearrange("(f p) d -> p f d", p=P)
    U = 2 * FG
    NOUT = 2 * NT

    with nc.Block() as block:
        @block.sync
        def _(s):
            def load_w1(i, q):
                for a in range(2):
                    s.dma_start(w1_raw[q][:, a, :, :], w_in_v[:, a, :, ds((i * FG + q) * P, P)]).then_inc(s_w1[q], 16)

            def load_w2(i):
                s.dma_start(w2_raw[:, :, :], w_out_v[:, ds(i * FG, FG), :]).then_inc(s_w2, 16)

            for q in range(FG):
                load_w1(0, q)
            load_w2(0)
            with s.Fori(1, NG) as i:
                for q in range(FG):
                    s.wait_ge(s_w1l[q], i)
                    carry(s, i)
                    load_w1(i, q)
                s.wait_ge(s_w2l, i)
                carry(s, i)
                load_w2(i)

        @block.tensor
        def _(t):
            def unit(i, u):
                q, half, b = u // 2, u % 2, u % 2
                if half == 0:
                    t.wait_ge(s_w1l[q], i + 1)
                if isinstance(i, int) and i == 0 and u < 2:
                    pass
                else:
                    t.wait_ge(s_prod, i * U + u - 1)
                for a in range(2):
                    for kk in range(KT):
                        rows = slice(half * HALF, (half + 1) * HALF)
                        for m, (w, x) in enumerate(((w1_hi, k.aT_hi), (w1_hi, k.aT_lo), (w1_lo, k.aT_hi))):
                            ins = t.matmul(ps[:, 2 * b + a, :], w[q][:, a, kk, :], x[:, kk, rows],
                                           start=(kk == 0 and m == 0), stop=(kk == KT - 1 and m == 2))
                ins.then_inc(s_unit, 1)

            def outputs(i):
                t.wait_ge(s_hl, (i + 1) * U)
                t.wait_ge(s_w2l, i + 1)
                for m in range(NOUT):
                    tt, dh = m // 2, m % 2
                    if not (isinstance(i, int) and i == 0 and m < 4):
                        t.wait_ge(s_acc, i * NOUT + m - 3)
                    for q in range(FG):
                        for n, (x, w) in enumerate(((hid_hi, w2_hi), (hid_hi, w2_lo), (hid_lo, w2_hi))):
                            ins = t.matmul(ps[:, 4 + m % 4, :], x[:, q, tt * P:(tt + 1) * P],
                                           w[:, q, dh * HALF:(dh + 1) * HALF],
                                           start=(q == 0 and n == 0), stop=(q == FG - 1 and n == 2))
                    ins.then_inc(s_tile, 1)

            def group(i):
                for u in range(1, U):
                    unit(i, u)
                unit(i + 1, 0)
                outputs(i)

            unit(0, 0)
            group(0)
            with t.Fori(1, NG - 1) as i:
                group(i)
            for u in range(1, U):
                unit(NG - 1, u)
            outputs(NG - 1)

        @block.scalar
        def _(a):
            def split_w1(i, q):
                a.wait_ge(s_w1[q], 32 * (i + 1))
                carry(a, i)
                if not (isinstance(i, int) and i == 0):
                    a.wait_ge(s_unit, (i - 1) * U + 2 * q + 2)
                    carry(a, i)
                split_hi(a, w1_hi[q][:, :, :, :], w1_raw[q][:, :, :, :]).then_inc(s_w1h[q], 1)

            def split_w2(i):
                a.wait_ge(s_w2, 16 * (i + 1))
                carry(a, i)
                if not (isinstance(i, int) and i == 0):
                    a.wait_ge(s_tile, i * NOUT)
                    carry(a, i)
                split_hi(a, w2_hi[:, :, :], w2_raw[:, :, :]).then_inc(s_w2h, 1)

            def silu(i, u):
                a.wait_ge(s_unit, i * U + u + 1)
                carry(a, i)
                if not (isinstance(i, int) and i == 0 and u < 2):
                    a.wait_ge(s_hl, i * U + u - 1)
                    carry(a, i)
                a.activation(act_out[u % 2][:, :], ps[:, 2 * (u % 2), :], ACT.Silu).then_inc(s_silu, 1)

            def group(i, more):
                silu(i, 1)
                if more:
                    split_w1(i + 1, 0)
                silu(i, 2)
                silu(i, 3)
                if more:
                    split_w1(i + 1, 1)
                    silu(i + 1, 0)
                    split_w2(i + 1)

            split_w1(0, 0)
            split_w1(0, 1)
            split_w2(0)
            silu(0, 0)
            group(0, True)
            with a.Fori(1, NG - 1) as i:
                group(i, True)
            group(NG - 1, False)

        @block.vector
        def _(v):
            def split_w1(i, q):
                v.wait_ge(s_w1h[q], i + 1)
                v.tensor_tensor(w1_lo[q][:, :, :, :], w1_raw[q][:, :, :, :],
                                w1_hi[q][:, :, :, :].bitcast(F32), ALU.subtract).then_inc(s_w1l[q], 1)

            def product(i, u):
                v.wait_ge(s_silu, i * U + u + 1)
                v.tensor_tensor(act_out[u % 2][:, :], act_out[u % 2][:, :], ps[:, 2 * (u % 2) + 1, :],
                                ALU.mult).then_inc(s_prod, 1)

            def accumulate(i):
                if not (isinstance(i, int) and i == 0):
                    v.wait_ge(s_acc, i * NOUT)
                for m in range(NOUT):
                    tt, dh = m // 2, m % 2
                    v.wait_ge(s_tile, i * NOUT + m + 1)
                    part = h[:, tt, dh * HALF:(dh + 1) * HALF]
                    v.tensor_tensor(part, part, ps[:, 4 + m % 4, :], ALU.add).then_inc(s_acc, 1)

            def group(i, more):
                product(i, 1)
                if more:
                    split_w1(i + 1, 0)
                product(i, 2)
                product(i, 3)
                if more:
                    split_w1(i + 1, 1)
                    product(i + 1, 0)
                accumulate(i)

            split_w1(0, 0)
            split_w1(0, 1)
            product(0, 0)
            group(0, True)
            with v.Fori(1, NG - 1) as i:
                group(i, True)
            group(NG - 1, False)

        @block.gpsimd
        def _(g):
            k.clear_old(g)
            def split_w2(i):
                g.wait_ge(s_w2h, i + 1)
                carry(g, i)
                g.tensor_tensor(w2_lo[:, :, :], w2_raw[:, :, :], w2_hi[:, :, :].bitcast(F32),
                                ALU.subtract).then_inc(s_w2l, 1)

            def hidden(i, u):
                g.wait_ge(s_prod, i * U + u + 1)
                carry(g, i)
                q, half = u // 2, u % 2
                if not (isinstance(i, int) and i == 0) and u == 0:
                    g.wait_ge(s_tile, i * NOUT)
                    carry(g, i)
                cols = slice(half * HALF, (half + 1) * HALF)
                g.tensor_copy(hid_hi[:, q, cols], act_out[u % 2][:, :]).then_inc(s_hh, 1)
                g.wait_ge(s_hh, i * U + u + 1)
                carry(g, i)
                g.tensor_tensor(hid_lo[:, q, cols], act_out[u % 2][:, :], hid_hi[:, q, cols].bitcast(F32),
                                ALU.subtract).then_inc(s_hl, 1)

            def group(i, more):
                for u in range(1, U):
                    hidden(i, u)
                if more:
                    hidden(i + 1, 0)
                    split_w2(i + 1)

            split_w2(0)
            hidden(0, 0)
            group(0, True)
            with g.Fori(1, NG - 1) as i:
                group(i, True)
            group(NG - 1, False)
    k.close()


def out_projection_block(k, tag, w, residual, scale, natural):
    nc, ps, h, x_hi, x_lo = k.nc, k.ps, k.h, k.aT_hi, k.aT_lo
    k.open()
    w_raw = [k.sb(f"{tag}_w_raw{b}", [P, KT, HALF]) for b in range(2)]
    w_hi = [k.sb(f"{tag}_w_hi{b}", [P, KT, HALF], F32R) for b in range(2)]
    w_lo = [k.sb(f"{tag}_w_lo{b}", [P, KT, HALF], F32R) for b in range(2)]
    loaded = [k.sem(f"{tag}_w_loaded{b}") for b in range(2)]
    back = [k.sem(f"{tag}_h_back{b}") for b in range(2)]
    x_h, x_l, w_h, w_l, w_l1, scaled, tile, acc = (
        k.sem(tag + n) for n in ("_x_hi_done", "_x_lo_done", "_w_hi_done", "_w_lo_done", "_w_lo1_done",
                                 "_scaled", "_tile_done", "_acc_done"))
    w_v = w.rearrange("(k p) d -> p k d", p=P)

    def cut(a, kk, source):
        if source and natural:
            return a[:, kk, :].rearrange("p (c s) -> p s c", s=NT)
        return a[:, kk, :].rearrange("p (s c) -> p s c", s=NT)

    with nc.Block() as block:
        @block.sync
        def _(s):
            for b in range(2):
                s.dma_start(w_raw[b][:, :, :], w_v[:, :, b * HALF:(b + 1) * HALF]).then_inc(loaded[b], 16)
            s.wait_ge(x_l, KT)
            for b in range(2):
                tts = slice(4 * b, 4 * b + 4)
                s.dma_start(h[:, tts, :], residual[:, tts, :]).then_inc(back[b], 16)

        @block.scalar
        def _(a):
            for b in range(2):
                a.wait_ge(loaded[b], 16)
                for kk in range(KT):
                    split_hi(a, w_hi[b][:, kk, :], w_raw[b][:, kk, :]).then_inc(w_h, 1)
                    if b == 0:
                        split_hi(a, cut(x_hi, kk, False), cut(h, kk, True)).then_inc(x_h, 1)
            for tt in range(NT):
                if tt % 4 == 0:
                    a.wait_ge(back[tt // 4], 16)
                a.activation(h[:, tt, :], h[:, tt, :], ACT.Copy, scale=scale).then_inc(scaled, 1)

        @block.vector
        def _(v):
            for kk in range(KT):
                v.wait_ge(w_h, kk + 1)
                v.tensor_tensor(w_lo[0][:, kk, :], w_raw[0][:, kk, :], w_hi[0][:, kk, :].bitcast(F32),
                                ALU.subtract).then_inc(w_l, 1)
            for m in range(2 * NT):
                dh, tt = m // NT, m % NT
                v.wait_ge(scaled, tt + 1)
                v.wait_ge(tile, m + 1)
                part = h[:, tt, dh * HALF:(dh + 1) * HALF]
                v.tensor_tensor(part, part, ps[:, m % 8, :], ALU.add).then_inc(acc, 1)

        @block.gpsimd
        def _(g):
            k.clear_old(g)
            for kk in range(KT):
                g.wait_ge(x_h, kk + 1)
                g.tensor_tensor(cut(x_lo, kk, False), cut(h, kk, True), cut(x_hi, kk, False).bitcast(F32),
                                ALU.subtract).then_inc(x_l, 1)
            for kk in range(KT):
                g.wait_ge(w_h, KT + kk + 1)
                g.tensor_tensor(w_lo[1][:, kk, :], w_raw[1][:, kk, :], w_hi[1][:, kk, :].bitcast(F32),
                                ALU.subtract).then_inc(w_l1, 1)

        @block.tensor
        def _(t):
            for m in range(2 * NT):
                dh, tt = m // NT, m % NT
                if m >= 8:
                    t.wait_ge(acc, m - 7)
                for kk in range(KT):
                    if m == 0:
                        t.wait_ge(x_l, kk + 1)
                    if tt == 0:
                        t.wait_ge(w_l1 if dh else w_l, kk + 1)
                    for n, (x, ww) in enumerate(((x_hi, w_hi), (x_hi, w_lo), (x_lo, w_hi))):
                        ins = t.matmul(ps[:, m % 8, :], x[:, kk, tt * P:(tt + 1) * P], ww[dh][:, kk, :],
                                       start=(kk == 0 and n == 0), stop=(kk == KT - 1 and n == 2))
                ins.then_inc(tile, 1)
    k.close()


def complex_product(link, e, out_re, out_im, a_re, a_im, b_re, b_im, t):
    for out, other, first, second, join in ((out_re, t, (a_re, b_re), (a_im, b_im), ALU.subtract),
                                            (out_im, t, (a_re, b_im), (a_im, b_re), ALU.add)):
        e.tensor_tensor(out, first[0], first[1], ALU.mult).then_inc(link.sem, 1)
        link.step()
        e.tensor_tensor(other, second[0], second[1], ALU.mult).then_inc(link.sem, 1)
        e.wait_ge(link.sem, link.step())
        carry(e, link.base)
        e.tensor_tensor(out, out, other, join).then_inc(link.sem, 1)
        e.wait_ge(link.sem, link.step())
        carry(e, link.base)


def s5_tables_block(k, x_rows, lam_re, lam_im, log_step, b_glu, d_skip, consts):
    nc, ps, h = k.nc, k.ps, k.h
    N = KT * DP
    rows = {n: k.sb("s5_rows_" + n, [N, P]) for n in ("re", "im", "re_dt", "im_dt")}
    ls, th, em, step = (k.sb("s5_step" + n, [N, 2]) for n in "abcd")
    lam = {n: k.sb("s5_lam_" + n, [P, N]) for n in ("re", "im", "re_dt", "im_dt")}
    w = {n: k.sb("s5_w_" + n, [P, N]) for n in ("t", "q", "r", "half", "sin", "cos", "c1", "tanh", "em",
                                                  "e", "m_re", "den", "inv")}
    asc = k.sb("s5_asc", [P, 2, N, L + 1])
    tmp4 = k.sb("s5_tmp4", [P, N, 4])
    x_in = [k.sem(f"s5_x_loaded{b}") for b in range(2)]
    p_in, chain, a_chain, p_turned = (k.sem("s5_" + n) for n in ("par_loaded", "tab_chain", "tab_act", "par_turned"))
    pe_t, act_t, dve_t, _ = transpose_and_split(
        k, "s5_x", lambda t, tt: t.wait_ge(x_in[tt // 4], 16), False)
    lam_rows = {"re": lam_re, "im": lam_im}
    ROWS_READY = 8 + 2
    LAM_READY = ROWS_READY + 4 + 7

    with nc.Block() as block:
        @block.gpsimd
        def _(g):
            k.clear_old(g)

        @block.sync
        def _(s):
            s.dma_start(k.ident[:, :], consts["ident"]).then_inc(p_in, 16)
            for b in range(2):
                tts = slice(4 * b, 4 * b + 4)
                s.dma_start(h[:, tts, :], x_rows[:, tts, :]).then_inc(x_in[b], 16)
            for n in ("re", "im"):
                s.dma_start(rows[n][:, :], lam_rows[n].rearrange("r (a b) p -> (r a) (b p)", b=2)).then_inc(p_in, 16)
            s.dma_start(ls[:, :], log_step.rearrange("r (a b) -> (r a) b", b=2)).then_inc(p_in, 16)
            s.dma_start(k.d_col[:, :], d_skip.rearrange("(j p) -> p j", p=P),
                        allow_slow_non_contiguous=True).then_inc(p_in, 16)
            s.dma_start(k.glu_col[:, :], b_glu.rearrange("(j p) -> p j", p=P),
                        allow_slow_non_contiguous=True).then_inc(p_in, 16)


        @block.tensor
        def _(t):
            t.wait_ge(p_in, 6 * 16)
            pe_t(t)
            t.wait_ge(chain, ROWS_READY)
            for q, n in enumerate(("re", "im", "re_dt", "im_dt")):
                ins = t.transpose(ps[:, 0, q * N:(q + 1) * N], rows[n][:, :], k.ident[0:N, 0:N])
            ins.then_inc(p_turned, 1)

        @block.scalar
        def _(a):
            act_t(a)
            a.wait_ge(p_in, 6 * 16)
            a.activation(th[:, :], ls[:, :], ACT.Tanh, scale=1.0 / 32).then_inc(a_chain, 1)
            a.wait_ge(chain, LAM_READY)
            a.activation(w["half"][:, :], w["r"][:, :], ACT.Sin, scale=0.5).then_inc(a_chain, 1)
            a.activation(w["sin"][:, :], w["r"][:, :], ACT.Sin).then_inc(a_chain, 1)
            a.activation(w["tanh"][:, :], lam["re_dt"][:, :], ACT.Tanh, scale=0.5).then_inc(a_chain, 1)

        @block.vector
        def _(v):
            dve_t(v)
            link = Steps(chain)
            v.wait_ge(a_chain, 1)
            v.tensor_scalar(em[:, :], th[:, :], -1.0, 1.0, ALU.mult, ALU.add).then_inc(chain, 1)
            v.wait_ge(chain, link.step())
            v.reciprocal(em[:, :], em[:, :]).then_inc(chain, 1)
            v.wait_ge(chain, link.step())
            v.tensor_scalar(step[:, :], th[:, :], 1.0, None, ALU.add).then_inc(chain, 1)
            v.wait_ge(chain, link.step())
            v.tensor_tensor(step[:, :], step[:, :], em[:, :], ALU.mult).then_inc(chain, 1)
            v.wait_ge(chain, link.step())
            for _ in range(4):
                v.tensor_tensor(step[:, :], step[:, :], step[:, :], ALU.mult).then_inc(chain, 1)
                v.wait_ge(chain, link.step())

            for n in ("re", "im"):
                v.tensor_tensor(rows[n + "_dt"][:, :].rearrange("r (b p) -> r b p", b=2),
                                rows[n][:, :].rearrange("r (b p) -> r b p", b=2),
                                bc(step[:, :], 2, [N, 2, ST]), ALU.mult).then_inc(chain, 1)
                v.wait_ge(chain, link.step())
            assert link.n == ROWS_READY
            v.wait_ge(p_turned, 1)
            for q, n in enumerate(("re", "im", "re_dt", "im_dt")):
                v.tensor_copy(lam[n][:, :].rearrange("p (j d r) -> p d j r", d=2, r=PR),
                              ps[:, 0, q * N:(q + 1) * N].rearrange("p (d j r) -> p d j r", d=2, r=PR)).then_inc(chain, 1)
                v.wait_ge(chain, link.step())
            round_by, c1, c2 = 1.5 * 2.0 ** 23, 6.28125, 2.0 ** -9 - 2.0 ** -14
            c2 = float(np.float32(round((2 * math.pi - c1) * 2 ** 20) / 2 ** 20))
            c3 = float(2 * math.pi - c1 - c2)
            q_, r_ = w["q"][:, :], w["r"][:, :]
            v.tensor_scalar(q_, lam["im_dt"][:, :], 1.0 / (2 * math.pi), round_by, ALU.mult, ALU.add).then_inc(chain, 1)
            v.wait_ge(chain, link.step())
            v.tensor_scalar(q_, q_, -round_by, None, ALU.add).then_inc(chain, 1)
            v.wait_ge(chain, link.step())
            v.scalar_tensor_tensor(r_, q_, -c1, lam["im_dt"][:, :], ALU.mult, ALU.add).then_inc(chain, 1)
            v.wait_ge(chain, link.step())
            v.scalar_tensor_tensor(r_, q_, -c2, r_, ALU.mult, ALU.add).then_inc(chain, 1)
            v.wait_ge(chain, link.step())
            v.scalar_tensor_tensor(r_, q_, -c3, r_, ALU.mult, ALU.add).then_inc(chain, 1)
            v.wait_ge(chain, link.step())
            v.tensor_scalar(r_, r_, 3.1415925, -3.1415925, ALU.min, ALU.max).then_inc(chain, 1)
            v.wait_ge(chain, link.step())
            v.tensor_tensor(w["den"][:, :], lam["re"][:, :], lam["re"][:, :], ALU.mult).then_inc(chain, 1)
            v.wait_ge(chain, link.step())
            assert link.n == LAM_READY
            v.wait_ge(a_chain, 4)
            W = {n: w[n][:, :] for n in w}
            v.tensor_tensor(W["c1"], W["half"], W["half"], ALU.mult).then_inc(chain, 1)
            v.wait_ge(chain, link.step())
            v.tensor_scalar(W["c1"], W["c1"], -2.0, None, ALU.mult).then_inc(chain, 1)
            v.wait_ge(chain, link.step())
            v.tensor_scalar(W["cos"], W["c1"], 1.0, None, ALU.add).then_inc(chain, 1)
            v.wait_ge(chain, link.step())
            v.tensor_scalar(W["t"], W["tanh"], -1.0, 1.0, ALU.mult, ALU.add).then_inc(chain, 1)
            v.wait_ge(chain, link.step())
            v.reciprocal(W["t"], W["t"]).then_inc(chain, 1)
            v.wait_ge(chain, link.step())
            v.scalar_tensor_tensor(W["em"], W["tanh"], 2.0, W["t"], ALU.mult, ALU.mult).then_inc(chain, 1)
            v.wait_ge(chain, link.step())
            v.tensor_scalar(W["e"], W["em"], 1.0, None, ALU.add).then_inc(chain, 1)
            v.wait_ge(chain, link.step())
            A = lambda ri, lo, hi: asc[:, ri, :, lo:hi]
            v.memset(asc[:, 0, :, 0], 1.0).then_inc(chain, 1)
            v.wait_ge(chain, link.step())
            v.memset(asc[:, 1, :, 0], 0.0).then_inc(chain, 1)
            v.wait_ge(chain, link.step())
            v.tensor_tensor(asc[:, 0, :, 1], W["e"], W["cos"], ALU.mult).then_inc(chain, 1)
            v.wait_ge(chain, link.step())
            v.tensor_tensor(asc[:, 1, :, 1], W["e"], W["sin"], ALU.mult).then_inc(chain, 1)
            v.wait_ge(chain, link.step())
            for lo, hi, by in ((1, 2, 1), (1, 3, 2), (1, 5, 4)):
                n = hi - lo
                z = [bc(asc[:, ri, :, by], 2, [P, N, n]) for ri in range(2)]
                complex_product(link, v, A(0, by + lo, by + hi), A(1, by + lo, by + hi),
                                A(0, lo, hi), A(1, lo, hi), z[0], z[1], tmp4[:, :, 0:n])
            byd = lambda a: a.rearrange("p (j d r) k -> p j d r k", d=2, r=PR)
            for ri in range(2):
                src = byd(asc[:, ri, :, :])
                v.tensor_copy(byd(k.pw[:, ri, :, :])[:, :, 0], src[:, :, 0]).then_inc(chain, 1)
                v.wait_ge(chain, link.step())
                v.tensor_copy(byd(k.pw[:, ri, :, :])[:, :, 1], src[:, :, 1, :, ::-1]).then_inc(chain, 1)
                v.wait_ge(chain, link.step())
                v.tensor_copy(byd(k.pw_in[:, ri, :, :])[:, :, 0], src[:, :, 0, :, L - 1::-1]).then_inc(chain, 1)
                v.wait_ge(chain, link.step())
                v.tensor_copy(byd(k.pw_in[:, ri, :, :])[:, :, 1], src[:, :, 1, :, 0:L]).then_inc(chain, 1)
                v.wait_ge(chain, link.step())
            v.tensor_scalar(k.pw[:, 2, :, :], k.pw[:, 1, :, :], -1.0, None, ALU.mult).then_inc(chain, 1)
            v.wait_ge(chain, link.step())
            for ri in range(2):
                v.tensor_copy(k.mu[:, 0, ri, :], asc[:, ri, :, L]).then_inc(chain, 1)
                v.wait_ge(chain, link.step())
            for lv in range(1, LV):
                a_, b_ = k.mu[:, lv - 1, 0, :], k.mu[:, lv - 1, 1, :]
                complex_product(link, v, k.mu[:, lv, 0, :], k.mu[:, lv, 1, :], a_, b_, a_, b_, W["t"])
            v.tensor_scalar(k.mu[:, :, 2, :], k.mu[:, :, 1, :], -1.0, None, ALU.mult).then_inc(chain, 1)
            v.wait_ge(chain, link.step())
            v.tensor_tensor(W["m_re"], W["em"], W["cos"], ALU.mult).then_inc(chain, 1)
            v.wait_ge(chain, link.step())
            v.tensor_tensor(W["m_re"], W["m_re"], W["c1"], ALU.add).then_inc(chain, 1)
            v.wait_ge(chain, link.step())
            m_im = asc[:, 1, :, 1]
            v.tensor_tensor(W["t"], lam["im"][:, :], lam["im"][:, :], ALU.mult).then_inc(chain, 1)
            v.wait_ge(chain, link.step())
            v.tensor_tensor(W["den"], W["den"], W["t"], ALU.add).then_inc(chain, 1)
            v.wait_ge(chain, link.step())
            v.reciprocal(W["inv"], W["den"]).then_inc(chain, 1)
            v.wait_ge(chain, link.step())
            l_re, l_im = lam["re"][:, :], lam["im"][:, :]
            v.tensor_tensor(W["t"], W["m_re"], l_re, ALU.mult).then_inc(chain, 1)
            v.wait_ge(chain, link.step())
            v.tensor_tensor(W["q"], m_im, l_im, ALU.mult).then_inc(chain, 1)
            v.wait_ge(chain, link.step())
            v.tensor_tensor(W["t"], W["t"], W["q"], ALU.add).then_inc(chain, 1)
            v.wait_ge(chain, link.step())
            v.tensor_tensor(k.coef[:, 0, :], W["t"], W["inv"], ALU.mult).then_inc(chain, 1)
            v.wait_ge(chain, link.step())
            v.tensor_tensor(W["t"], m_im, l_re, ALU.mult).then_inc(chain, 1)
            v.wait_ge(chain, link.step())
            v.tensor_tensor(W["q"], W["m_re"], l_im, ALU.mult).then_inc(chain, 1)
            v.wait_ge(chain, link.step())
            v.tensor_tensor(W["t"], W["t"], W["q"], ALU.subtract).then_inc(chain, 1)
            v.wait_ge(chain, link.step())
            v.tensor_tensor(k.coef[:, 1, :], W["t"], W["inv"], ALU.mult).then_inc(chain, 1)
            v.wait_ge(chain, link.step())


def s5_scan_block(k, w_in, b_re, b_im, c_re, c_im):
    nc, ps, h = k.nc, k.ps, k.h
    w_raw = k.sb("s5_w_raw", [P, KT, P])
    w_hi, w_lo = k.sb("s5_w_hi", [P, KT, P], F32R), k.sb("s5_w_lo", [P, KT, P], F32R)
    b_raw = k.sb("s5_b_raw", [P, 2, DP, GRP])
    c_raw = k.sb("s5_c_raw", [PR * GRP, 2, 2, P])
    c_t = k.sb("s5_c_t", [P, 2, DP, GRP])
    b_bar = k.sb("s5_b_bar", [P, 2, DP, GRP])
    gen_t = k.sb("s5_gen_t", [P, DP, L + 1, GRP])
    cl = [k.sb(f"s5_cl{b}", [P, 2, DP, L + 1, GRP]) for b in range(2)]
    bl = k.sb("s5_bl", [P, 2, DP, L, GRP])
    minm = k.sb("s5_min", [P, 2, DP, P])
    kern = k.sb("s5_kern", [P, 2, P])
    kern_rows = k.sb("s5_kern_rows", [P, 2 * L - 1, GRP])
    toep = k.sb("s5_toep", [P, GJ, P])
    u_grp = [k.sb(f"s5_u_grp{b}", [P, GJ, NC]) for b in range(2)]
    state = k.sb("s5_state", [P, DP, 2, NC + 2])
    sc1, sc2 = (k.sb("s5_scan_t" + n, [P, DP, 2, NC // 2]) for n in "12")
    y_grp, y_pre = k.sb("s5_y_grp", [P, GJ, NC]), k.sb("s5_y_pre", [P, T])
    S = {n: k.sem("s5_" + n) for n in (
        "w_loaded", "b_loaded", "c_loaded", "w_hi_done", "w_lo_done", "c_turned", "c_t_done", "u_done",
        "u_kept", "gen", "kern_done", "kern_kept", "kern_turned", "u_out", "kern_out", "y_out", "kern_rows_kept",
        "kern_rows_done", "bl_turned", "min_kept", "u_grouped", "toep_placed", "in_done", "state_kept",
        "scan_chain", "pads", "out_done", "y_kept", "y_ungrouped", "y_sum", "y_done")}
    u_scr, k_scr, y_scr = (nc.dram_tensor("s5_scratch_" + n, (P, c), F32, kind="Internal").ap()
                           for n, c in (("u", T), ("kern", (2 * L - 1) * GRP), ("y", GJ * NC)))
    w_v = w_in.rearrange("(k p) n -> p k n", p=P)
    b_v = [x.rearrange("r (a b) p c -> (b p) r a c", b=2) for x in (b_re, b_im)]
    c_v = [x.rearrange("r (a b) c p -> r c a b p", b=2) for x in (c_re, c_im)]
    GEN = 24
    CL_STEPS = 12
    SCAN = 5 * (2 * LV - 1)

    def first(n):
        return isinstance(n, int) and n == 0

    with nc.Block() as block:
        @block.sync
        def _(s):
            def load(n):
                if not first(n):
                    s.wait_ge(S["w_lo_done"], n)
                    carry(s, n)
                s.dma_start(w_raw[:, :, :], w_v[:, :, ds(n * P, P)]).then_inc(S["w_loaded"], 16)
                if not first(n):
                    s.wait_ge(S["c_turned"], n)
                    carry(s, n)
                for ri in range(2):
                    for d in range(2):
                        for q in range(PR):
                            s.dma_start(c_raw[q * GRP:(q + 1) * GRP, ri, d, :].rearrange("c (b p) -> c b p", b=2),
                                        c_v[ri][d, :, ds(n * PR + q, 1)].rearrange("c a b p -> c (a b) p")
                                        ).then_inc(S["c_loaded"], 16)
                if not first(n):
                    s.wait_ge(S["gen"], n * GEN)
                    carry(s, n)
                for ri in range(2):
                    for d in range(2):
                        s.dma_start(b_raw[:, ri, d * PR:(d + 1) * PR, :],
                                    b_v[ri][:, d, ds(n * PR, PR), :]).then_inc(S["b_loaded"], 16)

            def regroup_u(n, b):
                s.wait_ge(S["u_kept"], 2 * n + 2)
                carry(s, n)
                if not (isinstance(n, int) and n < 2):
                    s.wait_ge(S["out_done"], n - 1)
                    carry(s, n)
                if not first(n):
                    s.wait_ge(S["u_grouped"], 16 * L * n)
                    carry(s, n)
                s.dma_start(u_scr, h[:, ds(n, 1), :].rearrange("p a c -> p (a c)")).then_inc(S["u_out"], 16)
                s.wait_ge(S["u_out"], 16 * (n + 1))
                carry(s, n)
                v = u_scr.rearrange("(g h) (s c) -> s h g c", g=GJ, s=L)
                for r in range(L):
                    s.dma_start(u_grp[b][r * GRP:(r + 1) * GRP, :, :], v[r]).then_inc(S["u_grouped"], 16)

            def place_toeplitz(n):
                s.wait_ge(S["kern_rows_done"], n + 1)
                carry(s, n)
                if not first(n):
                    s.wait_ge(S["out_done"], n)
                    carry(s, n)
                    s.wait_ge(S["toep_placed"], 16 * L * n)
                    carry(s, n)
                s.dma_start(k_scr, kern_rows[:, :, :].rearrange("p a c -> p (a c)")).then_inc(S["kern_out"], 16)
                s.wait_ge(S["kern_out"], 16 * (n + 1))
                carry(s, n)
                v = k_scr.rearrange("(g h) e -> h g e", g=GJ)
                for r in range(L):
                    s.dma_start(toep[r * GRP:(r + 1) * GRP, :, :],
                                v[:, :, (L - 1 - r) * GRP:(2 * L - 1 - r) * GRP]).then_inc(S["toep_placed"], 16)

            def ungroup_y(n):
                s.wait_ge(S["y_kept"], 2 * (n + 1))
                carry(s, n)
                if not first(n):
                    s.wait_ge(S["y_sum"], n)
                    carry(s, n)
                    s.wait_ge(S["y_ungrouped"], 16 * GJ * n)
                    carry(s, n)
                s.dma_start(y_scr, y_grp[:, :, :].rearrange("p a c -> p (a c)")).then_inc(S["y_out"], 16)
                s.wait_ge(S["y_out"], 16 * (n + 1))
                carry(s, n)
                v = y_scr.rearrange("(t h) (g c) -> g h t c", t=L, g=GJ)
                for g in range(GJ):
                    s.dma_start(y_pre[g * GRP:(g + 1) * GRP, :].rearrange("h (t c) -> h t c", t=L), v[g]
                                ).then_inc(S["y_ungrouped"], 16)

            load(0)
            regroup_u(0, 0)
            load(1)
            place_toeplitz(0)

            def tile_step(n, b, more):
                regroup_u(n + 1, b)
                if more:
                    load(n + 2)
                ungroup_y(n)
                place_toeplitz(n + 1)

            for b in range(2):
                tile_step(b, 1 - b, True)
            with s.Fori(1, KT // 2 - 1) as i:
                for b in range(2):
                    tile_step(2 * i + b, 1 - b, True)
            tile_step(KT - 2, 1, False)
            ungroup_y(KT - 1)

        @block.tensor
        def _(t):
            def produce(n, b):
                t.wait_ge(S["c_loaded"], 16 * 16 * (n + 1))
                carry(t, n)
                if not first(n):
                    t.wait_ge(S["c_t_done"], n)
                    carry(t, n)
                    t.wait_ge(S["kern_kept"], 2 * n)
                    carry(t, n)
                for ri in range(2):
                    for d in range(2):
                        m = ri * 2 + d
                        ins = t.transpose(ps[:, 2, m * 64:(m + 1) * 64], c_raw[:, ri, d, :],
                                          k.ident[0:PR * GRP, 0:PR * GRP])
                ins.then_inc(S["c_turned"], 1)
                t.wait_ge(S["w_lo_done"], n + 1)
                if not first(n):
                    t.wait_ge(S["u_kept"], 2 * n)
                    if not (isinstance(n, int) and n < 2):
                        t.wait_ge(S["y_kept"], 2 * n - 2)
                for half in range(2):
                    cols = slice(half * HALF, (half + 1) * HALF)
                    for kk in range(KT):
                        for m, (w, x) in enumerate(((w_hi, k.aT_hi), (w_hi, k.aT_lo), (w_lo, k.aT_hi))):
                            ins = t.matmul(ps[:, half, :], w[:, kk, :], x[:, kk, cols],
                                           start=(kk == 0 and m == 0), stop=(kk == KT - 1 and m == 2))
                    ins.then_inc(S["u_done"], 1)
                t.wait_ge(S["gen"], n * GEN + CL_STEPS)
                if not first(n):
                    t.wait_ge(S["kern_rows_done"], n)
                for d in range(2):
                    for g in range(GJ):
                        rows, dp = slice((g % 2) * ST, (g % 2 + 1) * ST), d * PR + g // 2
                        bank = 2 + g % 2
                        at = 256 + (d * PR + g // 2) * GRP
                        for ri in range(2):
                            ins = t.matmul(ps[:, bank, at:at + GRP],
                                           cl[b][rows, ri, dp, d:d + L, :].rearrange("p a c -> p (a c)"),
                                           b_bar[rows, ri, dp, :], start=(ri == 0), stop=(ri == 1))
                ins.then_inc(S["kern_done"], 1)
                t.wait_ge(S["gen"], (n + 1) * GEN)
                if not first(n):
                    t.wait_ge(S["state_kept"], 4 * n)
                for m in range(4):
                    for q in range(4):
                        ri, dp = m // 2, (m % 2) * 4 + q
                        ins = t.transpose(ps[:, 4 + m, q * P:(q + 1) * P],
                                          bl[:, ri, dp, :, :].rearrange("p s c -> p (s c)"), k.ident[:, :])
                    ins.then_inc(S["bl_turned"], 1)
                t.wait_ge(S["kern_kept"], 2 * (n + 1))
                if not first(n):
                    t.wait_ge(S["kern_rows_done"], n)
                for d in range(2):
                    ins = t.transpose(ps[:, 3, d * P:(d + 1) * P], kern[:, d, :], k.ident[:, :])
                ins.then_inc(S["kern_turned"], 1)
                t.wait_ge(S["u_grouped"], 16 * GJ * (n + 1))
                t.wait_ge(S["min_kept"], 4 * (n + 1))
                for m in range(4):
                    for dp in (2 * m, 2 * m + 1):
                        for ri in range(2):
                            at = ((dp % 2) * 2 + ri) * P
                            for g2 in range(2):
                                rows = slice(g2 * ST, (g2 + 1) * ST)
                                ins = t.matmul(ps[rows, 4 + m, at:at + P], minm[:, ri, dp, rows],
                                               u_grp[b][:, 2 * (dp % PR) + g2, :], start=True, stop=True)
                    ins.then_inc(S["in_done"], 1)

            def outputs(n, b):
                t.wait_ge(S["toep_placed"], 16 * L * (n + 1))
                t.wait_ge(S["scan_chain"], (n + 1) * SCAN)
                if not (isinstance(n, int) and n == KT - 1):
                    t.wait_ge(S["u_kept"], 2 * n + 4)
                else:
                    t.wait_ge(S["y_kept"], 2 * n)
                for g in range(GJ):
                    g2, pr = g % 2, g // 2
                    rows = slice(g2 * ST, (g2 + 1) * ST)
                    o = ps[:, g2, pr * P:(pr + 1) * P]
                    t.matmul(o, toep[:, g, :], u_grp[b][:, g, :], start=True, stop=False)
                    for ri in range(2):
                        t.matmul(o, cl[b][rows, ri, pr, 1:L + 1, :].rearrange("p a c -> p (a c)"),
                                 state[rows, pr, ri, 0:NC], start=False, stop=False)
                    for ri in range(2):
                        ins = t.matmul(o, cl[b][rows, ri, PR + pr, 0:L, :].rearrange("p a c -> p (a c)"),
                                       state[rows, PR + pr, ri, NC - 1::-1], start=False, stop=(ri == 1))
                ins.then_inc(S["out_done"], 1)

            produce(0, 0)
            for b in range(2):
                produce(b + 1, 1 - b)
                outputs(b, b)
            with t.Fori(1, KT // 2 - 1) as i:
                for b in range(2):
                    produce(2 * i + b + 1, 1 - b)
                    outputs(2 * i + b, b)
            produce(KT - 1, 1)
            outputs(KT - 2, 0)
            outputs(KT - 1, 1)

        @block.scalar
        def _(a):
            def produce(n):
                a.wait_ge(S["w_loaded"], 16 * (n + 1))
                carry(a, n)
                if not first(n):
                    a.wait_ge(S["u_done"], 2 * n)
                    carry(a, n)
                split_hi(a, w_hi[:, :, :], w_raw[:, :, :]).then_inc(S["w_hi_done"], 1)
                a.wait_ge(S["c_turned"], n + 1)
                carry(a, n)
                if not first(n):
                    a.wait_ge(S["gen"], n * GEN)
                    carry(a, n)
                a.activation(c_t[:, :, :, :].rearrange("p a b c -> p (a b c)"), ps[:, 2, 0:256],
                             ACT.Copy).then_inc(S["c_t_done"], 1)
                for half in range(2):
                    a.wait_ge(S["u_done"], 2 * n + half + 1)
                    carry(a, n)
                    a.activation(h[:, ds(n, 1), half * HALF:(half + 1) * HALF].rearrange("p a c -> p (a c)"),
                                 ps[:, half, :], ACT.Copy).then_inc(S["u_kept"], 1)
                a.wait_ge(S["kern_done"], n + 1)
                carry(a, n)
                if not first(n):
                    a.wait_ge(S["kern_turned"], n)
                    carry(a, n)
                for g2 in range(2):
                    ins = a.activation(
                        kern[:, :, :].rearrange("p d (r b c) -> p d r b c", b=2, c=GRP)[:, :, :, g2, :]
                        .rearrange("p d r c -> p (d r) c"),
                        ps[:, 2 + g2, 256:256 + 128].rearrange("p (a c) -> p a c", c=GRP), ACT.Copy)
                    ins.then_inc(S["kern_kept"], 1)
                for m in range(4):
                    a.wait_ge(S["bl_turned"], 4 * n + m + 1)
                    carry(a, m)
                    if m == 0 and not first(n):
                        a.wait_ge(S["in_done"], 4 * n)
                        carry(a, n)
                    a.activation(minm[:, m // 2, (m % 2) * 4:(m % 2) * 4 + 4, :].rearrange("p a c -> p (a c)"),
                                 ps[:, 4 + m, :], ACT.Copy).then_inc(S["min_kept"], 1)
                a.wait_ge(S["kern_turned"], n + 1)
                carry(a, n)
                if not first(n):
                    a.wait_ge(S["kern_out"], 16 * n)
                    carry(a, n)
                a.activation(kern_rows[:, 0:L, :].rearrange("p a c -> p (a c)"), ps[:, 3, P:2 * P],
                             ACT.Copy).then_inc(S["kern_rows_kept"], 1)
                a.activation(kern_rows[:, L:2 * L - 1, :].rearrange("p a c -> p (a c)"), ps[:, 3, GRP:P],
                             ACT.Copy).then_inc(S["kern_rows_kept"], 1)

            def keep_states(n):
                if not first(n):
                    a.wait_ge(S["out_done"], n)
                    carry(a, n)
                for m in range(4):
                    a.wait_ge(S["in_done"], 4 * n + m + 1)
                    carry(a, m)
                    o = state[:, 2 * m:2 * m + 2, :, 1:NC + 1]
                    if m >= 2:
                        o = state[:, 2 * m:2 * m + 2, :, NC:0:-1]
                    a.activation(o.rearrange("p a b c -> p (a b) c"),
                                 ps[:, 4 + m, :].rearrange("p (a c) -> p a c", c=NC), ACT.Copy
                                 ).then_inc(S["state_kept"], 1)

            def finish(n):
                a.wait_ge(S["out_done"], n + 1)
                carry(a, n)
                if not first(n):
                    a.wait_ge(S["y_out"], 16 * n)
                    carry(a, n)
                for g2 in range(2):
                    a.activation(y_grp[:, :, :].rearrange("p (r b) c -> p r b c", b=2)[:, :, g2, :],
                                 ps[:, g2, :].rearrange("p (r c) -> p r c", c=NC), ACT.Copy
                                 ).then_inc(S["y_kept"], 1)

            def gelu(n):
                a.wait_ge(S["y_sum"], n + 1)
                carry(a, n)
                row = h[:, ds(n, 1), :].rearrange("p a c -> p (a c)")
                a.activation(row, row, ACT.Gelu_apprx_tanh).then_inc(S["y_done"], 1)

            produce(0)
            keep_states(0)

            def tile_step(n):
                produce(n + 1)
                finish(n)
                keep_states(n + 1)
                gelu(n)

            for b in range(2):
                tile_step(b)
            with a.Fori(1, KT // 2 - 1) as i:
                for b in range(2):
                    tile_step(2 * i + b)
            tile_step(KT - 2)
            finish(KT - 1)
            gelu(KT - 1)

        @block.vector
        def _(v):
            v.memset(state[:, :, :, 0], 0.0).then_inc(S["pads"], 1)
            v.memset(state[:, :, :, NC + 1], 0.0).then_inc(S["pads"], 1)
            v.wait_ge(S["pads"], 2)
            x_re = state[:, :, 0, 1:NC + 1]
            x_im = state[:, :, 1, 1:NC + 1]
            x = state[:, :, :, 1:NC + 1]

            def scan(n):
                v.wait_ge(S["state_kept"], 4 * (n + 1))
                link = Steps(S["scan_chain"], n * SCAN)
                for lv, down in [(q, False) for q in range(LV)] + [(q, True) for q in range(LV - 2, -1, -1)]:
                    d = 1 << lv
                    m = NC // (2 * d) - (1 if down else 0)
                    to = slice(3 * d - 1, None, 2 * d) if down else slice(2 * d - 1, None, 2 * d)
                    of = slice((2 * d if down else d) - 1, (2 * d if down else d) - 1 + (m - 1) * 2 * d + 1, 2 * d)
                    re, im, neg = (bc(k.mu[:, lv, q, ds(n * DP, DP)], 2, [P, DP, m]) for q in range(3))
                    t1, t2 = sc1[:, :, :, 0:m], sc2[:, :, :, 0:m]
                    both = k.mu[:, lv, 0, ds(n * DP, DP)].unsqueeze(2).unsqueeze(3).broadcast_to([P, DP, 2, m])
                    v.tensor_tensor(t1, x[:, :, :, of], both, ALU.mult).then_inc(S["scan_chain"], 1)
                    link.step()
                    v.tensor_tensor(t2[:, :, 0], x_im[:, :, of], neg, ALU.mult).then_inc(S["scan_chain"], 1)
                    link.step()
                    v.tensor_tensor(t2[:, :, 1], x_re[:, :, of], im, ALU.mult).then_inc(S["scan_chain"], 1)
                    v.wait_ge(S["scan_chain"], link.step())
                    v.tensor_tensor(x[:, :, :, to], x[:, :, :, to], t1, ALU.add).then_inc(S["scan_chain"], 1)
                    v.wait_ge(S["scan_chain"], link.step())
                    v.tensor_tensor(x[:, :, :, to], x[:, :, :, to], t2, ALU.add).then_inc(S["scan_chain"], 1)
                    v.wait_ge(S["scan_chain"], link.step())
                assert link.n == SCAN

            def kern_diagonal(n):
                v.wait_ge(S["kern_rows_kept"], 2 * (n + 1))
                v.tensor_tensor(kern_rows[:, L - 1, :], kern_rows[:, L - 1, :], ps[:, 3, 0:GRP],
                                ALU.add).then_inc(S["kern_rows_done"], 1)

            def finish(n):
                v.wait_ge(S["y_ungrouped"], 16 * GJ * (n + 1))
                row = h[:, ds(n, 1), :].rearrange("p a c -> p (a c)")
                v.scalar_tensor_tensor(row, row, k.d_col[:, ds(n, 1)], y_pre[:, :], ALU.mult, ALU.add
                                       ).then_inc(S["y_sum"], 1)

            kern_diagonal(0)

            def tile_step(n):
                scan(n)
                kern_diagonal(n + 1)
                finish(n)

            for b in range(2):
                tile_step(b)
            with v.Fori(1, KT // 2 - 1) as i:
                for b in range(2):
                    tile_step(2 * i + b)
            tile_step(KT - 2)
            scan(KT - 1)
            finish(KT - 1)

        @block.gpsimd
        def _(g):
            k.clear_old(g)
            def produce(n, b):
                g.wait_ge(S["w_hi_done"], n + 1)
                carry(g, n)
                g.tensor_tensor(w_lo[:, :, :], w_raw[:, :, :], w_hi[:, :, :].bitcast(F32),
                                ALU.subtract).then_inc(S["w_lo_done"], 1)
                link = Steps(S["gen"], n * GEN)
                g.wait_ge(S["b_loaded"], 16 * 4 * (n + 1))
                carry(g, n)
                if not first(n):
                    g.wait_ge(S["kern_done"], n)
                    carry(g, n)
                cf = [bc(k.coef[:, ri, ds(n * DP, DP)], 2, [P, DP, GRP]) for ri in range(2)]
                complex_product(link, g, b_bar[:, 0, :, :], b_bar[:, 1, :, :], b_raw[:, 0, :, :], b_raw[:, 1, :, :],
                                cf[0], cf[1], gen_t[:, :, 0, :])
                g.wait_ge(S["c_t_done"], n + 1)
                carry(g, n)
                if not (isinstance(n, int) and n < 2):
                    g.wait_ge(S["out_done"], n - 1)
                    carry(g, n)
                full = [P, DP, L + 1, GRP]
                c_re_, c_im_ = (bc(c_t[:, ri, :, :], 2, full) for ri in range(2))
                pre, pim, pneg = (bc(k.pw[:, q, ds(n * DP, DP), :], 3, full) for q in range(3))
                o_re, o_im, tmp = cl[b][:, 0], cl[b][:, 1], gen_t[:, :, :, :]
                g.tensor_tensor(o_re, c_re_, pre, ALU.mult).then_inc(S["gen"], 1)
                g.wait_ge(S["gen"], link.step())
                carry(g, n)
                g.tensor_tensor(tmp, c_im_, pneg, ALU.mult).then_inc(S["gen"], 1)
                g.wait_ge(S["gen"], link.step())
                carry(g, n)
                g.tensor_tensor(o_re, o_re, tmp, ALU.add).then_inc(S["gen"], 1)
                g.wait_ge(S["gen"], link.step())
                carry(g, n)
                g.tensor_tensor(o_im, c_re_, pneg, ALU.mult).then_inc(S["gen"], 1)
                g.wait_ge(S["gen"], link.step())
                carry(g, n)
                g.tensor_tensor(tmp, c_im_, pre, ALU.mult).then_inc(S["gen"], 1)
                g.wait_ge(S["gen"], link.step())
                carry(g, n)
                g.tensor_tensor(o_im, o_im, tmp, ALU.subtract).then_inc(S["gen"], 1)
                g.wait_ge(S["gen"], link.step())
                carry(g, n)
                assert link.n == CL_STEPS
                if not first(n):
                    g.wait_ge(S["bl_turned"], 4 * n)
                    carry(g, n)
                for d in range(2):
                    half = [P, PR, L, GRP]
                    dps = slice(d * PR, (d + 1) * PR)
                    b0, b1 = (bc(b_bar[:, ri, dps, :], 2, half) for ri in range(2))
                    p0, p1 = (bc(k.pw_in[:, q, ds(n * DP + d * PR, PR), :], 3, half) for q in range(2))
                    complex_product(link, g, bl[:, 0, dps], bl[:, 1, dps], b0, b1, p0, p1, tmp[:, dps, 0:L, :])
                assert link.n == GEN

            produce(0, 0)
            for b in range(2):
                produce(b + 1, 1 - b)
            with g.Fori(1, KT // 2 - 1) as i:
                for b in range(2):
                    produce(2 * i + b + 1, 1 - b)
            produce(KT - 1, 1)


def s5_gate_block(k, w_glu):
    nc, ps, h = k.nc, k.ps, k.h
    k.open()
    w_raw = [k.sb(f"glu_w_raw{b}", [P, KT, P]) for b in range(2)]
    w_hi = [k.sb(f"glu_w_hi{b}", [P, KT, P], F32R) for b in range(2)]
    w_lo = [k.sb(f"glu_w_lo{b}", [P, KT, P], F32R) for b in range(2)]
    gate = [k.sb(f"glu_gate{b}", [P, HALF]) for b in range(2)]
    loaded = [k.sem(f"glu_w_loaded{b}") for b in range(2)]
    w_h = [k.sem(f"glu_w_hi_done{b}") for b in range(2)]
    w_l = [k.sem(f"glu_w_lo_done{b}") for b in range(2)]
    x_h, x_l, unit, gated, mixed = (k.sem("glu" + n) for n in ("_y_hi_done", "_y_lo_done", "_unit_done",
                                                                 "_gate_done", "_mixed"))
    w_v = w_glu.rearrange("(k p) n -> p k n", p=P)
    PAIRS = KT // 2

    def row(a, n, half):
        return a[:, ds(n, 1), half * HALF:(half + 1) * HALF].rearrange("p a c -> p (a c)")

    with nc.Block() as block:
        @block.sync
        def _(s):
            def load(i, b):
                s.dma_start(w_raw[b][:, :, :], w_v[:, :, ds((2 * i + b) * P, P)]).then_inc(loaded[b], 16)

            for b in range(2):
                load(0, b)
            with s.Fori(1, PAIRS) as i:
                for b in range(2):
                    s.wait_ge(w_l[b], i)
                    carry(s, i)
                    load(i, b)

        @block.scalar
        def _(a):
            def split(i, b):
                a.wait_ge(loaded[b], 16 * (i + 1))
                carry(a, i)
                if not (isinstance(i, int) and i == 0):
                    a.wait_ge(unit, 4 * i - 2 + 2 * b)
                    carry(a, i)
                split_hi(a, w_hi[b][:, :, :], w_raw[b][:, :, :]).then_inc(w_h[b], 1)

            def gates(i, b):
                for half in range(2):
                    a.wait_ge(unit, 4 * i + 2 * b + half + 1)
                    carry(a, i)
                    if not (isinstance(i, int) and i == 0 and b == 0):
                        a.wait_ge(mixed, 4 * i + 2 * b + half - 1)
                        carry(a, i)
                    a.activation(gate[half][:, :], ps[:, 2 * b + half, :], ACT.Sigmoid,
                                 bias=k.glu_col[:, ds(2 * i + b, 1)]).then_inc(gated, 1)

            split(0, 0)
            for kk in range(KT):
                split_hi(a, k.aT_hi[:, kk, :], h[:, kk, :]).then_inc(x_h, 1)
            split(0, 1)
            gates(0, 0)
            gates_next = lambda i: (split(i, 0), gates(i - 1, 1), split(i, 1), gates(i, 0))
            with a.Fori(1, PAIRS) as i:
                gates_next(i)
            gates(PAIRS - 1, 1)

        @block.vector
        def _(v):
            def mix(i):
                for b in range(2):
                    for half in range(2):
                        v.wait_ge(gated, 4 * i + 2 * b + half + 1)
                        o = row(h, 2 * i + b, half)
                        v.tensor_tensor(o, o, gate[half][:, :], ALU.mult).then_inc(mixed, 1)

            for kk in range(KT):
                v.wait_ge(x_h, kk + 1)
                v.tensor_tensor(k.aT_lo[:, kk, :], h[:, kk, :], k.aT_hi[:, kk, :].bitcast(F32),
                                ALU.subtract).then_inc(x_l, 1)
            v.wait_ge(x_l, KT)
            with v.Fori(0, PAIRS) as i:
                mix(i)

        @block.gpsimd
        def _(g):
            k.clear_old(g)
            with g.Fori(0, PAIRS) as i:
                for b in range(2):
                    g.wait_ge(w_h[b], i + 1)
                    carry(g, i)
                    g.tensor_tensor(w_lo[b][:, :, :], w_raw[b][:, :, :], w_hi[b][:, :, :].bitcast(F32),
                                    ALU.subtract).then_inc(w_l[b], 1)

        @block.tensor
        def _(t):
            def tile(i, b, start):
                t.wait_ge(w_l[b], i + 1)
                for half in range(2):
                    if not start:
                        t.wait_ge(gated, 4 * i + 2 * b + half - 3)
                    cols = slice(half * HALF, (half + 1) * HALF)
                    for kk in range(KT):
                        if start and b == 0 and half == 0:
                            t.wait_ge(x_l, kk + 1)
                        for m, (w, x) in enumerate(((w_hi, k.aT_hi), (w_hi, k.aT_lo), (w_lo, k.aT_hi))):
                            ins = t.matmul(ps[:, 2 * b + half, :], w[b][:, kk, :], x[:, kk, cols],
                                           start=(kk == 0 and m == 0), stop=(kk == KT - 1 and m == 2))
                    ins.then_inc(unit, 1)

            for b in range(2):
                tile(0, b, True)
            with t.Fori(1, PAIRS) as i:
                for b in range(2):
                    tile(i, b, False)
    k.close()


def hgrn_block(k, w_in, lower_bound, norm_g, masks):
    nc, ps, h = k.nc, k.ps, k.h
    k.open()
    sb = lambda n, shape, dt=F32: k.sb("hg_" + n, shape, dt)
    w_raw = [sb(f"w_raw{b}", [P, KT, P]) for b in range(2)]
    w_hi = [sb(f"w_hi{b}", [P, KT, P], F32R) for b in range(2)]
    w_lo = [sb(f"w_lo{b}", [P, KT, P], F32R) for b in range(2)]
    q_raw, v_raw, gs = sb("q_raw", [P, T]), sb("v_raw", [P, T]), sb("gs", [P, T])
    f_raw = [sb(f"f_raw{d}", [P, T]) for d in range(2)]
    k_raw = [sb(f"k_raw{d}", [P, T]) for d in range(2)]
    Q = [sb(f"q_decayed{d}", [P, T]) for d in range(2)]
    K = [sb(f"k_decayed{d}", [P, T]) for d in range(2)]
    tot = [sb(f"gate_totals{d}", [P, T]) for d in range(2)]
    k_sum = sb("k_sum", [P, T])
    v_tok, scores = sb("v_tok", [P, NHC, P]), sb("scores", [P, NHC, HC])
    S = [sb(f"state{d}", [P, NHC, P]) for d in range(2)]
    sig = [sb(f"sigmoid{b}", [P, HALF]) for b in range(2)]
    mask = sb("masks", [P, HLV, HC], I32)
    lb_in, lb, ng = sb("lb_in", [P, 2, HEADS]), sb("lb", [P, 2, HEADS]), sb("norm_g", [P, 1])
    d_lb = sb("lb_diff", [P, HEADS])
    ms, rs, rt = (sb("rms" + n, [P, NHC]) for n in "abc")
    sq = sb("square", [P, P])
    E = {n: k.sem("hg_" + n) for n in (
        "consts", "lb_chain", "lb_act", "w_loaded0", "w_loaded1", "w_hi_done0", "w_hi_done1", "w_lo_done0",
        "w_lo_done1", "unit_done", "q_sig", "q_kept", "f_sig", "f_kept", "f_ready", "v_kept", "g_sig", "g_kept",
        "k_started", "init", "chain", "v_turned", "v_tok_kept", "diag_done", "diag_kept", "level_done",
        "level_moved", "k_turned", "k_turned_kept", "kv_done", "states_kept", "o_done", "o_squared",
        "o_normed", "o_turned", "o_kept")}
    w_v = w_in.rearrange("(k p) (o n) -> p o k n", p=P, o=5)
    OUTS = 5
    BUF = [0, 1, 0, 1, 0]
    USES = [BUF.count(0), BUF.count(1)]
    CORE = 4 + 2 * (HLV - 1) + 2 * (NHC - 2) + 1 + RSQRT_STEPS

    def first(n):
        return isinstance(n, int) and n == 0

    def uses(m, o):
        return m * USES[BUF[o]] + BUF[:o + 1].count(BUF[o])

    def last_unit(m, o):
        before = [q for q in range(o) if BUF[q] == BUF[o]]
        if before:
            return m * 2 * OUTS + 2 * before[-1] + 2
        return (m - 1) * 2 * OUTS + 2 * max(q for q in range(OUTS) if BUF[q] == BUF[o]) + 2

    def chunks(a):
        return a[:, :].rearrange("p (c t) -> p c t", t=HC)

    def halves(a, lv, side):
        return a[:, :].rearrange("p (b e s) -> p b e s", e=2, s=1 << lv)[:, :, side, :]

    def total(d, lv):
        if lv == 0:
            return f_raw[d][:, :]
        at = T - (T >> (lv - 1))
        return tot[d][:, at:at + (T >> lv)]

    def pair(d, lv, side):
        return total(d, lv).rearrange("p (b e) -> p b e", e=2)[:, :, side]

    def bank_rows(b):
        return ps[:, b:b + 2, :].rearrange("p b (c t) -> p (b c) t", t=P)

    with nc.Block() as block:
        @block.sync
        def _(s):
            s.dma_start(mask[:, :, :], masks.rearrange("l s t -> s l t")).then_inc(E["consts"], 16)
            for r in range(2):
                s.dma_start(lb_in[:, r, :], lower_bound[r].rearrange("(n p) -> p n", p=P),
                            allow_slow_non_contiguous=True).then_inc(E["consts"], 16)
            s.dma_start(ng[:, :], norm_g.rearrange("(p a) -> p a", a=1)).then_inc(E["consts"], 16)

            def load(m, o, start=False):
                b = BUF[o]
                if not start:
                    s.wait_ge(E[f"w_lo_done{b}"], uses(m, o) - 1)
                    carry(s, m)
                s.dma_start(w_raw[b][:, :, :], w_v[:, o, :, ds(m * P, P)]).then_inc(E[f"w_loaded{b}"], 16)

            for o in range(OUTS):
                load(0, o, start=o < 2)
            with s.Fori(1, HEADS) as m:
                for o in range(OUTS):
                    load(m, o)

        @block.gpsimd
        def _(g):
            k.clear_old(g)
            def split(m, o):
                b = BUF[o]
                g.wait_ge(E[f"w_hi_done{b}"], uses(m, o))
                carry(g, m)
                g.tensor_tensor(w_lo[b][:, :, :], w_raw[b][:, :, :], w_hi[b][:, :, :].bitcast(F32),
                                ALU.subtract).then_inc(E[f"w_lo_done{b}"], 1)

            with g.Fori(0, HEADS) as m:
                for o in range(OUTS):
                    split(m, o)

        @block.tensor
        def _(t):
            def unit(m, o, half):
                b = BUF[o]
                if half == 0:
                    t.wait_ge(E[f"w_lo_done{b}"], uses(m, o))
                if o == 0 and not first(m):
                    t.wait_ge(E["g_kept"], 2 * m - 1 + half)
                if o == 1:
                    t.wait_ge(E["q_kept"], 2 * m + 1 + half)
                if o in (2, 3):
                    t.wait_ge(E["f_kept"], 4 * m + 2 * (o - 2) + 1 + half)
                if o == 4:
                    t.wait_ge(E["v_kept"], 2 * m + 1 + half)
                cols = slice(half * HALF, (half + 1) * HALF)
                for kk in range(KT):
                    for q, (w, x) in enumerate(((w_hi, k.aT_hi), (w_hi, k.aT_lo), (w_lo, k.aT_hi))):
                        ins = t.matmul(ps[:, half, :], w[b][:, kk, :], x[:, kk, cols],
                                       start=(kk == 0 and q == 0), stop=(kk == KT - 1 and q == 2))
                ins.then_inc(E["unit_done"], 1)

            def start_core(n):
                t.wait_ge(E["v_kept"], 2 * (n + 1))
                if not first(n):
                    t.wait_ge(E["o_kept"], 2 * n)
                for c in range(NHC):
                    ins = t.transpose(ps[:, 4 + c // 4, (c % 4) * P:(c % 4 + 1) * P],
                                      v_raw[:, c * HC:(c + 1) * HC], k.ident[:, :])
                ins.then_inc(E["v_turned"], 1)
                t.wait_ge(E["init"], n + 1)
                if not first(n):
                    t.wait_ge(E["states_kept"], 2 * n)
                for c in range(NHC):
                    cols = slice(c * HC, (c + 1) * HC)
                    ins = t.matmul(ps[:, 6 + c // 4, (c % 4) * P:(c % 4 + 1) * P], k_sum[:, cols], q_raw[:, cols],
                                   start=True, stop=True)
                ins.then_inc(E["diag_done"], 1)
                if not first(n):
                    t.wait_ge(E["o_normed"], n)

            def level(n, lv):
                for d in range(2):
                    if lv:
                        t.wait_ge(E["level_moved"], 2 * HLV * n + 2 * (lv - 1) + d + 1)
                    for c in range(NHC):
                        q = chunks(Q[d])[:, c, :].rearrange("p (b e s) -> p b e s", e=2, s=1 << lv)[:, :, 1 - d, :]
                        ins = t.matmul(ps[:, 2 + d, c * (HC // 2):(c + 1) * (HC // 2)], chunks(K[d])[:, c, :], q,
                                       start=True, stop=True)
                    ins.then_inc(E["level_done"], 1)

            def turn_k(n):
                t.wait_ge(E["level_moved"], 2 * HLV * (n + 1))
                t.wait_ge(E["v_tok_kept"], n + 1)
                t.wait_ge(E["diag_kept"], n + 1)
                for d in range(2):
                    for c in range(NHC):
                        ins = t.transpose(ps[:, 4 + 2 * d + c // 4, (c % 4) * P:(c % 4 + 1) * P],
                                          chunks(K[d])[:, c, :], k.ident[:, :])
                    ins.then_inc(E["k_turned"], 1)

            def chunk_sums(n):
                for d in range(2):
                    t.wait_ge(E["k_turned_kept"], 2 * n + d + 1)
                    for c in (range(1, NHC) if d else range(NHC - 1)):
                        ins = t.matmul(ps[:, 4 + 2 * d + c // 4, (c % 4) * P:(c % 4 + 1) * P],
                                       chunks(K[d])[:, c, :], v_tok[:, c, :], start=True, stop=True)
                    ins.then_inc(E["kv_done"], 1)

            def outputs(n):
                t.wait_ge(E["states_kept"], 2 * (n + 1))
                for c in range(NHC):
                    o = ps[:, 2 + c // 4, (c % 4) * P:(c % 4 + 1) * P]
                    t.matmul(o, scores[:, c, :], v_tok[:, c, :], start=True, stop=False)
                    if c > 0:
                        ins = t.matmul(o, chunks(Q[0])[:, c, :], S[0][:, c, :], start=False, stop=(c == NHC - 1))
                    if c < NHC - 1:
                        ins = t.matmul(o, chunks(Q[1])[:, c, :], S[1][:, c, :], start=False, stop=True)
                ins.then_inc(E["o_done"], 1)

            def turn_o(n):
                t.wait_ge(E["o_normed"], n + 1)
                for c in range(NHC):
                    ins = t.transpose(ps[:, 4 + c // 4, (c % 4) * P:(c % 4 + 1) * P], chunks(k_sum)[:, c, :],
                                      k.ident[:, :])
                    if c % 4 == 3:
                        ins.then_inc(E["o_turned"], 1)

            def core(n, more):
                start_core(n)
                level(n, 0)
                for lv in range(1, HLV):
                    if more:
                        for u in {1: (0, 1), 2: (2,), 3: (3,), 4: (4,), 5: (5,), 6: (6,)}[lv]:
                            unit(n + 1, u // 2, u % 2)
                    level(n, lv)
                if more:
                    unit(n + 1, 3, 1)
                turn_k(n)
                if more:
                    unit(n + 1, 4, 0)
                chunk_sums(n)
                outputs(n)
                if more:
                    unit(n + 1, 4, 1)
                turn_o(n)

            t.wait_ge(E["consts"], 16 * 4)
            for u in range(2 * OUTS):
                unit(0, u // 2, u % 2)
            core(0, True)
            with t.Fori(1, HEADS - 1) as n:
                core(n, True)
            core(HEADS - 1, False)

        @block.scalar
        def _(a):
            a.wait_ge(E["lb_chain"], 1)
            a.activation(lb[:, 0, :], d_lb[:, :], ACT.Sigmoid).then_inc(E["lb_act"], 1)
            a.activation(lb[:, 1, :], d_lb[:, :], ACT.Sigmoid, scale=-1.0).then_inc(E["lb_act"], 1)
            a.wait_ge(E["lb_act"], 2)

            def split(m, o):
                b = BUF[o]
                a.wait_ge(E[f"w_loaded{b}"], 16 * uses(m, o))
                carry(a, m)
                if not (first(m) and o < 2):
                    a.wait_ge(E["unit_done"], last_unit(m, o))
                    carry(a, m)
                split_hi(a, w_hi[b][:, :, :], w_raw[b][:, :, :]).then_inc(E[f"w_hi_done{b}"], 1)

            def sigmoid_of(m, o, half, done):
                a.wait_ge(E["unit_done"], 2 * OUTS * m + 2 * o + half + 1)
                carry(a, m)
                other, base = ("g_kept", 2 * m - 1 + half) if o == 0 else ("q_kept", 2 * m + 1 + half)
                if not (o == 0 and first(m)):
                    a.wait_ge(E[other], base)
                    carry(a, m)
                a.activation(sig[half][:, :], ps[:, half, :], ACT.Sigmoid).then_inc(E[done], 1)

            def gate(m, d):
                if not first(m):
                    a.wait_ge(E["level_moved"], 2 * HLV * (m - 1) + 2)
                    carry(a, m)
                for half in range(2):
                    cols = slice(half * HALF, (half + 1) * HALF)
                    a.wait_ge(E["unit_done"], 2 * OUTS * m + 2 * (1 + d) + half + 1)
                    carry(a, m)
                    a.activation(f_raw[d][:, cols], ps[:, half, :], ACT.Sigmoid).then_inc(E["f_sig"], 1)
                    a.activation(k_raw[d][:, cols], ps[:, half, :], ACT.Sigmoid, scale=-1.0
                                 ).then_inc(E["f_kept"], 1)
                a.wait_ge(E["f_sig"], 4 * m + 2 * d + 2)
                carry(a, m)
                a.activation(f_raw[d][:, :], f_raw[d][:, :], ACT.Identity, bias=lb[:, 0, ds(m, 1)],
                             scale=lb[:, 1, ds(m, 1)]).then_inc(E["f_ready"], 1)

            def keep_v(m):
                if not first(m):
                    a.wait_ge(E["v_turned"], m)
                    carry(a, m)
                for half in range(2):
                    a.wait_ge(E["unit_done"], 2 * OUTS * m + 6 + half + 1)
                    carry(a, m)
                    a.activation(v_raw[:, half * HALF:(half + 1) * HALF], ps[:, half, :], ACT.Copy
                                 ).then_inc(E["v_kept"], 1)

            def start_core(n):
                a.wait_ge(E["f_kept"], 4 * (n + 1))
                carry(a, n)
                if not first(n):
                    a.wait_ge(E["kv_done"], 2 * n)
                    carry(a, n)
                for d in range(2):
                    a.activation(K[d][:, :], k_raw[d][:, :], ACT.Copy, scale=lb[:, 1, ds(n, 1)]
                                 ).then_inc(E["k_started"], 1)
                a.wait_ge(E["v_turned"], n + 1)
                carry(a, n)
                if not first(n):
                    a.wait_ge(E["o_done"], n)
                    carry(a, n)
                a.activation(v_tok[:, :, :], bank_rows(4), ACT.Copy).then_inc(E["v_tok_kept"], 1)

            def keep_turned_k(n):
                for d in range(2):
                    a.wait_ge(E["k_turned"], 2 * n + d + 1)
                    carry(a, n)
                    a.activation(chunks(K[d]), bank_rows(4 + 2 * d), ACT.Copy).then_inc(E["k_turned_kept"], 1)

            def squares(n):
                a.wait_ge(E["o_done"], n + 1)
                carry(a, n)
                for c in range(NHC):
                    if c or not first(n):
                        a.wait_ge(E["o_squared"], NHC * n + c)
                        carry(a, n)
                    a.activation(sq[:, :], ps[:, 2 + c // 4, (c % 4) * P:(c % 4 + 1) * P], ACT.Square,
                                 accum_out=ms[:, c:c + 1]).then_inc(E["o_squared"], 1)

            def core(n, more):
                start_core(n)
                if more:
                    split(n + 1, 1)
                    for half in range(2):
                        sigmoid_of(n + 1, 0, half, "q_sig")
                    split(n + 1, 2)
                    gate(n + 1, 0)
                    split(n + 1, 3)
                    gate(n + 1, 1)
                    split(n + 1, 4)
                    keep_v(n + 1)
                keep_turned_k(n)
                if more:
                    sigmoid_of(n + 1, 4, 0, "g_sig")
                squares(n)
                if more:
                    sigmoid_of(n + 1, 4, 1, "g_sig")

            split(0, 0)
            split(0, 1)
            for half in range(2):
                sigmoid_of(0, 0, half, "q_sig")
            split(0, 2)
            gate(0, 0)
            split(0, 3)
            gate(0, 1)
            split(0, 4)
            keep_v(0)
            for half in range(2):
                sigmoid_of(0, 4, half, "g_sig")
            split(1, 0)
            core(0, True)
            split(2, 0)
            with a.Fori(1, HEADS - 2) as n:
                core(n, True)
                split(n + 2, 0)
            core(HEADS - 2, True)
            core(HEADS - 1, False)

        @block.vector
        def _(v):
            v.wait_ge(E["consts"], 16 * 4)
            v.tensor_tensor(d_lb[:, :], lb_in[:, 1, :], lb_in[:, 0, :], ALU.subtract).then_inc(E["lb_chain"], 1)

            def keep_q(m, half):
                if half == 0 and not first(m):
                    v.wait_ge(E["diag_done"], m)
                v.wait_ge(E["q_sig"], 2 * m + half + 1)
                cols = slice(half * HALF, (half + 1) * HALF)
                v.tensor_tensor(q_raw[:, cols], sig[half][:, :], ps[:, half, :], ALU.mult
                                ).then_inc(E["q_kept"], 1)

            def keep_g(m, half):
                if not first(m):
                    v.wait_ge(E["o_kept"], 2 * m)
                v.wait_ge(E["g_sig"], 2 * m + half + 1)
                cols = slice(half * HALF, (half + 1) * HALF)
                v.scalar_tensor_tensor(gs[:, cols], ps[:, half, :], ng[:, :], sig[half][:, :], ALU.mult, ALU.mult
                                       ).then_inc(E["g_kept"], 1)

            def core(n, more):
                link = Steps(E["chain"], n * CORE)
                v.wait_ge(E["f_ready"], 2 * (n + 1))
                for d in range(2):
                    v.tensor_tensor(Q[d][:, :], q_raw[:, :], f_raw[d][:, :], ALU.mult).then_inc(E["chain"], 1)
                    link.step()
                v.wait_ge(E["k_started"], 2 * (n + 1))
                v.tensor_tensor(tot[0][:, 0:T // 2], pair(0, 0, 0), pair(0, 0, 1), ALU.mult).then_inc(E["chain"], 1)
                link.step()
                v.tensor_tensor(tot[1][:, 0:T // 2], pair(1, 0, 0), pair(1, 0, 1), ALU.mult).then_inc(E["chain"], 1)
                link.step()
                v.tensor_tensor(k_sum[:, :], K[0][:, :], K[1][:, :], ALU.add).then_inc(E["init"], 1)
                for lv in range(2, HLV + 1):
                    v.wait_ge(E["chain"], link.count())
                    for d in range(2):
                        v.tensor_tensor(total(d, lv), pair(d, lv - 1, 0), pair(d, lv - 1, 1), ALU.mult).then_inc(E["chain"], 1)
                        link.step()
                v.wait_ge(E["diag_done"], n + 1)
                for b in range(2):
                    ins = v.tensor_tensor(scores[:, 4 * b:4 * b + 4, :],
                                          ps[:, 6 + b, :].rearrange("p (c t) -> p c t", t=HC),
                                          bc(k.ident[:, :], 1, [P, 4, HC]), ALU.mult)
                ins.then_inc(E["diag_kept"], 1)
                v.wait_ge(E["chain"], link.count())
                v.wait_ge(E["diag_kept"], n + 1)
                for lv in range(HLV):
                    s_ = 1 << lv
                    nb = HC // (2 * s_)
                    for d in range(2):
                        v.wait_ge(E["level_done"], 2 * HLV * n + 2 * lv + d + 1)
                        carry(v, n)
                        if not (first(n) and lv + d == 0):
                            v.wait_ge(E["level_moved"], 2 * HLV * n + 2 * lv + d)
                            carry(v, n)
                        to = scores[:, :, :].rearrange("p c (b e s) -> p c b e s", e=2, s=s_)[:, :, :, 1 - d, :]
                        mk = mask[:, lv, :].rearrange("p (b e s) -> p b e s", e=2, s=s_)[:, :, 1 - d, :]
                        of = ps[:, 2 + d, :].rearrange("p (c b s) -> p c b s", c=NHC, s=s_)
                        v.copy_predicated(to.rearrange("p c b s -> p (c b) s"),
                                          bc(mk, 1, [P, NHC, nb, s_]),
                                          of.rearrange("p c b s -> p (c b) s"))
                        qs, ks = halves(Q[d], lv, 1 - d), halves(K[d], lv, d)
                        full = [P, T // (2 * s_), s_]
                        v.tensor_tensor(qs, qs, bc(pair(d, lv, d), 2, full), ALU.mult)
                        v.tensor_tensor(ks, ks, bc(pair(d, lv, 1 - d), 2, full), ALU.mult
                                        ).then_inc(E["level_moved"], 1)
                    if more and lv in (1, 2):
                        keep_q(n + 1, lv - 1)
                for d in range(2):
                    v.wait_ge(E["kv_done"], 2 * n + d + 1)
                    kv, tt = bank_rows(4 + 2 * d), total(d, HLV)
                    order = list(range(NHC)) if d == 0 else list(range(NHC - 1, -1, -1))
                    for i in range(NHC - 1):
                        c, nxt = order[i], order[i + 1]
                        if i == 0:
                            ins = v.tensor_copy(S[d][:, nxt, :], kv[:, c, :])
                        else:
                            ins = v.scalar_tensor_tensor(S[d][:, nxt, :], S[d][:, c, :], tt[:, c:c + 1],
                                                         kv[:, c, :], ALU.mult, ALU.add)
                        if i == NHC - 2:
                            ins.then_inc(E["states_kept"], 1)
                        else:
                            ins.then_inc(E["chain"], 1)
                            v.wait_ge(E["chain"], link.step())
                v.wait_ge(E["o_squared"], NHC * (n + 1))
                v.tensor_scalar(ms[:, :], ms[:, :], 1.0 / P, RMS_EPS, ALU.mult, ALU.add).then_inc(E["chain"], 1)
                v.wait_ge(E["chain"], link.step())
                rsqrt_steps(link, v, rs[:, :], rt[:, :], ms[:, :])
                for b in range(2):
                    ins = v.tensor_tensor(chunks(k_sum)[:, 4 * b:4 * b + 4, :],
                                          ps[:, 2 + b, :].rearrange("p (c t) -> p c t", t=P),
                                          bc(rs[:, 4 * b:4 * b + 4], 2, [P, 4, P]), ALU.mult)
                ins.then_inc(E["o_normed"], 1)
                for b in range(2):
                    v.wait_ge(E["o_turned"], 2 * n + b + 1)
                    v.tensor_tensor(h[:, ds(n, 1), b * HALF:(b + 1) * HALF].rearrange("p a c -> p (a c)"),
                                    ps[:, 4 + b, :], gs[:, b * HALF:(b + 1) * HALF], ALU.mult
                                    ).then_inc(E["o_kept"], 1)
                if more:
                    for half in range(2):
                        keep_g(n + 1, half)
                assert link.n == CORE

            for half in range(2):
                keep_q(0, half)
            for half in range(2):
                keep_g(0, half)
            core(0, True)
            with v.Fori(1, HEADS - 1) as n:
                core(n, True)
            core(HEADS - 1, False)
    k.close()


_INS = ["x", "ln_mix_g", "ln_mix_b", "ln_ffn_g", "ln_ffn_b", "ffn_w_in", "ffn_w_out", "s5_w_in",
        "s5_lam_re", "s5_lam_im", "s5_log_step", "s5_b_re", "s5_b_im", "s5_c_re", "s5_c_im", "s5_d",
        "s5_w_glu", "s5_b_glu", "s5_w_out", "hg_w_in", "hg_lower_bound", "hg_norm_g", "hg_w_out"]


def level_masks():
    s = np.arange(HC)
    return np.stack([(s[:, None] >> (lv + 1) == s[None] >> (lv + 1)) & (s[:, None] >> lv != s[None] >> lv)
                     for lv in range(HLV)]).astype(np.int32)


def program(nc, dram, out):
    with ExitStack() as ctx:
        k = Core(nc, ctx)
        TICKS.clear()
        TICKS.update({e.engine: k.sem(f"tick{n}", keep=True) for n, e in enumerate((nc.scalar, nc.gpsimd, nc.sync))})
        TICKS[None] = k.sem("tick_others", keep=True)
        k.ps = ctx.enter_context(nc.psum_tensor("ps", [P, 8, HALF], F32))
        k.h = k.sb("h", [P, NT, D], keep=True)
        k.aT_hi = k.sb("aT_hi", [P, KT, T], F32R, keep=True)
        k.aT_lo = k.sb("aT_lo", [P, KT, T], F32R, keep=True)
        k.ident = k.sb("ident", [P, P], keep=True)
        k.d_col, k.glu_col = k.sb("d_col", [P, KT], keep=True), k.sb("glu_col", [P, KT], keep=True)
        x_rows = dram["x"].rearrange("a (p s) d -> (a p) s d", s=NT)
        out_rows = out.rearrange("a t d -> (a t) d")

        def dump():
            done = k.sem("dump")
            with nc.Block() as block:
                @block.sync
                def _(s):
                    s.dma_start(out_rows.rearrange("(p s) d -> p s d", s=NT), k.h[:, :, :]).then_inc(done, 16)
                    s.wait_ge(done, 16)

        k.open()
        k.pw = k.sb("s5_pw", [P, 3, KT * DP, L + 1])
        k.pw_in = k.sb("s5_pw_in", [P, 2, KT * DP, L])
        k.mu = k.sb("s5_mu", [P, LV, 3, KT * DP])
        k.coef = k.sb("s5_coef", [P, 2, KT * DP])
        outer, k.phase = k.phase, ExitStack()
        s5_tables_block(k, x_rows, dram["s5_lam_re"][0], dram["s5_lam_im"][0], dram["s5_log_step"][0],
                        dram["s5_b_glu"][0], dram["s5_d"][0], dram)
        k.close()
        k.phase = ExitStack()
        s5_scan_block(k, dram["s5_w_in"][0], dram["s5_b_re"][0], dram["s5_b_im"][0],
                      dram["s5_c_re"][0], dram["s5_c_im"][0])
        k.close()
        outer.close()
        s5_gate_block(k, dram["s5_w_glu"][0])
        out_projection_block(k, "s5o", dram["s5_w_out"][0], x_rows, ALPHA, False)
        layer_norm_block(k, "ln0", dram["ln_mix_g"][0], dram["ln_mix_b"][0])
        ffn_block(k, "ffn0", dram["ffn_w_in"][0], dram["ffn_w_out"][0])
        scratch = dram["scratch"]
        layer_norm_block(k, "ln1", dram["ln_ffn_g"][0], dram["ln_ffn_b"][0], natural=True, spill=scratch)
        hgrn_block(k, dram["hg_w_in"][0], dram["hg_lower_bound"], dram["hg_norm_g"][0], dram["masks"])
        out_projection_block(k, "hgo", dram["hg_w_out"][0], scratch, 1.0, True)
        layer_norm_block(k, "ln2", dram["ln_mix_g"][1], dram["ln_mix_b"][1])
        ffn_block(k, "ffn1", dram["ffn_w_in"][1], dram["ffn_w_out"][1])
        layer_norm_block(k, "ln3", dram["ln_ffn_g"][1], dram["ln_ffn_b"][1], out=out_rows)


def kernel(**inputs):
    import concourse.bacc as _bacc
    from concourse.bass_utils import run_bass_kernel_spmd as _run

    nc = _bacc.Bacc("TRN2", target_bir_lowering=False, num_devices=1)
    arrays, dram = {}, {}
    for name in _INS:
        a = np.ascontiguousarray(inputs[name])
        arrays[f"in_{name}_dram"] = a
        dram[name] = nc.dram_tensor(f"in_{name}_dram", a.shape, mybir.dt.from_np(a.dtype), kind="ExternalInput").ap()
    for name, a in (("ident", np.eye(P, dtype=np.float32)), ("masks", level_masks())):
        arrays[f"const_{name}_dram"] = a
        dram[name] = nc.dram_tensor(f"const_{name}_dram", a.shape, mybir.dt.from_np(a.dtype), kind="ExternalInput").ap()
    dram["scratch"] = nc.dram_tensor("residual_scratch", (P, NT, D), F32, kind="Internal").ap()
    out = nc.dram_tensor("out_0_dram", (1, T, D), F32, kind="ExternalOutput").ap()
    program(nc, dram, out)
    r = _run(nc, [arrays], core_ids=[0])
    return r.results[0]["out_0_dram"]
```

```python
from contextlib import ExitStack
import math

import numpy as np

import concourse.bass as bass
from concourse import mybir

F32 = mybir.dt.float32
F32R = mybir.dt.float32r
I32 = mybir.dt.int32
ALU = mybir.AluOpType
ACT = mybir.ActivationFunctionType
AX_X = mybir.AxisListType.X
ds = bass.ds

P = 128
D = 1024
T = 1024
KT = D // P
NT = T // P
HALF = 512
FFN = 2816
NF = FFN // P
FG = 2
NG = NF // FG
DEPTH = 2
ALPHA = float((2 * DEPTH) ** 0.25)
LN_EPS = 1e-5
RMS_EPS = 1e-6
GRP = 16
ST = 64
SG = D // GRP
L = 8
NC = T // L
GJ = P // GRP
PR = GJ // 2
DP = 2 * PR
LV = 7
HEADS = 8
HC = 128
NHC = T // HC
HLV = 7


def split_hi(eng, hi, src):
    return eng.activation(hi, src, ACT.Copy)


class Steps:

    def __init__(self, sem, base=0):
        self.sem, self.base, self.n = sem, base, 0

    def step(self):
        self.n += 1
        return self.base + self.n

    def count(self):
        return self.base + self.n


class Core:

    def __init__(self, nc, ctx):
        self.nc, self.ctx = nc, ctx
        self.phase = None
        self.fresh, self.old = [], []

    def open(self):
        self.phase = ExitStack()
        self.phase.__enter__()

    def close(self):
        self.phase.close()
        self.end_sems()

    def end_sems(self):
        for s in self.old:
            self.nc.release_semaphore(s)
        self.old, self.fresh = self.fresh, []

    def clear_old(self, g):
        for s in self.old:
            g.sem_clear(s)

    def sb(self, name, shape, dt=F32, keep=False):
        return (self.ctx if keep else self.phase).enter_context(self.nc.sbuf_tensor(name, shape, dt))

    def sem(self, name, keep=False):
        if keep:
            return self.ctx.enter_context(self.nc.semaphore(name))
        self.fresh.append(self.nc.alloc_semaphore(name=name))
        return self.fresh[-1]


def carry(eng, n):
    if not isinstance(n, int):
        eng.sem_inc(TICKS.get(eng.engine, TICKS[None]), 1)


TICKS = {}


def bc(ap, axis, shape):
    return ap.unsqueeze(axis).broadcast_to(shape)


def rsqrt_steps(link, v, y, t, x):
    v.tensor_scalar(y.bitcast(I32), x.bitcast(I32), -0.5, 1597463007.0, ALU.mult, ALU.add).then_inc(link.sem, 1)
    v.wait_ge(link.sem, link.step())
    for _ in range(4):
        v.tensor_tensor(t, y, y, ALU.mult).then_inc(link.sem, 1)
        v.wait_ge(link.sem, link.step())
        v.tensor_tensor(t, t, x, ALU.mult).then_inc(link.sem, 1)
        v.wait_ge(link.sem, link.step())
        v.tensor_scalar(t, t, -0.5, 1.5, ALU.mult, ALU.add).then_inc(link.sem, 1)
        v.wait_ge(link.sem, link.step())
        v.tensor_tensor(y, y, t, ALU.mult).then_inc(link.sem, 1)
        v.wait_ge(link.sem, link.step())


RSQRT_STEPS = 17


def transpose_and_split(k, tag, loaded):
    ps, h, ident = k.ps, k.h, k.ident
    NX = 4
    xt = [k.sb(f"{tag}_turned_raw{b}", [P, 4, P]) for b in range(NX)]
    turned, raw_done, hi_done, lo_done = (k.sem(tag + n) for n in ("_turned", "_raw_done", "_hi_done", "_lo_done"))

    def out_view(a, n):
        return a[:, (n % 2) * 4:(n % 2) * 4 + 4, (n // 2) * P:(n // 2 + 1) * P]

    def bank(n):
        return ps[:, 4 + n % 4, :].rearrange("p (d c) -> p d c", d=4)

    def pe(t, steps):
        for n in steps:
            tt, d4 = n // 2, n % 2
            loaded(t, tt)
            if n >= 4:
                t.wait_ge(hi_done, n - 3)
            for q in range(4):
                d = d4 * 4 + q
                ins = t.transpose(ps[:, 4 + n % 4, q * P:(q + 1) * P], h[:, tt, d * P:(d + 1) * P], ident[:, :])
            ins.then_inc(turned, 1)

    def act(a, steps):
        for n in steps:
            a.wait_ge(turned, n + 1)
            if n >= NX:
                a.wait_ge(lo_done, n - NX + 1)
            a.activation(xt[n % NX][:, :, :], bank(n), ACT.Copy).then_inc(raw_done, 1)
            split_hi(a, out_view(k.aT_hi, n), bank(n)).then_inc(hi_done, 1)

    def pool(g, steps):
        for n in steps:
            g.wait_ge(raw_done, n + 1)
            g.wait_ge(hi_done, n + 1)
            g.tensor_tensor(out_view(k.aT_lo, n), xt[n % NX][:, :, :], out_view(k.aT_hi, n).bitcast(F32),
                            ALU.subtract).then_inc(lo_done, 1)

    return pe, act, pool


def token_moments(link, v, k, mv, var, y, tmp):
    for tt in range(NT):
        v.bn_aggr(mv[:, tt, :], k.stats[:, tt, :, :].rearrange("p a b -> p (a b)")).then_inc(link.sem, 1)
        link.step()
    v.wait_ge(link.sem, link.count())
    v.tensor_scalar(var[:, :], mv[:, :, 1], LN_EPS, None, ALU.add).then_inc(link.sem, 1)
    v.wait_ge(link.sem, link.step())
    rsqrt_steps(link, v, y[:, :], tmp[:, :], var[:, :])


def layer_norm_block(k, tag, gamma, beta, first_weights, natural=False, spill=None):
    nc, ps, h = k.nc, k.ps, k.h
    k.open()
    g_col, b_col = k.sb(tag + "_g", [P, KT]), k.sb(tag + "_b", [P, KT])
    mv = k.sb(tag + "_mv", [P, NT, 2])
    var, y, tmp = (k.sb(tag + n, [P, NT]) for n in ("_var", "_y", "_tmp"))
    NX = 4
    xt = [k.sb(f"{tag}_xt{b}", [P, 4, P]) for b in range(NX)]
    w_loaded = [k.sem(f"{tag}_w_loaded{n}") for n in range(len(first_weights))]
    (loaded, w_hi_pool, w_hi_done, w_lo_done, chain, normed, turned, even_done, odd_done, hi_done, lo_done,
     stored) = (k.sem(f"{tag}_{n}") for n in (
         "loaded", "w_hi_pool", "w_hi_done", "w_lo_done", "chain", "normed", "turned", "even_done", "odd_done",
         "hi_done", "lo_done", "stored"))
    STEPS = [(hh, d) for hh in range(2) for d in range(KT)]

    def out_view(a, n):
        hh, d = STEPS[n]
        if natural:
            return a[:, d, :].rearrange("p (c s) -> p s c", s=NT)[:, 4 * hh:4 * hh + 4, :]
        return a[:, d, hh * HALF:(hh + 1) * HALF].rearrange("p (s c) -> p s c", s=4)

    with nc.Block() as block:
        @block.sync
        def _(s):
            for col, row in ((g_col, gamma), (b_col, beta)):
                s.dma_start(col[:, :], row.rearrange("(k p) -> p k", p=P), allow_slow_non_contiguous=True
                            ).then_inc(loaded, 16)
            for n, (raw, hi, lo, loads) in enumerate(first_weights):
                for to, of in loads:
                    s.dma_start(to, of).then_inc(w_loaded[n], 16)
            if spill is not None:
                for tt in range(NT):
                    s.wait_ge(normed, tt + 1)
                    s.dma_start(spill[:, tt, :], h[:, tt, :]).then_inc(stored, 16)
                s.wait_ge(stored, 16 * NT)

        @block.vector
        def _(v):
            token_moments(Steps(chain), v, k, mv, var, y, tmp)
            for tt in range(NT):
                v.tensor_scalar(h[:, tt, :], h[:, tt, :], mv[:, tt, 0:1], y[:, tt:tt + 1],
                                ALU.subtract, ALU.mult).then_inc(normed, 1)
            v.wait_ge(loaded, 32)
            for n in range(len(STEPS)):
                if n + 1 < len(STEPS) and (n + 1) % 2:
                    d = STEPS[n + 1][1]
                    v.wait_ge(turned, n + 2)
                    if n + 1 >= NX:
                        v.wait_ge(lo_done, n + 2 - NX)
                    v.tensor_scalar(xt[(n + 1) % NX][:, :, :].rearrange("p a c -> p (a c)"), ps[:, (n + 1) % 8, :],
                                    g_col[:, d:d + 1], b_col[:, d:d + 1], ALU.mult, ALU.add
                                    ).then_inc(odd_done, 1)
                v.wait_ge(hi_done, n + 1)
                v.tensor_tensor(out_view(k.aT_lo, n), xt[n % NX][:, :, :], out_view(k.aT_hi, n).bitcast(F32),
                                ALU.subtract).then_inc(lo_done, 1)

        @block.tensor
        def _(t):
            for n, (hh, d) in enumerate(STEPS):
                if d == 0:
                    t.wait_ge(normed, 4 * (hh + 1))
                if n >= 8:
                    t.wait_ge(odd_done if n % 2 else even_done, (n - 8) // 2 + 1)
                for q in range(4):
                    ins = t.transpose(ps[:, n % 8, q * P:(q + 1) * P], h[:, 4 * hh + q, d * P:(d + 1) * P],
                                      k.ident[:, :])
                ins.then_inc(turned, 1)

        @block.scalar
        def _(a):
            for n, (raw, hi, lo, loads) in enumerate(first_weights):
                if n < 2:
                    a.wait_ge(w_loaded[n], 16 * len(loads))
                    split_hi(a, hi, raw).then_inc(w_hi_done, 1)
            a.wait_ge(loaded, 32)
            for n in range(len(STEPS) + 1):
                if n < len(STEPS) and n % 2 == 0:
                    d = STEPS[n][1]
                    a.wait_ge(turned, n + 1)
                    if n >= NX:
                        a.wait_ge(lo_done, n - NX + 1)
                    a.activation(xt[n % NX][:, :, :].rearrange("p a c -> p (a c)"), ps[:, n % 8, :], ACT.Identity,
                                 bias=b_col[:, d:d + 1], scale=g_col[:, d:d + 1]).then_inc(even_done, 1)
                if n >= 1:
                    a.wait_ge(even_done if n % 2 else odd_done, (n - 1) // 2 + 1)
                    split_hi(a, out_view(k.aT_hi, n - 1), xt[(n - 1) % NX][:, :, :]).then_inc(hi_done, 1)

        @block.gpsimd
        def _(g):
            k.clear_old(g)
            for n, (raw, hi, lo, loads) in enumerate(first_weights):
                if n < 2:
                    g.wait_ge(w_hi_done, n + 1)
                else:
                    g.wait_ge(w_loaded[n], 16 * len(loads))
                    g.tensor_copy(hi, raw).then_inc(w_hi_pool, 1)
                    g.wait_ge(w_hi_pool, 1)
                g.tensor_tensor(lo, raw, hi.bitcast(F32), ALU.subtract).then_inc(w_lo_done, 1)
    k.close()


def final_norm_block(k, tag, gamma, beta, out):
    nc, h = k.nc, k.h
    k.open()
    g_row, b_row = k.sb(tag + "_g", [P, D]), k.sb(tag + "_b", [P, D])
    mv = k.sb(tag + "_mv", [P, NT, 2])
    var, y, tmp, offset = (k.sb(tag + n, [P, NT]) for n in ("_var", "_y", "_tmp", "_offset"))
    loaded, chain, factors, normed, scaled, scaled_g, done, done_g, stored = (k.sem(f"{tag}_{n}") for n in (
        "loaded", "chain", "factors", "normed", "scaled", "scaled_g", "done", "done_g", "stored"))
    BY_POOL = (2, 6)
    with nc.Block() as block:
        @block.sync
        def _(s):
            s.dma_start(g_row[:, :], gamma.partition_broadcast(P)).then_inc(loaded, 16)
            s.dma_start(b_row[:, :], beta.partition_broadcast(P)).then_inc(loaded, 16)
            rows = out.rearrange("(p s) d -> p s d", s=NT)
            by_dve = [tt for tt in range(NT) if tt not in BY_POOL]
            for n, tt in enumerate(by_dve):
                s.wait_ge(done, n + 1)
                s.dma_start(rows[:, tt, :], h[:, tt, :]).then_inc(stored, 16)
                if n == 3:
                    s.wait_ge(done_g, 1)
                    s.dma_start(rows[:, BY_POOL[0], :], h[:, BY_POOL[0], :]).then_inc(stored, 16)
            s.wait_ge(done_g, 2)
            s.dma_start(rows[:, BY_POOL[1], :], h[:, BY_POOL[1], :]).then_inc(stored, 16)
            s.wait_ge(stored, 16 * NT)

        @block.vector
        def _(v):
            token_moments(Steps(chain), v, k, mv, var, y, tmp)
            v.scalar_tensor_tensor(offset[:, :], mv[:, :, 0], -1.0, y[:, :], ALU.mult, ALU.mult).then_inc(factors, 1)
            v.wait_ge(loaded, 32)
            n = 0
            for tt in range(NT):
                if tt in BY_POOL:
                    continue
                v.wait_ge(normed, tt + 1)
                v.tensor_tensor(h[:, tt, :], h[:, tt, :], g_row[:, :], ALU.mult).then_inc(scaled, 1)
                n += 1
                v.wait_ge(scaled, n)
                v.tensor_tensor(h[:, tt, :], h[:, tt, :], b_row[:, :], ALU.add).then_inc(done, 1)

        @block.scalar
        def _(a):
            a.wait_ge(factors, 1)
            for tt in range(NT):
                a.activation(h[:, tt, :], h[:, tt, :], ACT.Identity, bias=offset[:, tt:tt + 1],
                             scale=y[:, tt:tt + 1]).then_inc(normed, 1)

        @block.gpsimd
        def _(g):
            k.clear_old(g)
            g.wait_ge(loaded, 32)
            for n, tt in enumerate(BY_POOL):
                g.wait_ge(normed, tt + 1)
                g.tensor_tensor(h[:, tt, :], h[:, tt, :], g_row[:, :], ALU.mult).then_inc(scaled_g, 1)
                g.wait_ge(scaled_g, n + 1)
                g.tensor_tensor(h[:, tt, :], h[:, tt, :], b_row[:, :], ALU.add).then_inc(done_g, 1)
    k.close()


def halves_stats(v, k, tt, dh):
    return v.bn_stats(k.stats[:, tt, dh, :], k.h[:, tt, dh * HALF:(dh + 1) * HALF])


def apply_affine(v, sem, count, h, tt, g_row, ab_row):
    v.scalar_tensor_tensor(h[:, tt, :], h[:, tt, :], ALPHA, g_row[:, :], ALU.mult, ALU.mult).then_inc(sem, 1)
    v.wait_ge(sem, count + 1)
    v.tensor_tensor(h[:, tt, :], h[:, tt, :], ab_row[:, :], ALU.add).then_inc(sem, 1)


def ffn_weights(k, tag, w_in, w_out):
    k.open()
    w1_raw = [k.sb(f"{tag}_w1_raw{b}", [P, 2, KT, P]) for b in range(2)]
    w1_hi = [k.sb(f"{tag}_w1_hi{b}", [P, 2, KT, P], F32R) for b in range(2)]
    w1_lo = [k.sb(f"{tag}_w1_lo{b}", [P, 2, KT, P], F32R) for b in range(2)]
    w2_raw = k.sb(tag + "_w2_raw", [P, FG, D])
    w2_hi = k.sb(tag + "_w2_hi", [P, FG, D], F32R)
    w2_lo = k.sb(tag + "_w2_lo", [P, FG, D], F32R)
    w_in_v = w_in.rearrange("(k p) (a n) -> p a k n", p=P, a=2)
    w_out_v = w_out.rearrange("(f p) d -> p f d", p=P)
    first = [(w1_raw[q][:, :, :, :], w1_hi[q][:, :, :, :], w1_lo[q][:, :, :, :],
              [(w1_raw[q][:, a, :, :], w_in_v[:, a, :, q * P:(q + 1) * P]) for a in range(2)]) for q in range(FG)]
    first.append((w2_raw[:, :, :], w2_hi[:, :, :], w2_lo[:, :, :], [(w2_raw[:, :, :], w_out_v[:, 0:FG, :])]))
    return (w1_raw, w1_hi, w1_lo, w2_raw, w2_hi, w2_lo, w_in_v, w_out_v), first


def ffn_block(k, tag, weights, gamma, beta):
    nc, ps, h = k.nc, k.ps, k.h
    w1_raw, w1_hi, w1_lo, w2_raw, w2_hi, w2_lo, w_in_v, w_out_v = weights
    g_row, ab_row = k.sb(tag + "_g", [P, D]), k.sb(tag + "_b", [P, D])
    hid_hi = k.sb(tag + "_hid_hi", [P, FG, T], F32R)
    hid_lo = k.sb(tag + "_hid_lo", [P, FG, T], F32R)
    act_out = [k.sb(f"{tag}_act_out{b}", [P, HALF]) for b in range(2)]
    s_w1 = [k.sem(f"{tag}_w1_loaded{b}") for b in range(2)]
    s_w1h = [k.sem(f"{tag}_w1_hi_done{b}") for b in range(2)]
    s_w1l = [k.sem(f"{tag}_w1_lo_done{b}") for b in range(2)]
    s_w2, s_w2h, s_w2l = (k.sem(tag + n) for n in ("_w2_loaded", "_w2_hi_done", "_w2_lo_done"))
    s_unit, s_silu, s_prod, s_hh, s_hl, s_tile, s_acc = (
        k.sem(tag + n) for n in ("_unit_done", "_silu_done", "_prod_done", "_hid_hi_done", "_hid_done",
                                 "_out_tile_done", "_acc_done"))
    rows_loaded, rows_ready, affine_done, stats_done = (
        k.sem(tag + n) for n in ("_rows_loaded", "_rows_ready", "_affine_done", "_stats_done"))
    U = 2 * FG
    NOUT = 2 * NT

    with nc.Block() as block:
        @block.sync
        def _(s):
            def load_w1(i, q):
                for a in range(2):
                    s.dma_start(w1_raw[q][:, a, :, :], w_in_v[:, a, :, ds((i * FG + q) * P, P)]).then_inc(s_w1[q], 16)

            def load_w2(i):
                s.dma_start(w2_raw[:, :, :], w_out_v[:, ds(i * FG, FG), :]).then_inc(s_w2, 16)

            s.dma_start(g_row[:, :], gamma.partition_broadcast(P)).then_inc(rows_loaded, 16)
            s.dma_start(ab_row[:, :], beta.partition_broadcast(P)).then_inc(rows_loaded, 16)
            for q in range(FG):
                load_w1(1, q)
            load_w2(1)
            with s.Fori(2, NG) as i:
                for q in range(FG):
                    s.wait_ge(s_w1l[q], i - 1)
                    carry(s, i)
                    load_w1(i, q)
                s.wait_ge(s_w2l, i - 1)
                carry(s, i)
                load_w2(i)

        @block.tensor
        def _(t):
            def unit(i, u):
                q, half, b = u // 2, u % 2, u % 2
                if half == 0 and not (isinstance(i, int) and i == 0):
                    t.wait_ge(s_w1l[q], i)
                if isinstance(i, int) and i == 0 and u < 2:
                    pass
                else:
                    t.wait_ge(s_prod, i * U + u - 1)
                for a in range(2):
                    for kk in range(KT):
                        rows = slice(half * HALF, (half + 1) * HALF)
                        for m, (w, x) in enumerate(((w1_hi, k.aT_hi), (w1_hi, k.aT_lo), (w1_lo, k.aT_hi))):
                            ins = t.matmul(ps[:, 2 * b + a, :], w[q][:, a, kk, :], x[:, kk, rows],
                                           start=(kk == 0 and m == 0), stop=(kk == KT - 1 and m == 2))
                ins.then_inc(s_unit, 1)

            def outputs(i):
                t.wait_ge(s_hl, (i + 1) * U)
                if not (isinstance(i, int) and i == 0):
                    t.wait_ge(s_w2l, i)
                for m in range(NOUT):
                    tt, dh = m // 2, m % 2
                    if not (isinstance(i, int) and i == 0 and m < 4):
                        t.wait_ge(s_acc, i * NOUT + m - 3)
                    for q in range(FG):
                        for n, (x, w) in enumerate(((hid_hi, w2_hi), (hid_hi, w2_lo), (hid_lo, w2_hi))):
                            ins = t.matmul(ps[:, 4 + m % 4, :], x[:, q, tt * P:(tt + 1) * P],
                                           w[:, q, dh * HALF:(dh + 1) * HALF],
                                           start=(q == 0 and n == 0), stop=(q == FG - 1 and n == 2))
                    ins.then_inc(s_tile, 1)

            def group(i):
                for u in range(1, U):
                    unit(i, u)
                unit(i + 1, 0)
                outputs(i)

            unit(0, 0)
            group(0)
            with t.Fori(1, NG - 1) as i:
                group(i)
            for u in range(1, U):
                unit(NG - 1, u)
            outputs(NG - 1)

        @block.scalar
        def _(a):
            def split_w1(i, q):
                a.wait_ge(s_w1[q], 32 * i)
                carry(a, i)
                a.wait_ge(s_unit, (i - 1) * U + 2 * q + 2)
                carry(a, i)
                split_hi(a, w1_hi[q][:, :, :, :], w1_raw[q][:, :, :, :]).then_inc(s_w1h[q], 1)

            def split_w2(i):
                a.wait_ge(s_w2, 16 * i)
                carry(a, i)
                a.wait_ge(s_tile, i * NOUT)
                carry(a, i)
                split_hi(a, w2_hi[:, :, :], w2_raw[:, :, :]).then_inc(s_w2h, 1)

            def silu(i, u):
                a.wait_ge(s_unit, i * U + u + 1)
                carry(a, i)
                if not (isinstance(i, int) and i == 0 and u < 2):
                    a.wait_ge(s_hl, i * U + u - 1)
                    carry(a, i)
                a.activation(act_out[u % 2][:, :], ps[:, 2 * (u % 2), :], ACT.Silu).then_inc(s_silu, 1)

            def group(i, more):
                silu(i, 1)
                if more:
                    split_w1(i + 1, 0)
                silu(i, 2)
                silu(i, 3)
                if more:
                    split_w1(i + 1, 1)
                    silu(i + 1, 0)
                    split_w2(i + 1)

            silu(0, 0)
            group(0, True)
            with a.Fori(1, NG - 1) as i:
                group(i, True)
            group(NG - 1, False)

        @block.vector
        def _(v):
            def split_w1(i, q):
                v.wait_ge(s_w1h[q], i)
                v.tensor_tensor(w1_lo[q][:, :, :, :], w1_raw[q][:, :, :, :],
                                w1_hi[q][:, :, :, :].bitcast(F32), ALU.subtract).then_inc(s_w1l[q], 1)

            def product(i, u):
                v.wait_ge(s_silu, i * U + u + 1)
                v.tensor_tensor(act_out[u % 2][:, :], act_out[u % 2][:, :], ps[:, 2 * (u % 2) + 1, :],
                                ALU.mult).then_inc(s_prod, 1)

            def affine(tts):
                for tt in tts:
                    apply_affine(v, affine_done, 2 * tt, h, tt, g_row, ab_row)

            def accumulate(i, last=False):
                if isinstance(i, int) and i == 0:
                    v.wait_ge(affine_done, 2 * NT)
                if not (isinstance(i, int) and i == 0):
                    v.wait_ge(s_acc, i * NOUT)
                for m in range(NOUT):
                    tt, dh = m // 2, m % 2
                    v.wait_ge(s_tile, i * NOUT + m + 1)
                    part = h[:, tt, dh * HALF:(dh + 1) * HALF]
                    v.tensor_tensor(part, part, ps[:, 4 + m % 4, :], ALU.add).then_inc(s_acc, 1)
                    if last and m:
                        v.wait_ge(s_acc, i * NOUT + m)
                        halves_stats(v, k, m // 2 if m % 2 else m // 2 - 1, 1 - m % 2).then_inc(stats_done, 1)
                if last:
                    v.wait_ge(s_acc, (i + 1) * NOUT)
                    halves_stats(v, k, NT - 1, 1).then_inc(stats_done, 1)

            def group(i, more, start=False):
                product(i, 1)
                if more:
                    split_w1(i + 1, 0)
                if start:
                    affine(range(3, 5))
                product(i, 2)
                if start:
                    affine(range(5, NT))
                product(i, 3)
                if more:
                    split_w1(i + 1, 1)
                    product(i + 1, 0)
                accumulate(i, last=not more)

            product(0, 0)
            v.wait_ge(rows_ready, 1)
            affine(range(3))
            group(0, True, start=True)
            with v.Fori(1, NG - 1) as i:
                group(i, True)
            group(NG - 1, False)

        @block.gpsimd
        def _(g):
            k.clear_old(g)
            def split_w2(i):
                g.wait_ge(s_w2h, i)
                carry(g, i)
                g.tensor_tensor(w2_lo[:, :, :], w2_raw[:, :, :], w2_hi[:, :, :].bitcast(F32),
                                ALU.subtract).then_inc(s_w2l, 1)

            def hidden(i, u):
                g.wait_ge(s_prod, i * U + u + 1)
                carry(g, i)
                q, half = u // 2, u % 2
                if not (isinstance(i, int) and i == 0) and u == 0:
                    g.wait_ge(s_tile, i * NOUT)
                    carry(g, i)
                cols = slice(half * HALF, (half + 1) * HALF)
                g.tensor_copy(hid_hi[:, q, cols], act_out[u % 2][:, :]).then_inc(s_hh, 1)
                g.wait_ge(s_hh, i * U + u + 1)
                carry(g, i)
                g.tensor_tensor(hid_lo[:, q, cols], act_out[u % 2][:, :], hid_hi[:, q, cols].bitcast(F32),
                                ALU.subtract).then_inc(s_hl, 1)

            def group(i, more):
                for u in range(1, U):
                    hidden(i, u)
                if more:
                    hidden(i + 1, 0)
                    split_w2(i + 1)

            g.wait_ge(rows_loaded, 32)
            g.tensor_scalar(ab_row[:, :], ab_row[:, :], ALPHA, None, ALU.mult).then_inc(rows_ready, 1)
            hidden(0, 0)
            group(0, True)
            with g.Fori(1, NG - 1) as i:
                group(i, True)
            group(NG - 1, False)
    k.close()


def out_projection_block(k, tag, w, residual, natural, gamma=None, beta=None):
    nc, ps, h, x_hi, x_lo = k.nc, k.ps, k.h, k.aT_hi, k.aT_lo
    k.open()
    w_raw = [k.sb(f"{tag}_w_raw{b}", [P, KT, HALF]) for b in range(2)]
    w_hi = [k.sb(f"{tag}_w_hi{b}", [P, KT, HALF], F32R) for b in range(2)]
    w_lo = [k.sb(f"{tag}_w_lo{b}", [P, KT, HALF], F32R) for b in range(2)]
    loaded = [k.sem(f"{tag}_w_loaded{b}") for b in range(2)]
    back = [k.sem(f"{tag}_h_back{b}") for b in range(2)]
    x_h, x_l, w_h, w_l, w_l1, scaled, tile, acc = (
        k.sem(tag + n) for n in ("_x_hi_done", "_x_lo_done", "_w_hi_done", "_w_lo_done", "_w_lo1_done",
                                 "_scaled", "_tile_done", "_acc_done"))
    rows_loaded, rows_ready, stats_done = (k.sem(tag + n) for n in ("_rows_loaded", "_rows_ready", "_stats_done"))
    if gamma is not None:
        g_row, ab_row = k.sb(tag + "_g", [P, D]), k.sb(tag + "_b", [P, D])
    w_v = w.rearrange("(k p) d -> p k d", p=P)

    def cut(a, kk, source):
        if source and natural:
            return a[:, kk, :].rearrange("p (c s) -> p s c", s=NT)
        return a[:, kk, :].rearrange("p (s c) -> p s c", s=NT)

    with nc.Block() as block:
        @block.sync
        def _(s):
            for b in range(2):
                s.dma_start(w_raw[b][:, :, :], w_v[:, :, b * HALF:(b + 1) * HALF]).then_inc(loaded[b], 16)
            if gamma is not None:
                s.dma_start(g_row[:, :], gamma.partition_broadcast(P)).then_inc(rows_loaded, 16)
                s.dma_start(ab_row[:, :], beta.partition_broadcast(P)).then_inc(rows_loaded, 16)
            s.wait_ge(x_l, KT)
            for b in range(2):
                tts = slice(4 * b, 4 * b + 4)
                s.dma_start(h[:, tts, :], residual[:, tts, :]).then_inc(back[b], 16)

        @block.scalar
        def _(a):
            X_AHEAD = 3
            for kk in range(X_AHEAD):
                split_hi(a, cut(x_hi, kk, False), cut(h, kk, True)).then_inc(x_h, 1)
            for b in range(2):
                a.wait_ge(loaded[b], 16)
                for kk in range(KT):
                    split_hi(a, w_hi[b][:, kk, :], w_raw[b][:, kk, :]).then_inc(w_h, 1)
                    if b == 0 and kk + X_AHEAD < KT:
                        split_hi(a, cut(x_hi, kk + X_AHEAD, False), cut(h, kk + X_AHEAD, True)).then_inc(x_h, 1)
            if gamma is None:
                for tt in range(NT):
                    if tt % 4 == 0:
                        a.wait_ge(back[tt // 4], 16)
                    a.activation(h[:, tt, :], h[:, tt, :], ACT.Copy, scale=ALPHA).then_inc(scaled, 1)
            else:
                a.wait_ge(rows_loaded, 32)
                a.activation(ab_row[:, :], ab_row[:, :], ACT.Copy, scale=ALPHA).then_inc(rows_ready, 1)

        @block.vector
        def _(v):
            for kk in range(KT):
                v.wait_ge(x_h, kk + 1)
                v.tensor_tensor(cut(x_lo, kk, False), cut(h, kk, True), cut(x_hi, kk, False).bitcast(F32),
                                ALU.subtract).then_inc(x_l, 1)
            if gamma is not None:
                v.wait_ge(rows_ready, 1)
            for m in range(2 * NT):
                dh, tt = m // NT, m % NT
                if gamma is not None and dh == 0:
                    if tt % 4 == 0:
                        v.wait_ge(back[tt // 4], 16)
                    apply_affine(v, scaled, 2 * tt, h, tt, g_row, ab_row)
                v.wait_ge(scaled, tt + 1 if gamma is None else 2 * tt + 2)
                v.wait_ge(tile, m + 1)
                part = h[:, tt, dh * HALF:(dh + 1) * HALF]
                v.tensor_tensor(part, part, ps[:, m % 8, :], ALU.add).then_inc(acc, 1)
                if m:
                    v.wait_ge(acc, m)
                    halves_stats(v, k, (m - 1) % NT, (m - 1) // NT).then_inc(stats_done, 1)
            v.wait_ge(acc, 2 * NT)
            halves_stats(v, k, NT - 1, 1).then_inc(stats_done, 1)

        @block.gpsimd
        def _(g):
            k.clear_old(g)
            for kk in range(KT):
                g.wait_ge(w_h, kk + 1)
                g.tensor_tensor(w_lo[0][:, kk, :], w_raw[0][:, kk, :], w_hi[0][:, kk, :].bitcast(F32),
                                ALU.subtract).then_inc(w_l, 1)
            for kk in range(KT):
                g.wait_ge(w_h, KT + kk + 1)
                g.tensor_tensor(w_lo[1][:, kk, :], w_raw[1][:, kk, :], w_hi[1][:, kk, :].bitcast(F32),
                                ALU.subtract).then_inc(w_l1, 1)

        @block.tensor
        def _(t):
            for m in range(2 * NT):
                dh, tt = m // NT, m % NT
                if m >= 8:
                    t.wait_ge(acc, m - 7)
                for kk in range(KT):
                    if m == 0:
                        t.wait_ge(x_l, kk + 1)
                    if tt == 0:
                        t.wait_ge(w_l1 if dh else w_l, kk + 1)
                    for n, (x, ww) in enumerate(((x_hi, w_hi), (x_hi, w_lo), (x_lo, w_hi))):
                        ins = t.matmul(ps[:, m % 8, :], x[:, kk, tt * P:(tt + 1) * P], ww[dh][:, kk, :],
                                       start=(kk == 0 and n == 0), stop=(kk == KT - 1 and n == 2))
                ins.then_inc(tile, 1)
    k.close()


def complex_product(link, e, out_re, out_im, a_re, a_im, b_re, b_im, t):
    for out, other, first, second, join in ((out_re, t, (a_re, b_re), (a_im, b_im), ALU.subtract),
                                            (out_im, t, (a_re, b_im), (a_im, b_re), ALU.add)):
        e.tensor_tensor(out, first[0], first[1], ALU.mult).then_inc(link.sem, 1)
        link.step()
        e.tensor_tensor(other, second[0], second[1], ALU.mult).then_inc(link.sem, 1)
        e.wait_ge(link.sem, link.step())
        carry(e, link.base)
        e.tensor_tensor(out, out, other, join).then_inc(link.sem, 1)
        e.wait_ge(link.sem, link.step())
        carry(e, link.base)


def s5_tables_block(k, x_rows, lam_re, lam_im, log_step, b_glu, d_skip, consts, c_re, c_im, c_rows):
    nc, ps, h = k.nc, k.ps, k.h
    N = KT * DP
    rows = {n: k.sb("s5_rows_" + n, [N, P]) for n in ("re", "im", "re_dt", "im_dt")}
    ls, th, em, step = (k.sb("s5_step" + n, [N, 2]) for n in "abcd")
    lam = {n: k.sb("s5_lam_" + n, [P, N]) for n in ("re", "im", "re_dt", "im_dt")}
    w = {n: k.sb("s5_w_" + n, [P, N]) for n in ("t", "q", "r", "half", "sin", "cos", "c1", "tanh", "em",
                                                  "e", "m_re", "den", "inv")}
    asc = k.sb("s5_asc", [P, 2, N, L + 1])
    tmp4 = k.sb("s5_tmp4", [P, N, 4])
    x_in = [k.sem(f"s5_x_loaded{b}") for b in range(2)]
    ident_in, cols_in, c_copied, p_in, chain, a_chain, p_turned = (k.sem("s5_" + n) for n in (
        "ident_loaded", "cols_loaded", "c_copied", "par_loaded", "tab_chain", "tab_act", "par_turned"))
    pe_t, act_t, pool_t = transpose_and_split(
        k, "s5_x", lambda t, tt: t.wait_ge(x_in[tt // 4], 16))
    lam_rows = {"re": lam_re, "im": lam_im}
    ROWS_READY = 8 + 2
    LAM_READY = ROWS_READY + 4 + 7

    with nc.Block() as block:
        @block.gpsimd
        def _(g):
            k.clear_old(g)
            pool_t(g, range(2 * NT))

        @block.sync
        def _(s):
            for n in ("re", "im"):
                s.dma_start(rows[n][:, :], lam_rows[n].rearrange("r (a b) p -> (r a) (b p)", b=2)).then_inc(p_in, 16)
            s.dma_start(ls[:, :], log_step.rearrange("r (a b) -> (r a) b", b=2)).then_inc(p_in, 16)
            s.dma_start(k.ident[:, :], consts["ident"]).then_inc(ident_in, 16)
            for b in range(2):
                tts = slice(4 * b, 4 * b + 4)
                s.dma_start(h[:, tts, :], x_rows[:, tts, :]).then_inc(x_in[b], 16)
            s.dma_start(k.d_col[:, :], d_skip.rearrange("(j p) -> p j", p=P),
                        allow_slow_non_contiguous=True).then_inc(cols_in, 16)
            s.dma_start(k.glu_col[:, :], b_glu.rearrange("(j p) -> p j", p=P),
                        allow_slow_non_contiguous=True).then_inc(cols_in, 16)
            for ri, c in enumerate((c_re, c_im)):
                for r in range(2):
                    for b in range(2):
                        s.dma_start(c_rows[ri, :, r, b * ST:(b + 1) * ST].rearrange("(a c) p -> a c p", c=GRP),
                                    c[r].rearrange("(a b) c p -> b a c p", b=2)[b]).then_inc(c_copied, 16)
            s.wait_ge(cols_in, 2 * 16)
            s.wait_ge(c_copied, 8 * 16)

        @block.tensor
        def _(t):
            t.wait_ge(ident_in, 16)
            pe_t(t, range(8))
            t.wait_ge(chain, ROWS_READY)
            for q, n in enumerate(("re", "im", "re_dt", "im_dt")):
                ins = t.transpose(ps[:, 0, q * N:(q + 1) * N], rows[n][:, :], k.ident[0:N, 0:N])
            ins.then_inc(p_turned, 1)
            pe_t(t, range(8, 2 * NT))

        @block.scalar
        def _(a):
            a.wait_ge(p_in, 3 * 16)
            a.activation(th[:, :], ls[:, :], ACT.Tanh, scale=1.0 / 32).then_inc(a_chain, 1)
            act_t(a, range(8))
            a.wait_ge(chain, LAM_READY)
            a.activation(w["half"][:, :], w["r"][:, :], ACT.Sin, scale=0.5).then_inc(a_chain, 1)
            a.activation(w["sin"][:, :], w["r"][:, :], ACT.Sin).then_inc(a_chain, 1)
            a.activation(w["tanh"][:, :], lam["re_dt"][:, :], ACT.Tanh, scale=0.5).then_inc(a_chain, 1)
            act_t(a, range(8, 2 * NT))

        @block.vector
        def _(v):
            v.wait_ge(p_in, 3 * 16)
            link = Steps(chain)
            v.wait_ge(a_chain, 1)
            v.tensor_scalar(em[:, :], th[:, :], -1.0, 1.0, ALU.mult, ALU.add).then_inc(chain, 1)
            v.wait_ge(chain, link.step())
            v.reciprocal(em[:, :], em[:, :]).then_inc(chain, 1)
            v.wait_ge(chain, link.step())
            v.tensor_scalar(step[:, :], th[:, :], 1.0, None, ALU.add).then_inc(chain, 1)
            v.wait_ge(chain, link.step())
            v.tensor_tensor(step[:, :], step[:, :], em[:, :], ALU.mult).then_inc(chain, 1)
            v.wait_ge(chain, link.step())
            for _ in range(4):
                v.tensor_tensor(step[:, :], step[:, :], step[:, :], ALU.mult).then_inc(chain, 1)
                v.wait_ge(chain, link.step())

            for n in ("re", "im"):
                v.tensor_tensor(rows[n + "_dt"][:, :].rearrange("r (b p) -> r b p", b=2),
                                rows[n][:, :].rearrange("r (b p) -> r b p", b=2),
                                bc(step[:, :], 2, [N, 2, ST]), ALU.mult).then_inc(chain, 1)
                v.wait_ge(chain, link.step())
            assert link.n == ROWS_READY
            v.wait_ge(p_turned, 1)
            for q, n in enumerate(("re", "im", "re_dt", "im_dt")):
                v.tensor_copy(lam[n][:, :].rearrange("p (j d r) -> p d j r", d=2, r=PR),
                              ps[:, 0, q * N:(q + 1) * N].rearrange("p (d j r) -> p d j r", d=2, r=PR)).then_inc(chain, 1)
                v.wait_ge(chain, link.step())
            round_by, c1, c2 = 1.5 * 2.0 ** 23, 6.28125, 2.0 ** -9 - 2.0 ** -14
            c2 = float(np.float32(round((2 * math.pi - c1) * 2 ** 20) / 2 ** 20))
            c3 = float(2 * math.pi - c1 - c2)
            q_, r_ = w["q"][:, :], w["r"][:, :]
            v.tensor_scalar(q_, lam["im_dt"][:, :], 1.0 / (2 * math.pi), round_by, ALU.mult, ALU.add).then_inc(chain, 1)
            v.wait_ge(chain, link.step())
            v.tensor_scalar(q_, q_, -round_by, None, ALU.add).then_inc(chain, 1)
            v.wait_ge(chain, link.step())
            v.scalar_tensor_tensor(r_, q_, -c1, lam["im_dt"][:, :], ALU.mult, ALU.add).then_inc(chain, 1)
            v.wait_ge(chain, link.step())
            v.scalar_tensor_tensor(r_, q_, -c2, r_, ALU.mult, ALU.add).then_inc(chain, 1)
            v.wait_ge(chain, link.step())
            v.scalar_tensor_tensor(r_, q_, -c3, r_, ALU.mult, ALU.add).then_inc(chain, 1)
            v.wait_ge(chain, link.step())
            v.tensor_scalar(r_, r_, 3.1415925, -3.1415925, ALU.min, ALU.max).then_inc(chain, 1)
            v.wait_ge(chain, link.step())
            v.tensor_tensor(w["den"][:, :], lam["re"][:, :], lam["re"][:, :], ALU.mult).then_inc(chain, 1)
            v.wait_ge(chain, link.step())
            assert link.n == LAM_READY
            v.wait_ge(a_chain, 4)
            W = {n: w[n][:, :] for n in w}
            v.tensor_tensor(W["c1"], W["half"], W["half"], ALU.mult).then_inc(chain, 1)
            v.wait_ge(chain, link.step())
            v.tensor_scalar(W["c1"], W["c1"], -2.0, None, ALU.mult).then_inc(chain, 1)
            v.wait_ge(chain, link.step())
            v.tensor_scalar(W["cos"], W["c1"], 1.0, None, ALU.add).then_inc(chain, 1)
            v.wait_ge(chain, link.step())
            v.tensor_scalar(W["t"], W["tanh"], -1.0, 1.0, ALU.mult, ALU.add).then_inc(chain, 1)
            v.wait_ge(chain, link.step())
            v.reciprocal(W["t"], W["t"]).then_inc(chain, 1)
            v.wait_ge(chain, link.step())
            v.scalar_tensor_tensor(W["em"], W["tanh"], 2.0, W["t"], ALU.mult, ALU.mult).then_inc(chain, 1)
            v.wait_ge(chain, link.step())
            v.tensor_scalar(W["e"], W["em"], 1.0, None, ALU.add).then_inc(chain, 1)
            v.wait_ge(chain, link.step())
            A = lambda ri, lo, hi: asc[:, ri, :, lo:hi]
            v.memset(asc[:, 0, :, 0], 1.0).then_inc(chain, 1)
            v.wait_ge(chain, link.step())
            v.memset(asc[:, 1, :, 0], 0.0).then_inc(chain, 1)
            v.wait_ge(chain, link.step())
            v.tensor_tensor(asc[:, 0, :, 1], W["e"], W["cos"], ALU.mult).then_inc(chain, 1)
            v.wait_ge(chain, link.step())
            v.tensor_tensor(asc[:, 1, :, 1], W["e"], W["sin"], ALU.mult).then_inc(chain, 1)
            v.wait_ge(chain, link.step())
            for lo, hi, by in ((1, 2, 1), (1, 3, 2), (1, 5, 4)):
                n = hi - lo
                z = [bc(asc[:, ri, :, by], 2, [P, N, n]) for ri in range(2)]
                complex_product(link, v, A(0, by + lo, by + hi), A(1, by + lo, by + hi),
                                A(0, lo, hi), A(1, lo, hi), z[0], z[1], tmp4[:, :, 0:n])
            byd = lambda a: a.rearrange("p (j d r) k -> p j d r k", d=2, r=PR)
            for ri in range(2):
                src = byd(asc[:, ri, :, :])
                v.tensor_copy(byd(k.pw[:, ri, :, :])[:, :, 0], src[:, :, 0]).then_inc(chain, 1)
                v.wait_ge(chain, link.step())
                v.tensor_copy(byd(k.pw[:, ri, :, :])[:, :, 1], src[:, :, 1, :, ::-1]).then_inc(chain, 1)
                v.wait_ge(chain, link.step())
                v.tensor_copy(byd(k.pw_in[:, ri, :, :])[:, :, 0], src[:, :, 0, :, L - 1::-1]).then_inc(chain, 1)
                v.wait_ge(chain, link.step())
                v.tensor_copy(byd(k.pw_in[:, ri, :, :])[:, :, 1], src[:, :, 1, :, 0:L]).then_inc(chain, 1)
                v.wait_ge(chain, link.step())
            v.tensor_scalar(k.pw[:, 1, :, :], k.pw[:, 1, :, :], -1.0, None, ALU.mult).then_inc(chain, 1)
            v.wait_ge(chain, link.step())
            for ri in range(2):
                v.tensor_copy(k.mu[:, 0, ri, :], asc[:, ri, :, L]).then_inc(chain, 1)
                v.wait_ge(chain, link.step())
            for lv in range(1, LV):
                a_, b_ = k.mu[:, lv - 1, 0, :], k.mu[:, lv - 1, 1, :]
                complex_product(link, v, k.mu[:, lv, 0, :], k.mu[:, lv, 1, :], a_, b_, a_, b_, W["t"])
            v.tensor_scalar(k.mu[:, :, 2, :], k.mu[:, :, 1, :], -1.0, None, ALU.mult).then_inc(chain, 1)
            v.wait_ge(chain, link.step())
            v.tensor_tensor(W["m_re"], W["em"], W["cos"], ALU.mult).then_inc(chain, 1)
            v.wait_ge(chain, link.step())
            v.tensor_tensor(W["m_re"], W["m_re"], W["c1"], ALU.add).then_inc(chain, 1)
            v.wait_ge(chain, link.step())
            m_im = asc[:, 1, :, 1]
            v.tensor_tensor(W["t"], lam["im"][:, :], lam["im"][:, :], ALU.mult).then_inc(chain, 1)
            v.wait_ge(chain, link.step())
            v.tensor_tensor(W["den"], W["den"], W["t"], ALU.add).then_inc(chain, 1)
            v.wait_ge(chain, link.step())
            v.reciprocal(W["inv"], W["den"]).then_inc(chain, 1)
            v.wait_ge(chain, link.step())
            l_re, l_im = lam["re"][:, :], lam["im"][:, :]
            v.tensor_tensor(W["t"], W["m_re"], l_re, ALU.mult).then_inc(chain, 1)
            v.wait_ge(chain, link.step())
            v.tensor_tensor(W["q"], m_im, l_im, ALU.mult).then_inc(chain, 1)
            v.wait_ge(chain, link.step())
            v.tensor_tensor(W["t"], W["t"], W["q"], ALU.add).then_inc(chain, 1)
            v.wait_ge(chain, link.step())
            v.tensor_tensor(k.coef[:, 0, :], W["t"], W["inv"], ALU.mult).then_inc(chain, 1)
            v.wait_ge(chain, link.step())
            v.tensor_tensor(W["t"], m_im, l_re, ALU.mult).then_inc(chain, 1)
            v.wait_ge(chain, link.step())
            v.tensor_tensor(W["q"], W["m_re"], l_im, ALU.mult).then_inc(chain, 1)
            v.wait_ge(chain, link.step())
            v.tensor_tensor(W["t"], W["t"], W["q"], ALU.subtract).then_inc(chain, 1)
            v.wait_ge(chain, link.step())
            v.tensor_tensor(k.coef[:, 1, :], W["t"], W["inv"], ALU.mult).then_inc(chain, 1)
            v.wait_ge(chain, link.step())


def s5_scan_block(k, w_in, b_re, b_im, c_rows):
    nc, ps, h = k.nc, k.ps, k.h
    w_raw = k.sb("s5_w_raw", [P, KT, P])
    w_hi, w_lo = k.sb("s5_w_hi", [P, KT, P], F32R), k.sb("s5_w_lo", [P, KT, P], F32R)
    b_raw = k.sb("s5_b_raw", [P, 2, DP, GRP])
    c_raw = k.sb("s5_c_raw", [PR * GRP, 2, 2, P])
    c_t = k.sb("s5_c_t", [P, 2, DP, GRP])
    b_bar = k.sb("s5_b_bar", [P, 2, DP, GRP])
    b_pair = k.sb("s5_b_pair", [P, 2, DP, 2, GRP])
    gen_t = k.sb("s5_gen_t", [P, DP, L + 1, GRP])
    cl = [k.sb(f"s5_cl{b}", [P, 2, DP, L + 1, GRP]) for b in range(2)]
    bl = k.sb("s5_bl", [P, 2, DP, L, GRP])
    minm = k.sb("s5_min", [P, 2, DP, P])
    kern = k.sb("s5_kern", [P, 2, P])
    kern_rows = k.sb("s5_kern_rows", [P, 2 * L - 1, GRP])
    toep = k.sb("s5_toep", [P, GJ, P])
    u_grp = [k.sb(f"s5_u_grp{b}", [P, GJ, NC]) for b in range(2)]
    state = k.sb("s5_state", [P, DP, 2, NC + 2])
    sc1, sc2 = (k.sb("s5_scan_t" + n, [P, DP, 2, NC // 2]) for n in "12")
    y_grp, y_pre = k.sb("s5_y_grp", [P, GJ, NC]), k.sb("s5_y_pre", [P, T])
    S = {n: k.sem("s5_" + n) for n in (
        "w_loaded", "b_loaded", "c_loaded", "w_hi_done", "w_lo_done", "c_turned", "c_t_done", "u_done",
        "u_kept", "gen", "b_placed", "kern_done", "kern_kept", "kern_turned", "u_out0", "u_out1", "kern_out", "y_out", "kern_rows_kept",
        "kern_rows_done", "bl_turned", "min_kept", "u_grouped", "toep_placed", "in_done", "state_kept",
        "scan_chain", "pads", "out_done", "y_kept", "y_ungrouped", "y_sum", "y_done")}
    u_scr, k_scr, y_scr = (nc.dram_tensor("s5_scratch_" + n, (P, c), F32, kind="Internal").ap()
                           for n, c in (("u", T), ("kern", (2 * L - 1) * GRP), ("y", GJ * NC)))
    w_v = w_in.rearrange("(k p) n -> p k n", p=P)
    b_v = [x.rearrange("r (a b) p c -> (b p) r a c", b=2) for x in (b_re, b_im)]
    GEN = 24
    BAR_STEPS, BL_STEPS = 6, 18
    SCAN = 5 * (2 * LV - 1)

    def first(n):
        return isinstance(n, int) and n == 0

    with nc.Block() as block:
        @block.sync
        def _(s):
            def load_w(n):
                if not first(n):
                    s.wait_ge(S["w_lo_done"], n)
                    carry(s, n)
                s.dma_start(w_raw[:, :, :], w_v[:, :, ds(n * P, P)]).then_inc(S["w_loaded"], 16)

            def load_parameters(n):
                if not first(n):
                    s.wait_ge(S["c_turned"], n)
                    carry(s, n)
                for ri in range(2):
                    s.dma_start(c_raw[:, ri, :, :], c_rows[ri, ds(n * PR * GRP, PR * GRP), :, :]
                                ).then_inc(S["c_loaded"], 16)
                if not first(n):
                    s.wait_ge(S["gen"], (n - 1) * GEN + BAR_STEPS)
                    carry(s, n)
                for ri in range(2):
                    for d in range(2):
                        s.dma_start(b_raw[:, ri, d * PR:(d + 1) * PR, :],
                                    b_v[ri][:, d, ds(n * PR, PR), :]).then_inc(S["b_loaded"], 16)

            def regroup_u(n, b):
                if not (isinstance(n, int) and n < 2):
                    s.wait_ge(S["out_done"], n - 1)
                    carry(s, n)
                if not first(n):
                    s.wait_ge(S["u_grouped"], 16 * L * n)
                    carry(s, n)
                for half in range(2):
                    s.wait_ge(S["u_kept"], 2 * n + half + 1)
                    carry(s, n)
                    s.dma_start(u_scr[:, half * HALF:(half + 1) * HALF],
                                h[:, ds(n, 1), half * HALF:(half + 1) * HALF].rearrange("p a c -> p (a c)")
                                ).then_inc(S[f"u_out{half}"], 16)
                v = u_scr.rearrange("(g h) (s c) -> s h g c", g=GJ, s=L)
                for r in range(L):
                    if r % (L // 2) == 0:
                        s.wait_ge(S[f"u_out{r // (L // 2)}"], 16 * (n + 1))
                        carry(s, n)
                    s.dma_start(u_grp[b][r * GRP:(r + 1) * GRP, :, :], v[r]).then_inc(S["u_grouped"], 16)

            def place_toeplitz(n):
                s.wait_ge(S["kern_rows_done"], n + 1)
                carry(s, n)
                if not first(n):
                    s.wait_ge(S["out_done"], n)
                    carry(s, n)
                    s.wait_ge(S["toep_placed"], 16 * L * n)
                    carry(s, n)
                s.dma_start(k_scr, kern_rows[:, :, :].rearrange("p a c -> p (a c)")).then_inc(S["kern_out"], 16)
                s.wait_ge(S["kern_out"], 16 * (n + 1))
                carry(s, n)
                v = k_scr.rearrange("(g h) e -> h g e", g=GJ)
                for r in range(L):
                    s.dma_start(toep[r * GRP:(r + 1) * GRP, :, :],
                                v[:, :, (L - 1 - r) * GRP:(2 * L - 1 - r) * GRP]).then_inc(S["toep_placed"], 16)

            def ungroup_y(n):
                s.wait_ge(S["y_kept"], 2 * (n + 1))
                carry(s, n)
                if not first(n):
                    s.wait_ge(S["y_sum"], n)
                    carry(s, n)
                    s.wait_ge(S["y_ungrouped"], 16 * GJ * n)
                    carry(s, n)
                s.dma_start(y_scr, y_grp[:, :, :].rearrange("p a c -> p (a c)")).then_inc(S["y_out"], 16)
                s.wait_ge(S["y_out"], 16 * (n + 1))
                carry(s, n)
                v = y_scr.rearrange("(t h) (g c) -> g h t c", t=L, g=GJ)
                for g in range(GJ):
                    s.dma_start(y_pre[g * GRP:(g + 1) * GRP, :].rearrange("h (t c) -> h t c", t=L), v[g]
                                ).then_inc(S["y_ungrouped"], 16)

            for n in range(2):
                load_w(n)
                load_parameters(n)
            regroup_u(0, 0)
            load_w(2)
            place_toeplitz(0)
            load_w(3)
            load_parameters(2)
            regroup_u(1, 1)

            def tile_step(n, b, tiles_left=4):
                place_toeplitz(n + 1)
                if tiles_left >= 4:
                    load_w(n + 4)
                if tiles_left >= 3:
                    load_parameters(n + 3)
                if tiles_left >= 2:
                    regroup_u(n + 2, b)
                ungroup_y(n)

            for b in range(2):
                tile_step(b, b)
            with s.Fori(1, KT // 2 - 2) as i:
                for b in range(2):
                    tile_step(2 * i + b, b)
            for n in range(KT - 4, KT - 1):
                tile_step(n, n % 2, KT - 1 - n)
            ungroup_y(KT - 1)

        @block.tensor
        def _(t):
            def turn_c(n):
                t.wait_ge(S["c_loaded"], 16 * 2 * (n + 1))
                carry(t, n)
                if not first(n):
                    t.wait_ge(S["c_t_done"], n)
                    carry(t, n)
                    t.wait_ge(S["kern_kept"], n)
                    carry(t, n)
                for ri in range(2):
                    for d in range(2):
                        m = ri * 2 + d
                        ins = t.transpose(ps[:, 2, m * 64:(m + 1) * 64], c_raw[:, ri, d, :],
                                          k.ident[0:PR * GRP, 0:PR * GRP])
                ins.then_inc(S["c_turned"], 1)

            def inputs(n):
                t.wait_ge(S["w_lo_done"], n + 1)
                if not first(n):
                    t.wait_ge(S["u_kept"], 2 * n)
                    if not (isinstance(n, int) and n < 3):
                        t.wait_ge(S["y_kept"], 2 * n - 4)
                for half in range(2):
                    cols = slice(half * HALF, (half + 1) * HALF)
                    for kk in range(KT):
                        for m, (w, x) in enumerate(((w_hi, k.aT_hi), (w_hi, k.aT_lo), (w_lo, k.aT_hi))):
                            ins = t.matmul(ps[:, half, :], w[:, kk, :], x[:, kk, cols],
                                           start=(kk == 0 and m == 0), stop=(kk == KT - 1 and m == 2))
                    ins.then_inc(S["u_done"], 1)

            def produce(n, b, more=True):
                t.wait_ge(S["gen"], n * GEN + BL_STEPS)
                if not first(n):
                    t.wait_ge(S["state_kept"], 4 * n)
                for m in range(4):
                    for q in range(4):
                        ri, dp = m // 2, (m % 2) * 4 + q
                        ins = t.transpose(ps[:, 4 + m, q * P:(q + 1) * P],
                                          bl[:, ri, dp, :, :].rearrange("p s c -> p (s c)"), k.ident[:, :])
                    ins.then_inc(S["bl_turned"], 1)
                if more:
                    inputs(n + 1)
                t.wait_ge(S["gen"], (n + 1) * GEN)
                t.wait_ge(S["b_placed"], 2 * (n + 1))
                for d in range(2):
                    for pr in range(PR):
                        dp = d * PR + pr
                        for ri in range(2):
                            ins = t.matmul(ps[:, 2, 256 + dp * 2 * GRP:256 + (dp + 1) * 2 * GRP],
                                           cl[b][:, ri, dp, d:d + L, :].rearrange("p a c -> p (a c)"),
                                           b_pair[:, ri, dp, :, :].rearrange("p a c -> p (a c)"),
                                           start=(ri == 0), stop=(ri == 1))
                ins.then_inc(S["kern_done"], 1)
                if more:
                    turn_c(n + 1)
                t.wait_ge(S["kern_kept"], n + 1)
                if not first(n):
                    t.wait_ge(S["kern_rows_done"], n)
                for d in range(2):
                    ins = t.transpose(ps[:, 3, d * P:(d + 1) * P], kern[:, d, :], k.ident[:, :])
                ins.then_inc(S["kern_turned"], 1)
                t.wait_ge(S["u_grouped"], 16 * GJ * (n + 1))
                t.wait_ge(S["min_kept"], 4 * (n + 1))
                for m in range(4):
                    for dp in (2 * m, 2 * m + 1):
                        for ri in range(2):
                            at = ((dp % 2) * 2 + ri) * P
                            for g2 in range(2):
                                rows = slice(g2 * ST, (g2 + 1) * ST)
                                ins = t.matmul(ps[rows, 4 + m, at:at + P], minm[:, ri, dp, rows],
                                               u_grp[b][:, 2 * (dp % PR) + g2, :], start=True, stop=True)
                    ins.then_inc(S["in_done"], 1)

            def outputs(n, b):
                t.wait_ge(S["toep_placed"], 16 * L * (n + 1))
                if not (isinstance(n, int) and n >= KT - 2):
                    t.wait_ge(S["u_kept"], 2 * n + 6)
                else:
                    t.wait_ge(S["y_kept"], 2 * n)
                for g in range(GJ):
                    g2, pr = g % 2, g // 2
                    t.matmul(ps[:, g2, pr * P:(pr + 1) * P], toep[:, g, :], u_grp[b][:, g, :],
                             start=(pr == 0), stop=False)
                t.wait_ge(S["scan_chain"], (n + 1) * SCAN)
                for g in range(GJ):
                    g2, pr = g % 2, g // 2
                    rows = slice(g2 * ST, (g2 + 1) * ST)
                    o = ps[:, g2, pr * P:(pr + 1) * P]
                    for ri in range(2):
                        t.matmul(o, cl[b][rows, ri, pr, 1:L + 1, :].rearrange("p a c -> p (a c)"),
                                 state[rows, pr, ri, 0:NC], start=False, stop=False)
                    for ri in range(2):
                        ins = t.matmul(o, cl[b][rows, ri, PR + pr, 0:L, :].rearrange("p a c -> p (a c)"),
                                       state[rows, PR + pr, ri, NC - 1::-1], start=False,
                                       stop=(ri == 1 and pr == PR - 1))
                ins.then_inc(S["out_done"], 1)

            turn_c(0)
            inputs(0)
            produce(0, 0)
            for b in range(2):
                produce(b + 1, 1 - b)
                outputs(b, b)
            with t.Fori(1, KT // 2 - 1) as i:
                for b in range(2):
                    produce(2 * i + b + 1, 1 - b)
                    outputs(2 * i + b, b)
            produce(KT - 1, 1, more=False)
            outputs(KT - 2, 0)
            outputs(KT - 1, 1)

        @block.scalar
        def _(a):
            def split_w(n):
                a.wait_ge(S["w_loaded"], 16 * (n + 1))
                carry(a, n)
                if not first(n):
                    a.wait_ge(S["u_done"], 2 * n)
                    carry(a, n)
                split_hi(a, w_hi[:, :, :], w_raw[:, :, :]).then_inc(S["w_hi_done"], 1)

            def keep_u(n):
                for half in range(2):
                    a.wait_ge(S["u_done"], 2 * n + half + 1)
                    carry(a, n)
                    a.activation(h[:, ds(n, 1), half * HALF:(half + 1) * HALF].rearrange("p a c -> p (a c)"),
                                 ps[:, half, :], ACT.Copy).then_inc(S["u_kept"], 1)

            def keep_c(n):
                a.wait_ge(S["c_turned"], n + 1)
                carry(a, n)
                if not first(n):
                    a.wait_ge(S["gen"], n * GEN)
                    carry(a, n)
                a.activation(c_t[:, :, :, :].rearrange("p a b c -> p (a b c)"), ps[:, 2, 0:256],
                             ACT.Copy).then_inc(S["c_t_done"], 1)

            def produce(n, more=True):
                a.wait_ge(S["gen"], n * GEN + BAR_STEPS)
                carry(a, n)
                if not first(n):
                    a.wait_ge(S["kern_done"], n)
                    carry(a, n)
                for g2 in range(2):
                    rows = slice(g2 * ST, (g2 + 1) * ST)
                    a.activation(b_pair[rows, :, :, g2, :].rearrange("p a b c -> p (a b) c"),
                                 b_bar[rows, :, :, :].rearrange("p a b c -> p (a b) c"), ACT.Copy
                                 ).then_inc(S["b_placed"], 1)
                for m in range(4):
                    a.wait_ge(S["bl_turned"], 4 * n + m + 1)
                    carry(a, n)
                    if m == 0 and not first(n):
                        a.wait_ge(S["in_done"], 4 * n)
                        carry(a, n)
                    a.activation(minm[:, m // 2, (m % 2) * 4:(m % 2) * 4 + 4, :].rearrange("p a c -> p (a c)"),
                                 ps[:, 4 + m, :], ACT.Copy).then_inc(S["min_kept"], 1)
                if more:
                    keep_u(n + 1)
                if more and not (isinstance(n, int) and n == KT - 2):
                    split_w(n + 2)
                a.wait_ge(S["kern_done"], n + 1)
                carry(a, n)
                if not first(n):
                    a.wait_ge(S["kern_turned"], n)
                    carry(a, n)
                a.activation(kern[:, :, :].rearrange("p d c -> p (d c)"), ps[:, 2, 256:512], ACT.Copy
                             ).then_inc(S["kern_kept"], 1)
                if more:
                    keep_c(n + 1)
                a.wait_ge(S["kern_turned"], n + 1)
                carry(a, n)
                if not first(n):
                    a.wait_ge(S["kern_out"], 16 * n)
                    carry(a, n)
                a.activation(kern_rows[:, 0:L, :].rearrange("p a c -> p (a c)"), ps[:, 3, P:2 * P],
                             ACT.Copy).then_inc(S["kern_rows_kept"], 1)
                a.activation(kern_rows[:, L:2 * L - 1, :].rearrange("p a c -> p (a c)"), ps[:, 3, GRP:P],
                             ACT.Copy).then_inc(S["kern_rows_kept"], 1)

            def keep_states(n):
                if not first(n):
                    a.wait_ge(S["out_done"], n)
                    carry(a, n)
                for m in range(4):
                    a.wait_ge(S["in_done"], 4 * n + m + 1)
                    carry(a, n)
                    o = state[:, 2 * m:2 * m + 2, :, 1:NC + 1]
                    if m >= 2:
                        o = state[:, 2 * m:2 * m + 2, :, NC:0:-1]
                    a.activation(o.rearrange("p a b c -> p (a b) c"),
                                 ps[:, 4 + m, :].rearrange("p (a c) -> p a c", c=NC), ACT.Copy
                                 ).then_inc(S["state_kept"], 1)

            def finish(n):
                a.wait_ge(S["out_done"], n + 1)
                carry(a, n)
                if not first(n):
                    a.wait_ge(S["y_out"], 16 * n)
                    carry(a, n)
                for g2 in range(2):
                    a.activation(y_grp[:, :, :].rearrange("p (r b) c -> p r b c", b=2)[:, :, g2, :],
                                 ps[:, g2, :].rearrange("p (r c) -> p r c", c=NC), ACT.Copy
                                 ).then_inc(S["y_kept"], 1)

            def gelu(n):
                a.wait_ge(S["y_sum"], n + 1)
                carry(a, n)
                row = h[:, ds(n, 1), :].rearrange("p a c -> p (a c)")
                a.activation(row, row, ACT.Gelu_apprx_tanh).then_inc(S["y_done"], 1)

            a.wait_ge(S["pads"], 3)
            split_w(0)
            keep_c(0)
            keep_u(0)
            split_w(1)
            produce(0)
            keep_states(0)

            def tile_step(n, more=True):
                produce(n + 1, more)
                keep_states(n + 1)
                finish(n)
                if not first(n):
                    gelu(n - 1)

            for n in range(2):
                tile_step(n)
            with a.Fori(2, KT - 3) as n:
                tile_step(n)
            tile_step(KT - 3)
            tile_step(KT - 2, more=False)
            finish(KT - 1)
            gelu(KT - 2)
            gelu(KT - 1)

        @block.vector
        def _(v):
            v.memset(state[:, :, :, 0], 0.0).then_inc(S["pads"], 1)
            v.memset(state[:, :, :, NC + 1], 0.0).then_inc(S["pads"], 1)
            v.memset(b_pair[:, :, :, :, :], 0.0).then_inc(S["pads"], 1)
            v.wait_ge(S["pads"], 3)
            x_re = state[:, :, 0, 1:NC + 1]
            x_im = state[:, :, 1, 1:NC + 1]
            x = state[:, :, :, 1:NC + 1]

            def scan(n):
                v.wait_ge(S["state_kept"], 4 * (n + 1))
                link = Steps(S["scan_chain"], n * SCAN)
                for lv, down in [(q, False) for q in range(LV)] + [(q, True) for q in range(LV - 2, -1, -1)]:
                    d = 1 << lv
                    m = NC // (2 * d) - (1 if down else 0)
                    to = slice(3 * d - 1, None, 2 * d) if down else slice(2 * d - 1, None, 2 * d)
                    of = slice((2 * d if down else d) - 1, (2 * d if down else d) - 1 + (m - 1) * 2 * d + 1, 2 * d)
                    re, im, neg = (bc(k.mu[:, lv, q, ds(n * DP, DP)], 2, [P, DP, m]) for q in range(3))
                    t1, t2 = sc1[:, :, :, 0:m], sc2[:, :, :, 0:m]
                    both = k.mu[:, lv, 0, ds(n * DP, DP)].unsqueeze(2).unsqueeze(3).broadcast_to([P, DP, 2, m])
                    v.tensor_tensor(t1, x[:, :, :, of], both, ALU.mult).then_inc(S["scan_chain"], 1)
                    link.step()
                    v.tensor_tensor(t2[:, :, 0], x_im[:, :, of], neg, ALU.mult).then_inc(S["scan_chain"], 1)
                    link.step()
                    v.tensor_tensor(t2[:, :, 1], x_re[:, :, of], im, ALU.mult).then_inc(S["scan_chain"], 1)
                    v.wait_ge(S["scan_chain"], link.step())
                    v.tensor_tensor(x[:, :, :, to], x[:, :, :, to], t1, ALU.add).then_inc(S["scan_chain"], 1)
                    v.wait_ge(S["scan_chain"], link.step())
                    v.tensor_tensor(x[:, :, :, to], x[:, :, :, to], t2, ALU.add).then_inc(S["scan_chain"], 1)
                    v.wait_ge(S["scan_chain"], link.step())
                assert link.n == SCAN

            def kern_diagonal(n):
                v.wait_ge(S["kern_rows_kept"], 2 * (n + 1))
                v.tensor_tensor(kern_rows[:, L - 1, :], kern_rows[:, L - 1, :], ps[:, 3, 0:GRP],
                                ALU.add).then_inc(S["kern_rows_done"], 1)

            def finish(n):
                v.wait_ge(S["y_ungrouped"], 16 * GJ * (n + 1))
                row = h[:, ds(n, 1), :].rearrange("p a c -> p (a c)")
                v.scalar_tensor_tensor(row, row, k.d_col[:, ds(n, 1)], y_pre[:, :], ALU.mult, ALU.add
                                       ).then_inc(S["y_sum"], 1)

            kern_diagonal(0)

            def tile_step(n):
                scan(n)
                kern_diagonal(n + 1)
                if not first(n):
                    finish(n - 1)

            for b in range(2):
                tile_step(b)
            with v.Fori(1, KT // 2 - 1) as i:
                for b in range(2):
                    tile_step(2 * i + b)
            tile_step(KT - 2)
            scan(KT - 1)
            finish(KT - 2)
            finish(KT - 1)

        @block.gpsimd
        def _(g):
            k.clear_old(g)
            def split_w(n):
                g.wait_ge(S["w_hi_done"], n + 1)
                carry(g, n)
                g.tensor_tensor(w_lo[:, :, :], w_raw[:, :, :], w_hi[:, :, :].bitcast(F32),
                                ALU.subtract).then_inc(S["w_lo_done"], 1)

            def produce(n, b):
                link = Steps(S["gen"], n * GEN)
                g.wait_ge(S["b_loaded"], 16 * 4 * (n + 1))
                carry(g, n)
                if not first(n):
                    g.wait_ge(S["b_placed"], 2 * n)
                    carry(g, n)
                cf = [bc(k.coef[:, ri, ds(n * DP, DP)], 2, [P, DP, GRP]) for ri in range(2)]
                complex_product(link, g, b_bar[:, 0, :, :], b_bar[:, 1, :, :], b_raw[:, 0, :, :], b_raw[:, 1, :, :],
                                cf[0], cf[1], gen_t[:, :, 0, :])
                tmp = gen_t[:, :, :, :]
                if not first(n):
                    g.wait_ge(S["bl_turned"], 4 * n)
                    carry(g, n)
                for d in range(2):
                    half = [P, PR, L, GRP]
                    dps = slice(d * PR, (d + 1) * PR)
                    b0, b1 = (bc(b_bar[:, ri, dps, :], 2, half) for ri in range(2))
                    p0, p1 = (bc(k.pw_in[:, q, ds(n * DP + d * PR, PR), :], 3, half) for q in range(2))
                    complex_product(link, g, bl[:, 0, dps], bl[:, 1, dps], b0, b1, p0, p1, tmp[:, dps, 0:L, :])
                assert link.n == BL_STEPS
                if not (isinstance(n, int) and n == KT - 1):
                    split_w(n + 1)
                g.wait_ge(S["c_t_done"], n + 1)
                carry(g, n)
                if not (isinstance(n, int) and n < 2):
                    g.wait_ge(S["out_done"], n - 1)
                    carry(g, n)
                full = [P, DP, L + 1, GRP]
                c_re_, c_im_ = (bc(c_t[:, ri, :, :], 2, full) for ri in range(2))
                pre, pneg = (bc(k.pw[:, q, ds(n * DP, DP), :], 3, full) for q in range(2))
                o_re, o_im = cl[b][:, 0], cl[b][:, 1]
                g.tensor_tensor(o_re, c_re_, pre, ALU.mult).then_inc(S["gen"], 1)
                g.wait_ge(S["gen"], link.step())
                carry(g, n)
                g.tensor_tensor(tmp, c_im_, pneg, ALU.mult).then_inc(S["gen"], 1)
                g.wait_ge(S["gen"], link.step())
                carry(g, n)
                g.tensor_tensor(o_re, o_re, tmp, ALU.add).then_inc(S["gen"], 1)
                g.wait_ge(S["gen"], link.step())
                carry(g, n)
                g.tensor_tensor(o_im, c_re_, pneg, ALU.mult).then_inc(S["gen"], 1)
                g.wait_ge(S["gen"], link.step())
                carry(g, n)
                g.tensor_tensor(tmp, c_im_, pre, ALU.mult).then_inc(S["gen"], 1)
                g.wait_ge(S["gen"], link.step())
                carry(g, n)
                g.tensor_tensor(o_im, o_im, tmp, ALU.subtract).then_inc(S["gen"], 1)
                g.wait_ge(S["gen"], link.step())
                carry(g, n)
                assert link.n == GEN

            split_w(0)
            produce(0, 0)
            for b in range(2):
                produce(b + 1, 1 - b)
            with g.Fori(1, KT // 2 - 1) as i:
                for b in range(2):
                    produce(2 * i + b + 1, 1 - b)
            produce(KT - 1, 1)


def s5_gate_block(k, w_glu):
    nc, ps, h = k.nc, k.ps, k.h
    k.open()
    w_raw = [k.sb(f"glu_w_raw{b}", [P, KT, P]) for b in range(2)]
    w_hi = [k.sb(f"glu_w_hi{b}", [P, KT, P], F32R) for b in range(2)]
    w_lo = [k.sb(f"glu_w_lo{b}", [P, KT, P], F32R) for b in range(2)]
    gate = [k.sb(f"glu_gate{b}", [P, HALF]) for b in range(2)]
    loaded = [k.sem(f"glu_w_loaded{b}") for b in range(2)]
    w_h = [k.sem(f"glu_w_hi_done{b}") for b in range(2)]
    w_l = [k.sem(f"glu_w_lo_done{b}") for b in range(2)]
    x_h, x_l, unit, gated, mixed = (k.sem("glu" + n) for n in ("_y_hi_done", "_y_lo_done", "_unit_done",
                                                                 "_gate_done", "_mixed"))
    w_v = w_glu.rearrange("(k p) n -> p k n", p=P)
    PAIRS = KT // 2

    def row(a, n, half):
        return a[:, ds(n, 1), half * HALF:(half + 1) * HALF].rearrange("p a c -> p (a c)")

    with nc.Block() as block:
        @block.sync
        def _(s):
            def load(i, b):
                s.dma_start(w_raw[b][:, :, :], w_v[:, :, ds((2 * i + b) * P, P)]).then_inc(loaded[b], 16)

            for b in range(2):
                load(0, b)
            with s.Fori(1, PAIRS) as i:
                for b in range(2):
                    s.wait_ge(w_l[b], i)
                    carry(s, i)
                    load(i, b)

        @block.scalar
        def _(a):
            def split(i, b):
                a.wait_ge(loaded[b], 16 * (i + 1))
                carry(a, i)
                if not (isinstance(i, int) and i == 0):
                    a.wait_ge(unit, 4 * i - 2 + 2 * b)
                    carry(a, i)
                split_hi(a, w_hi[b][:, :, :], w_raw[b][:, :, :]).then_inc(w_h[b], 1)

            def gates(i, b):
                for half in range(2):
                    a.wait_ge(unit, 4 * i + 2 * b + half + 1)
                    carry(a, i)
                    if not (isinstance(i, int) and i == 0 and b == 0):
                        a.wait_ge(mixed, 4 * i + 2 * b + half - 1)
                        carry(a, i)
                    a.activation(gate[half][:, :], ps[:, 2 * b + half, :], ACT.Sigmoid,
                                 bias=k.glu_col[:, ds(2 * i + b, 1)]).then_inc(gated, 1)

            split(0, 0)
            for kk in range(KT):
                split_hi(a, k.aT_hi[:, kk, :], h[:, kk, :]).then_inc(x_h, 1)
            split(0, 1)
            gates(0, 0)
            gates_next = lambda i: (split(i, 0), gates(i - 1, 1), split(i, 1), gates(i, 0))
            with a.Fori(1, PAIRS) as i:
                gates_next(i)
            gates(PAIRS - 1, 1)

        @block.vector
        def _(v):
            def mix(i):
                for b in range(2):
                    for half in range(2):
                        v.wait_ge(gated, 4 * i + 2 * b + half + 1)
                        o = row(h, 2 * i + b, half)
                        v.tensor_tensor(o, o, gate[half][:, :], ALU.mult).then_inc(mixed, 1)

            for kk in range(KT):
                v.wait_ge(x_h, kk + 1)
                v.tensor_tensor(k.aT_lo[:, kk, :], h[:, kk, :], k.aT_hi[:, kk, :].bitcast(F32),
                                ALU.subtract).then_inc(x_l, 1)
            v.wait_ge(x_l, KT)
            with v.Fori(0, PAIRS) as i:
                mix(i)

        @block.gpsimd
        def _(g):
            k.clear_old(g)
            with g.Fori(0, PAIRS) as i:
                for b in range(2):
                    g.wait_ge(w_h[b], i + 1)
                    carry(g, i)
                    g.tensor_tensor(w_lo[b][:, :, :], w_raw[b][:, :, :], w_hi[b][:, :, :].bitcast(F32),
                                    ALU.subtract).then_inc(w_l[b], 1)

        @block.tensor
        def _(t):
            def tile(i, b, start):
                t.wait_ge(w_l[b], i + 1)
                for half in range(2):
                    if not start:
                        t.wait_ge(gated, 4 * i + 2 * b + half - 3)
                    cols = slice(half * HALF, (half + 1) * HALF)
                    for kk in range(KT):
                        if start and b == 0 and half == 0:
                            t.wait_ge(x_l, kk + 1)
                        for m, (w, x) in enumerate(((w_hi, k.aT_hi), (w_hi, k.aT_lo), (w_lo, k.aT_hi))):
                            ins = t.matmul(ps[:, 2 * b + half, :], w[b][:, kk, :], x[:, kk, cols],
                                           start=(kk == 0 and m == 0), stop=(kk == KT - 1 and m == 2))
                    ins.then_inc(unit, 1)

            for b in range(2):
                tile(0, b, True)
            with t.Fori(1, PAIRS) as i:
                for b in range(2):
                    tile(i, b, False)
    k.close()


HG_OUTS = 5


def hgrn_weights(k, w_in):
    k.open()
    w_raw = [k.sb(f"hg_w_raw{b}", [P, KT, P]) for b in range(2)]
    w_hi = [k.sb(f"hg_w_hi{b}", [P, KT, P], F32R) for b in range(2)]
    w_lo = [k.sb(f"hg_w_lo{b}", [P, KT, P], F32R) for b in range(2)]
    w_v = w_in.rearrange("(k p) (o n) -> p o k n", p=P, o=HG_OUTS)
    first = [(w_raw[b][:, :, :], w_hi[b][:, :, :], w_lo[b][:, :, :], [(w_raw[b][:, :, :], w_v[:, b, :, 0:P])])
             for b in range(2)]
    return (w_raw, w_hi, w_lo, w_v), first


def hgrn_block(k, weights, lower_bound, norm_g, masks):
    nc, ps, h = k.nc, k.ps, k.h
    w_raw, w_hi, w_lo, w_v = weights
    sb = lambda n, shape, dt=F32: k.sb("hg_" + n, shape, dt)
    q_raw, v_raw, gs = sb("q_raw", [P, T]), sb("v_raw", [P, T]), sb("gs", [P, T])
    f_raw = [sb(f"f_raw{d}", [P, T]) for d in range(2)]
    k_raw = [sb(f"k_raw{d}", [P, T]) for d in range(2)]
    Q = [sb(f"q_decayed{d}", [P, T]) for d in range(2)]
    K = [sb(f"k_decayed{d}", [P, T]) for d in range(2)]
    tot = [sb(f"gate_totals{d}", [P, T]) for d in range(2)]
    k_sum = sb("k_sum", [P, T])
    v_tok, scores = sb("v_tok", [P, NHC, P]), sb("scores", [P, NHC, HC])
    S = [sb(f"state{d}", [P, NHC, P]) for d in range(2)]
    sig = [sb(f"sigmoid{b}", [P, HALF]) for b in range(2)]
    mask = sb("masks", [P, HLV, HC], I32)
    lb_in, lb, ng = sb("lb_in", [P, 2, HEADS]), sb("lb", [P, 2, HEADS]), sb("norm_g", [P, 1])
    d_lb = sb("lb_diff", [P, HEADS])
    ms, rs, rt = (sb("rms" + n, [P, NHC]) for n in "abc")
    sq = sb("square", [P, P])
    E = {n: k.sem("hg_" + n) for n in (
        "consts", "lb_chain", "lb_act", "w_loaded0", "w_loaded1", "w_hi_done0", "w_hi_done1", "w_lo_done0",
        "w_lo_done1", "unit_done", "q_sig", "q_kept", "f_sig", "f_kept", "f_ready", "v_kept", "g_sig", "g_kept",
        "k_started", "init", "prepared", "chain", "v_turned", "v_tok_kept", "diag_done", "diag_kept", "level_done",
        "level_moved", "k_turned", "k_turned_kept", "kv_done", "states_kept", "o_done", "o_squared",
        "o_normed", "o_turned", "o_kept")}
    OUTS = HG_OUTS
    BUF = [0, 1, 0, 1, 0]
    USES = [BUF.count(0), BUF.count(1)]
    CORE = 2 * (NHC - 2) + 1 + RSQRT_STEPS
    PREPARED = 2 * HLV + 2

    def first(n):
        return isinstance(n, int) and n == 0

    def uses(m, o):
        return m * USES[BUF[o]] + BUF[:o + 1].count(BUF[o]) - 1

    def last_unit(m, o):
        before = [q for q in range(o) if BUF[q] == BUF[o]]
        if before:
            return m * 2 * OUTS + 2 * before[-1] + 2
        return (m - 1) * 2 * OUTS + 2 * max(q for q in range(OUTS) if BUF[q] == BUF[o]) + 2

    def chunks(a):
        return a[:, :].rearrange("p (c t) -> p c t", t=HC)

    def halves(a, lv, side):
        return a[:, :].rearrange("p (b e s) -> p b e s", e=2, s=1 << lv)[:, :, side, :]

    def total(d, lv):
        if lv == 0:
            return f_raw[d][:, :]
        at = T - (T >> (lv - 1))
        return tot[d][:, at:at + (T >> lv)]

    def pair(d, lv, side):
        return total(d, lv).rearrange("p (b e) -> p b e", e=2)[:, :, side]

    def bank_rows(b):
        return ps[:, b:b + 2, :].rearrange("p b (c t) -> p (b c) t", t=P)

    with nc.Block() as block:
        @block.sync
        def _(s):
            s.dma_start(mask[:, :, :], masks.rearrange("l s t -> s l t")).then_inc(E["consts"], 16)
            for r in range(2):
                s.dma_start(lb_in[:, r, :], lower_bound[r].rearrange("(n p) -> p n", p=P),
                            allow_slow_non_contiguous=True).then_inc(E["consts"], 16)
            s.dma_start(ng[:, :], norm_g.rearrange("(p a) -> p a", a=1)).then_inc(E["consts"], 16)

            def load(m, o):
                b = BUF[o]
                if not (first(m) and uses(m, o) == 1):
                    s.wait_ge(E[f"w_lo_done{b}"], uses(m, o) - 1)
                    carry(s, m)
                s.dma_start(w_raw[b][:, :, :], w_v[:, o, :, ds(m * P, P)]).then_inc(E[f"w_loaded{b}"], 16)

            for o in range(2, OUTS):
                load(0, o)
            with s.Fori(1, HEADS) as m:
                for o in range(OUTS):
                    load(m, o)

        @block.gpsimd
        def _(g):
            k.clear_old(g)
            def split(m, o):
                b = BUF[o]
                g.wait_ge(E[f"w_hi_done{b}"], uses(m, o))
                carry(g, m)
                g.tensor_tensor(w_lo[b][:, :, :], w_raw[b][:, :, :], w_hi[b][:, :, :].bitcast(F32),
                                ALU.subtract).then_inc(E[f"w_lo_done{b}"], 1)

            for o in range(2, OUTS):
                split(0, o)
            with g.Fori(1, HEADS) as m:
                for o in range(OUTS):
                    split(m, o)

        @block.tensor
        def _(t):
            def unit(m, o, half):
                b = BUF[o]
                if half == 0 and not (first(m) and o < 2):
                    t.wait_ge(E[f"w_lo_done{b}"], uses(m, o))
                if o == 0 and not first(m):
                    t.wait_ge(E["g_kept"], 2 * m - 1 + half)
                if o == 1:
                    t.wait_ge(E["q_kept"], 2 * m + 1 + half)
                if o in (2, 3):
                    t.wait_ge(E["f_kept"], 4 * m + 2 * (o - 2) + 1 + half)
                if o == 4:
                    t.wait_ge(E["v_kept"], 2 * m + 1 + half)
                cols = slice(half * HALF, (half + 1) * HALF)
                for kk in range(KT):
                    for q, (w, x) in enumerate(((w_hi, k.aT_hi), (w_hi, k.aT_lo), (w_lo, k.aT_hi))):
                        ins = t.matmul(ps[:, half, :], w[b][:, kk, :], x[:, kk, cols],
                                       start=(kk == 0 and q == 0), stop=(kk == KT - 1 and q == 2))
                ins.then_inc(E["unit_done"], 1)

            def turn_v(n):
                t.wait_ge(E["v_kept"], 2 * (n + 1))
                if not first(n):
                    t.wait_ge(E["states_kept"], 2 * n)
                for c in range(NHC):
                    ins = t.transpose(ps[:, 6 + c // 4, (c % 4) * P:(c % 4 + 1) * P],
                                      v_raw[:, c * HC:(c + 1) * HC], k.ident[:, :])
                ins.then_inc(E["v_turned"], 1)

            def diagonal(n):
                t.wait_ge(E["init"], n + 1)
                t.wait_ge(E["v_tok_kept"], n + 1)
                for c in range(NHC):
                    cols = slice(c * HC, (c + 1) * HC)
                    ins = t.matmul(ps[:, 6 + c // 4, (c % 4) * P:(c % 4 + 1) * P], k_sum[:, cols], q_raw[:, cols],
                                   start=True, stop=True)
                ins.then_inc(E["diag_done"], 1)

            def level(n, lv):
                if lv == 0:
                    t.wait_ge(E["prepared"], (n + 1) * PREPARED)
                    if not first(n):
                        t.wait_ge(E["o_normed"], n)
                for d in range(2):
                    if lv:
                        t.wait_ge(E["level_moved"], 2 * HLV * n + 2 * (lv - 1) + d + 1)
                    for c in range(NHC):
                        q = chunks(Q[d])[:, c, :].rearrange("p (b e s) -> p b e s", e=2, s=1 << lv)[:, :, 1 - d, :]
                        ins = t.matmul(ps[:, 2 + d, c * (HC // 2):(c + 1) * (HC // 2)], chunks(K[d])[:, c, :], q,
                                       start=True, stop=True)
                    ins.then_inc(E["level_done"], 1)

            def turn_k(n):
                t.wait_ge(E["level_moved"], 2 * HLV * (n + 1))
                if not first(n):
                    t.wait_ge(E["o_kept"], 2 * n)
                t.wait_ge(E["diag_kept"], n + 1)
                for d in range(2):
                    for c in range(NHC):
                        ins = t.transpose(ps[:, 4 + 2 * d + c // 4, (c % 4) * P:(c % 4 + 1) * P],
                                          chunks(K[d])[:, c, :], k.ident[:, :])
                    ins.then_inc(E["k_turned"], 1)

            def chunk_sums(n):
                for d in range(2):
                    t.wait_ge(E["k_turned_kept"], 2 * n + d + 1)
                    for c in (range(1, NHC) if d else range(NHC - 1)):
                        ins = t.matmul(ps[:, 4 + 2 * d + c // 4, (c % 4) * P:(c % 4 + 1) * P],
                                       chunks(K[d])[:, c, :], v_tok[:, c, :], start=True, stop=True)
                    ins.then_inc(E["kv_done"], 1)

            def outputs(n):
                t.wait_ge(E["states_kept"], 2 * (n + 1))
                for c in range(NHC):
                    o = ps[:, 2 + c // 4, (c % 4) * P:(c % 4 + 1) * P]
                    t.matmul(o, scores[:, c, :], v_tok[:, c, :], start=True, stop=False)
                    if c > 0:
                        ins = t.matmul(o, chunks(Q[0])[:, c, :], S[0][:, c, :], start=False, stop=(c == NHC - 1))
                    if c < NHC - 1:
                        ins = t.matmul(o, chunks(Q[1])[:, c, :], S[1][:, c, :], start=False, stop=True)
                ins.then_inc(E["o_done"], 1)

            def turn_o(n):
                t.wait_ge(E["o_normed"], n + 1)
                for c in range(NHC):
                    ins = t.transpose(ps[:, 4 + c // 4, (c % 4) * P:(c % 4 + 1) * P], scores[:, c, :],
                                      k.ident[:, :])
                    if c % 4 == 3:
                        ins.then_inc(E["o_turned"], 1)

            def core(n, more):
                level(n, 0)
                for lv in range(1, HLV):
                    if more:
                        unit(n + 1, (lv - 1) // 2, (lv - 1) % 2)
                    level(n, lv)
                if more:
                    unit(n + 1, 3, 0)
                turn_k(n)
                if more:
                    unit(n + 1, 3, 1)
                chunk_sums(n)
                if more:
                    unit(n + 1, 4, 0)
                outputs(n)
                if more:
                    turn_v(n + 1)
                    unit(n + 1, 4, 1)
                    diagonal(n + 1)
                turn_o(n)

            for u in range(2 * OUTS):
                unit(0, u // 2, u % 2)
            turn_v(0)
            diagonal(0)
            core(0, True)
            with t.Fori(1, HEADS - 1) as n:
                core(n, True)
            core(HEADS - 1, False)

        @block.scalar
        def _(a):
            a.wait_ge(E["lb_chain"], 1)
            a.activation(lb[:, 0, :], d_lb[:, :], ACT.Sigmoid).then_inc(E["lb_act"], 1)
            a.activation(lb[:, 1, :], d_lb[:, :], ACT.Sigmoid, scale=-1.0).then_inc(E["lb_act"], 1)
            a.wait_ge(E["lb_act"], 2)

            def split(m, o):
                b = BUF[o]
                a.wait_ge(E[f"w_loaded{b}"], 16 * uses(m, o))
                carry(a, m)
                a.wait_ge(E["unit_done"], last_unit(m, o))
                carry(a, m)
                split_hi(a, w_hi[b][:, :, :], w_raw[b][:, :, :]).then_inc(E[f"w_hi_done{b}"], 1)

            def sigmoid_of(m, o, half, done):
                a.wait_ge(E["unit_done"], 2 * OUTS * m + 2 * o + half + 1)
                carry(a, m)
                other, base = ("g_kept", 2 * m - 1 + half) if o == 0 else ("q_kept", 2 * m + 1 + half)
                if not (o == 0 and first(m)):
                    a.wait_ge(E[other], base)
                    carry(a, m)
                a.activation(sig[half][:, :], ps[:, half, :], ACT.Sigmoid).then_inc(E[done], 1)

            def gate(m, d):
                if not first(m):
                    a.wait_ge(E["level_moved"], 2 * HLV * (m - 1) + 2)
                    carry(a, m)
                for half in range(2):
                    cols = slice(half * HALF, (half + 1) * HALF)
                    a.wait_ge(E["unit_done"], 2 * OUTS * m + 2 * (1 + d) + half + 1)
                    carry(a, m)
                    a.activation(f_raw[d][:, cols], ps[:, half, :], ACT.Sigmoid).then_inc(E["f_sig"], 1)
                    a.activation(k_raw[d][:, cols], ps[:, half, :], ACT.Sigmoid, scale=-1.0
                                 ).then_inc(E["f_kept"], 1)
                a.wait_ge(E["f_sig"], 4 * m + 2 * d + 2)
                carry(a, m)
                a.activation(f_raw[d][:, :], f_raw[d][:, :], ACT.Identity, bias=lb[:, 0, ds(m, 1)],
                             scale=lb[:, 1, ds(m, 1)]).then_inc(E["f_ready"], 1)

            def keep_v(m, half):
                if not first(m):
                    a.wait_ge(E["v_turned"], m)
                    carry(a, m)
                a.wait_ge(E["unit_done"], 2 * OUTS * m + 6 + half + 1)
                carry(a, m)
                a.activation(v_raw[:, half * HALF:(half + 1) * HALF], ps[:, half, :], ACT.Copy
                             ).then_inc(E["v_kept"], 1)

            def start_k(n):
                a.wait_ge(E["f_kept"], 4 * (n + 1))
                carry(a, n)
                if not first(n):
                    a.wait_ge(E["kv_done"], 2 * n)
                    carry(a, n)
                for d in range(2):
                    a.activation(K[d][:, :], k_raw[d][:, :], ACT.Copy, scale=lb[:, 1, ds(n, 1)]
                                 ).then_inc(E["k_started"], 1)

            def keep_turned_v(n):
                a.wait_ge(E["v_turned"], n + 1)
                carry(a, n)
                if not first(n):
                    a.wait_ge(E["o_done"], n)
                    carry(a, n)
                a.activation(v_tok[:, :, :], bank_rows(6), ACT.Copy).then_inc(E["v_tok_kept"], 1)

            def keep_turned_k(n):
                for d in range(2):
                    a.wait_ge(E["k_turned"], 2 * n + d + 1)
                    carry(a, n)
                    a.activation(chunks(K[d]), bank_rows(4 + 2 * d), ACT.Copy).then_inc(E["k_turned_kept"], 1)

            def squares(n):
                a.wait_ge(E["o_done"], n + 1)
                carry(a, n)
                for c in range(NHC):
                    if c or not first(n):
                        a.wait_ge(E["o_squared"], NHC * n + c)
                        carry(a, n)
                    a.activation(sq[:, :], ps[:, 2 + c // 4, (c % 4) * P:(c % 4 + 1) * P], ACT.Square,
                                 accum_out=ms[:, c:c + 1]).then_inc(E["o_squared"], 1)

            def core(n, more):
                if more:
                    split(n + 1, 1)
                    for half in range(2):
                        sigmoid_of(n + 1, 0, half, "q_sig")
                    split(n + 1, 2)
                    gate(n + 1, 0)
                    split(n + 1, 3)
                    gate(n + 1, 1)
                    split(n + 1, 4)
                    keep_v(n + 1, 0)
                keep_turned_k(n)
                if more:
                    keep_v(n + 1, 1)
                    start_k(n + 1)
                    sigmoid_of(n + 1, 4, 0, "g_sig")
                squares(n)
                if more:
                    keep_turned_v(n + 1)
                    sigmoid_of(n + 1, 4, 1, "g_sig")

            for half in range(2):
                sigmoid_of(0, 0, half, "q_sig")
            split(0, 2)
            gate(0, 0)
            split(0, 3)
            gate(0, 1)
            split(0, 4)
            for half in range(2):
                keep_v(0, half)
            for half in range(2):
                sigmoid_of(0, 4, half, "g_sig")
            start_k(0)
            keep_turned_v(0)
            split(1, 0)
            core(0, True)
            split(2, 0)
            with a.Fori(1, HEADS - 2) as n:
                core(n, True)
                split(n + 2, 0)
            core(HEADS - 2, True)
            core(HEADS - 1, False)

        @block.vector
        def _(v):
            v.wait_ge(E["consts"], 16 * 4)
            v.tensor_tensor(d_lb[:, :], lb_in[:, 1, :], lb_in[:, 0, :], ALU.subtract).then_inc(E["lb_chain"], 1)

            def keep_q(m, half):
                if half == 0 and not first(m):
                    v.wait_ge(E["diag_done"], m)
                v.wait_ge(E["q_sig"], 2 * m + half + 1)
                cols = slice(half * HALF, (half + 1) * HALF)
                v.tensor_tensor(q_raw[:, cols], sig[half][:, :], ps[:, half, :], ALU.mult
                                ).then_inc(E["q_kept"], 1)

            def keep_g(m, half):
                if not first(m):
                    v.wait_ge(E["o_kept"], 2 * m)
                v.wait_ge(E["g_sig"], 2 * m + half + 1)
                cols = slice(half * HALF, (half + 1) * HALF)
                v.scalar_tensor_tensor(gs[:, cols], ps[:, half, :], ng[:, :], sig[half][:, :], ALU.mult, ALU.mult
                                       ).then_inc(E["g_kept"], 1)

            def prepare_totals(n):
                link = Steps(E["prepared"], n * PREPARED)
                v.wait_ge(E["f_ready"], 2 * (n + 1))
                if not first(n):
                    v.wait_ge(E["states_kept"], 2 * n)
                for lv in range(1, HLV + 1):
                    for d in range(2):
                        v.tensor_tensor(total(d, lv), pair(d, lv - 1, 0), pair(d, lv - 1, 1), ALU.mult
                                        ).then_inc(E["prepared"], 1)
                        link.step()
                    v.wait_ge(E["prepared"], link.count())
                v.wait_ge(E["k_started"], 2 * (n + 1))
                v.tensor_tensor(k_sum[:, :], K[0][:, :], K[1][:, :], ALU.add).then_inc(E["init"], 1)

            def prepare_q(n):
                if not first(n):
                    v.wait_ge(E["o_done"], n)
                for d in range(2):
                    v.tensor_tensor(Q[d][:, :], q_raw[:, :], f_raw[d][:, :], ALU.mult).then_inc(E["prepared"], 1)

            def core(n, more):
                link = Steps(E["chain"], n * CORE)
                v.wait_ge(E["prepared"], (n + 1) * PREPARED)
                v.wait_ge(E["diag_done"], n + 1)
                for b in range(2):
                    ins = v.tensor_tensor(scores[:, 4 * b:4 * b + 4, :],
                                          ps[:, 6 + b, :].rearrange("p (c t) -> p c t", t=HC),
                                          bc(k.ident[:, :], 1, [P, 4, HC]), ALU.mult)
                ins.then_inc(E["diag_kept"], 1)
                v.wait_ge(E["diag_kept"], n + 1)
                for lv in range(HLV):
                    s_ = 1 << lv
                    nb = HC // (2 * s_)
                    for d in range(2):
                        v.wait_ge(E["level_done"], 2 * HLV * n + 2 * lv + d + 1)
                        carry(v, n)
                        if not (first(n) and lv + d == 0):
                            v.wait_ge(E["level_moved"], 2 * HLV * n + 2 * lv + d)
                            carry(v, n)
                        to = scores[:, :, :].rearrange("p c (b e s) -> p c b e s", e=2, s=s_)[:, :, :, 1 - d, :]
                        mk = mask[:, lv, :].rearrange("p (b e s) -> p b e s", e=2, s=s_)[:, :, 1 - d, :]
                        of = ps[:, 2 + d, :].rearrange("p (c b s) -> p c b s", c=NHC, s=s_)
                        v.copy_predicated(to.rearrange("p c b s -> p (c b) s"),
                                          bc(mk, 1, [P, NHC, nb, s_]),
                                          of.rearrange("p c b s -> p (c b) s"))
                        qs, ks = halves(Q[d], lv, 1 - d), halves(K[d], lv, d)
                        full = [P, T // (2 * s_), s_]
                        v.tensor_tensor(qs, qs, bc(pair(d, lv, d), 2, full), ALU.mult)
                        v.tensor_tensor(ks, ks, bc(pair(d, lv, 1 - d), 2, full), ALU.mult
                                        ).then_inc(E["level_moved"], 1)
                    if more and lv < 2:
                        keep_q(n + 1, lv)
                for d in range(2):
                    v.wait_ge(E["kv_done"], 2 * n + d + 1)
                    kv, tt = bank_rows(4 + 2 * d), total(d, HLV)
                    order = list(range(NHC)) if d == 0 else list(range(NHC - 1, -1, -1))
                    for i in range(NHC - 1):
                        c, nxt = order[i], order[i + 1]
                        if i == 0:
                            ins = v.tensor_copy(S[d][:, nxt, :], kv[:, c, :])
                        else:
                            ins = v.scalar_tensor_tensor(S[d][:, nxt, :], S[d][:, c, :], tt[:, c:c + 1],
                                                         kv[:, c, :], ALU.mult, ALU.add)
                        if i == NHC - 2:
                            ins.then_inc(E["states_kept"], 1)
                        else:
                            ins.then_inc(E["chain"], 1)
                            v.wait_ge(E["chain"], link.step())
                if more:
                    prepare_totals(n + 1)
                    prepare_q(n + 1)
                v.wait_ge(E["o_squared"], NHC * (n + 1))
                v.tensor_scalar(ms[:, :], ms[:, :], 1.0 / P, RMS_EPS, ALU.mult, ALU.add).then_inc(E["chain"], 1)
                v.wait_ge(E["chain"], link.step())
                rsqrt_steps(link, v, rs[:, :], rt[:, :], ms[:, :])
                for b in range(2):
                    ins = v.tensor_tensor(scores[:, 4 * b:4 * b + 4, :],
                                          ps[:, 2 + b, :].rearrange("p (c t) -> p c t", t=P),
                                          bc(rs[:, 4 * b:4 * b + 4], 2, [P, 4, P]), ALU.mult)
                ins.then_inc(E["o_normed"], 1)
                for b in range(2):
                    v.wait_ge(E["o_turned"], 2 * n + b + 1)
                    v.tensor_tensor(h[:, ds(n, 1), b * HALF:(b + 1) * HALF].rearrange("p a c -> p (a c)"),
                                    ps[:, 4 + b, :], gs[:, b * HALF:(b + 1) * HALF], ALU.mult
                                    ).then_inc(E["o_kept"], 1)
                if more:
                    for half in range(2):
                        keep_g(n + 1, half)
                assert link.n == CORE

            for half in range(2):
                keep_q(0, half)
            for half in range(2):
                keep_g(0, half)
            prepare_totals(0)
            prepare_q(0)
            core(0, True)
            with v.Fori(1, HEADS - 1) as n:
                core(n, True)
            core(HEADS - 1, False)
    k.close()


_INS = ["x", "ln_mix_g", "ln_mix_b", "ln_ffn_g", "ln_ffn_b", "ffn_w_in", "ffn_w_out", "s5_w_in",
        "s5_lam_re", "s5_lam_im", "s5_log_step", "s5_b_re", "s5_b_im", "s5_c_re", "s5_c_im", "s5_d",
        "s5_w_glu", "s5_b_glu", "s5_w_out", "hg_w_in", "hg_lower_bound", "hg_norm_g", "hg_w_out"]


def level_masks():
    s = np.arange(HC)
    return np.stack([(s[:, None] >> (lv + 1) == s[None] >> (lv + 1)) & (s[:, None] >> lv != s[None] >> lv)
                     for lv in range(HLV)]).astype(np.int32)


def program(nc, dram, out):
    with ExitStack() as ctx:
        k = Core(nc, ctx)
        TICKS.clear()
        TICKS.update({e.engine: k.sem(f"tick{n}", keep=True) for n, e in enumerate((nc.scalar, nc.gpsimd, nc.sync))})
        TICKS[None] = k.sem("tick_others", keep=True)
        k.ps = ctx.enter_context(nc.psum_tensor("ps", [P, 8, HALF], F32))
        k.h = k.sb("h", [P, NT, D], keep=True)
        k.aT_hi = k.sb("aT_hi", [P, KT, T], F32R, keep=True)
        k.aT_lo = k.sb("aT_lo", [P, KT, T], F32R, keep=True)
        k.stats = k.sb("stats", [P, NT, 2, 6], keep=True)
        k.ident = k.sb("ident", [P, P], keep=True)
        k.d_col, k.glu_col = k.sb("d_col", [P, KT], keep=True), k.sb("glu_col", [P, KT], keep=True)
        x_rows = dram["x"].rearrange("a (p s) d -> (a p) s d", s=NT)
        out_rows = out.rearrange("a t d -> (a t) d")

        k.open()
        k.pw = k.sb("s5_pw", [P, 2, KT * DP, L + 1])
        k.pw_in = k.sb("s5_pw_in", [P, 2, KT * DP, L])
        k.mu = k.sb("s5_mu", [P, LV, 3, KT * DP])
        k.coef = k.sb("s5_coef", [P, 2, KT * DP])
        c_rows = nc.dram_tensor("s5_c_rows", (2, KT * PR * GRP, 2, 2 * ST), F32, kind="Internal").ap()
        outer, k.phase = k.phase, ExitStack()
        s5_tables_block(k, x_rows, dram["s5_lam_re"][0], dram["s5_lam_im"][0], dram["s5_log_step"][0],
                        dram["s5_b_glu"][0], dram["s5_d"][0], dram, dram["s5_c_re"][0], dram["s5_c_im"][0], c_rows)
        k.close()
        k.phase = ExitStack()
        s5_scan_block(k, dram["s5_w_in"][0], dram["s5_b_re"][0], dram["s5_b_im"][0],
                      c_rows)
        k.close()
        outer.close()
        s5_gate_block(k, dram["s5_w_glu"][0])
        out_projection_block(k, "s5o", dram["s5_w_out"][0], x_rows, False)
        mix_g, mix_b, ffn_g, ffn_b = (dram[n] for n in ("ln_mix_g", "ln_mix_b", "ln_ffn_g", "ln_ffn_b"))
        weights, first = ffn_weights(k, "ffn0", dram["ffn_w_in"][0], dram["ffn_w_out"][0])
        outer, k.phase = k.phase, None
        layer_norm_block(k, "ln0", mix_g[0], mix_b[0], first)
        k.phase = outer
        ffn_block(k, "ffn0", weights, mix_g[0], mix_b[0])
        weights, first = hgrn_weights(k, dram["hg_w_in"][0])
        outer, k.phase = k.phase, None
        layer_norm_block(k, "ln1", ffn_g[0], ffn_b[0], first, natural=True, spill=dram["scratch"])
        k.phase = outer
        hgrn_block(k, weights, dram["hg_lower_bound"], dram["hg_norm_g"][0], dram["masks"])
        out_projection_block(k, "hgo", dram["hg_w_out"][0], dram["scratch"], True, ffn_g[0], ffn_b[0])
        weights, first = ffn_weights(k, "ffn1", dram["ffn_w_in"][1], dram["ffn_w_out"][1])
        outer, k.phase = k.phase, None
        layer_norm_block(k, "ln2", mix_g[1], mix_b[1], first)
        k.phase = outer
        ffn_block(k, "ffn1", weights, mix_g[1], mix_b[1])
        final_norm_block(k, "ln3", ffn_g[1], ffn_b[1], out_rows)


def kernel(**inputs):
    import concourse.bacc as _bacc
    from concourse.bass_utils import run_bass_kernel_spmd as _run

    nc = _bacc.Bacc("TRN2", target_bir_lowering=False, num_devices=1)
    arrays, dram = {}, {}
    for name in _INS:
        a = np.ascontiguousarray(inputs[name])
        arrays[f"in_{name}_dram"] = a
        dram[name] = nc.dram_tensor(f"in_{name}_dram", a.shape, mybir.dt.from_np(a.dtype), kind="ExternalInput").ap()
    for name, a in (("ident", np.eye(P, dtype=np.float32)), ("masks", level_masks())):
        arrays[f"const_{name}_dram"] = a
        dram[name] = nc.dram_tensor(f"const_{name}_dram", a.shape, mybir.dt.from_np(a.dtype), kind="ExternalInput").ap()
    dram["scratch"] = nc.dram_tensor("residual_scratch", (P, NT, D), F32, kind="Internal").ap()
    out = nc.dram_tensor("out_0_dram", (1, T, D), F32, kind="ExternalOutput").ap()
    program(nc, dram, out)
    r = _run(nc, [arrays], core_ids=[0])
    return r.results[0]["out_0_dram"]
```
